# Optimizing a Trainium2 kernel written in Bass

```python
import math
import jax, jax.numpy as jnp
from jax import lax
import numpy as np

D_MODEL = 1024
BATCH = 1
SEQ = 512
DEPTH = 1

N_META = 16
CHUNK = 128
ROPE_BASE = 10000.0
EPS = 1e-6
MLA_HEADS = 8
MLA_Q_LORA = 384
MLA_KV_LORA = 256
MLA_NOPE = 64
MLA_ROPE = 32
MLA_V = 64
MLA_QK = MLA_NOPE + MLA_ROPE
RET_HEADS = 8
RET_DK = 64
RET_DV = 128
PEER_HEADS = 8
PEER_NKEYS = 128
PEER_EXPERTS = PEER_NKEYS * PEER_NKEYS
PEER_DQ = 128
PEER_TOPK = 16
PEER_BLOCK = 256
IN_SIZES = (MLA_Q_LORA, MLA_KV_LORA, MLA_ROPE, RET_HEADS * RET_DK, RET_HEADS * RET_DK,
            RET_HEADS * RET_DV, RET_HEADS * RET_DV, D_MODEL, D_MODEL)
IN_WIDTH = sum(IN_SIZES)


def rmsnorm(x, g):
    xf = x.astype(jnp.float32)
    y = xf * lax.rsqrt(jnp.mean(xf * xf, axis=-1, keepdims=True) + EPS)
    return (y * g.astype(jnp.float32)).astype(x.dtype)

def rope(x, pos):
    half = x.shape[-1] // 2
    inv = ROPE_BASE ** (-jnp.arange(half, dtype=jnp.float32) / half)
    ang = pos.astype(jnp.float32)[:, None] * inv[None, :]
    cos, sin = jnp.cos(ang), jnp.sin(ang)
    xf = x.astype(jnp.float32)
    x1, x2 = xf[..., :half], xf[..., half:]
    return jnp.concatenate([x1 * cos - x2 * sin, x1 * sin + x2 * cos], -1).astype(x.dtype)

def causal_block_attention(q, k, v):
    B, H, L, dqk = q.shape
    dv = v.shape[-1]
    nblk = -(-L // CHUNK)
    Lp = nblk * CHUNK
    qp = jnp.pad(q, ((0, 0), (0, 0), (0, Lp - L), (0, 0)))
    kpos = jnp.arange(L)
    scale = 1.0 / math.sqrt(dqk)

    def one_block(i):
        qb = lax.dynamic_slice_in_dim(qp, i * CHUNK, CHUNK, axis=2)
        s = jnp.einsum('bhqd,bhkd->bhqk', qb, k).astype(jnp.float32) * scale
        qpos = i * CHUNK + jnp.arange(CHUNK)
        s = jnp.where(kpos[None, :] <= qpos[:, None], s, -jnp.inf)
        p = jax.nn.softmax(s, axis=-1)
        return jnp.einsum('bhqk,bhkd->bhqd', p.astype(v.dtype), v)

    out = lax.map(one_block, jnp.arange(nblk))
    out = out.transpose(1, 2, 0, 3, 4).reshape(B, H, Lp, dv)
    return out[:, :, :L]

def mla_branch(c_q, c_kv, k_pe, pos, g_q_lora, w_uq, g_kv_lora, w_ukv, g_qk_q, g_qk_k):
    B, L, _ = c_q.shape
    q = (rmsnorm(c_q, g_q_lora) @ w_uq).reshape(B, L, MLA_HEADS, MLA_QK)
    kv = (rmsnorm(c_kv, g_kv_lora) @ w_ukv).reshape(B, L, MLA_HEADS, MLA_NOPE + MLA_V)
    k_nope, v = kv[..., :MLA_NOPE], kv[..., MLA_NOPE:]
    k = jnp.concatenate([k_nope, jnp.broadcast_to(k_pe[:, :, None, :], (B, L, MLA_HEADS, MLA_ROPE))], -1)
    q = rmsnorm(q, g_qk_q).transpose(0, 2, 1, 3)
    k = rmsnorm(k, g_qk_k).transpose(0, 2, 1, 3)
    q = jnp.concatenate([q[..., :MLA_NOPE], rope(q[..., MLA_NOPE:], pos)], -1)
    k = jnp.concatenate([k[..., :MLA_NOPE], rope(k[..., MLA_NOPE:], pos)], -1)
    o = causal_block_attention(q, k, v.transpose(0, 2, 1, 3))
    return o.transpose(0, 2, 1, 3).reshape(B, L, MLA_HEADS * MLA_V)

def retention_branch(q, k, v, gate, pos, g_gn):
    B, L, _ = q.shape
    H, C = RET_HEADS, CHUNK
    q = rope(q.reshape(B, L, H, RET_DK).transpose(0, 2, 1, 3), pos)
    k = rope(k.reshape(B, L, H, RET_DK).transpose(0, 2, 1, 3), pos) * (RET_DK ** -0.5)
    v = v.reshape(B, L, H, RET_DV).transpose(0, 2, 1, 3)
    P = (-N_META) % C
    Lp = L + P
    NC = Lp // C
    padf = lambda t: jnp.pad(t, ((0, 0), (0, 0), (P, 0), (0, 0))).reshape(B, H, NC, C, t.shape[-1])
    qc, kc, vc = padf(q), padf(k), padf(v)

    log_gamma = jnp.log(1.0 - 2.0 ** (-5.0 - jnp.arange(H, dtype=jnp.float32)))
    idx = jnp.arange(C, dtype=jnp.float32)
    diff = idx[:, None] - idx[None, :]
    decay = jnp.where(diff[None] >= 0, jnp.exp(jnp.maximum(diff, 0.0)[None] * log_gamma[:, None, None]), 0.0)
    zeta = jnp.exp((C - 1 - idx)[None, :] * log_gamma[:, None])
    xi = jnp.exp((idx + 1)[None, :] * log_gamma[:, None])
    gamma_c = jnp.exp(C * log_gamma)

    scores = jnp.einsum('bhncd,bhnmd->bhncm', qc, kc) * decay[None, :, None]
    inner = jnp.einsum('bhncm,bhnme->bhnce', scores, vc)
    chunk_kv = jnp.einsum('bhnmd,bhnme->bhnde', kc * zeta[None, :, None, :, None], vc)

    def step(state, kv_n):
        return gamma_c[None, :, None, None] * state + kv_n, state

    init = jnp.zeros((B, H, RET_DK, RET_DV), chunk_kv.dtype)
    _, prev_states = lax.scan(step, init, jnp.moveaxis(chunk_kv, 2, 0))
    prev_states = jnp.moveaxis(prev_states, 0, 2)
    cross = jnp.einsum('bhncd,bhnde->bhnce', qc, prev_states) * xi[None, :, None, :, None]
    y = (inner + cross).reshape(B, H, Lp, RET_DV)[:, :, P:]

    yf = y.astype(jnp.float32)
    mu = jnp.mean(yf, -1, keepdims=True)
    var = jnp.mean((yf - mu) ** 2, -1, keepdims=True)
    yn = ((yf - mu) * lax.rsqrt(var + EPS)).transpose(0, 2, 1, 3).reshape(B, L, H * RET_DV)
    yn = (yn * g_gn.astype(jnp.float32)).astype(gate.dtype)
    return jax.nn.silu(gate) * yn

def mixer_sublayer(h, pos, g_mix, w_in, g_q_lora, w_uq, g_kv_lora, w_ukv, g_qk_q, g_qk_k,
                   w_mla_out, g_ret_gn, w_ret_out, w_mix_out):
    hn = rmsnorm(h, g_mix)
    z = hn @ w_in
    c_q, c_kv, k_pe, r_q, r_k, r_v, r_g, za, zr = jnp.split(z, np.cumsum(IN_SIZES)[:-1].tolist(), axis=-1)
    y_a = mla_branch(c_q, c_kv, k_pe, pos, g_q_lora, w_uq, g_kv_lora, w_ukv, g_qk_q, g_qk_k) @ w_mla_out
    y_r = retention_branch(r_q, r_k, r_v, r_g, pos, g_ret_gn) @ w_ret_out
    merged = jax.nn.sigmoid(za) * y_a + jax.nn.sigmoid(zr) * y_r
    return merged @ w_mix_out

def peer_sublayer(h, g_ffn, w_peer_q, keys_1, keys_2, peer_u, peer_v):
    shape = h.shape
    x = rmsnorm(h, g_ffn).reshape(-1, shape[-1])
    T = x.shape[0]
    q = (x @ w_peer_q).reshape(T, PEER_HEADS, PEER_DQ)
    half = PEER_DQ // 2
    s1 = jnp.einsum('thd,kd->thk', q[..., :half], keys_1).astype(jnp.float32)
    s2 = jnp.einsum('thd,kd->thk', q[..., half:], keys_2).astype(jnp.float32)
    v1, i1 = lax.top_k(s1, PEER_TOPK)
    v2, i2 = lax.top_k(s2, PEER_TOPK)
    cand = (v1[..., :, None] + v2[..., None, :]).reshape(T, PEER_HEADS, PEER_TOPK * PEER_TOPK)
    sc, ci = lax.top_k(cand, PEER_TOPK)
    e1 = jnp.take_along_axis(i1, ci // PEER_TOPK, axis=-1)
    e2 = jnp.take_along_axis(i2, ci % PEER_TOPK, axis=-1)
    eidx = (e1 * PEER_NKEYS + e2).reshape(T, PEER_HEADS * PEER_TOPK)
    gates = jax.nn.softmax(sc, axis=-1).reshape(T, PEER_HEADS * PEER_TOPK).astype(x.dtype)

    pad = (-T) % PEER_BLOCK
    nb = (T + pad) // PEER_BLOCK
    xb = jnp.pad(x, ((0, pad), (0, 0))).reshape(nb, PEER_BLOCK, -1)
    ib = jnp.pad(eidx, ((0, pad), (0, 0))).reshape(nb, PEER_BLOCK, -1)
    gb = jnp.pad(gates, ((0, pad), (0, 0))).reshape(nb, PEER_BLOCK, -1)

    def block(args):
        xt, it, gt = args
        act = jax.nn.gelu(jnp.einsum('td,tkd->tk', xt, peer_u[it]), approximate=False)
        return jnp.einsum('tk,tkd->td', gt * act, peer_v[it])

    y = lax.map(block, (xb, ib, gb)).reshape(nb * PEER_BLOCK, -1)[:T]
    return y.reshape(shape)

def first_inputs(seed: int = 0) -> dict:
    key = jax.random.key(seed)
    ks = jax.random.split(key, 20)
    f32 = jnp.float32
    nrm = lambda k, s, sc: jax.random.normal(k, s, f32) * sc
    gain = lambda k, s: 1.0 + 0.02 * jax.random.normal(k, s, f32)
    return {
        "x": nrm(ks[0], (BATCH, SEQ, D_MODEL), 1.0),
        "meta_tokens": nrm(ks[1], (N_META, D_MODEL), 1.0),
        "g_mix": gain(ks[2], (DEPTH, D_MODEL)),
        "w_in": nrm(ks[3], (DEPTH, D_MODEL, IN_WIDTH), D_MODEL ** -0.5),
        "g_q_lora": gain(ks[4], (DEPTH, MLA_Q_LORA)),
        "w_uq": nrm(ks[5], (DEPTH, MLA_Q_LORA, MLA_HEADS * MLA_QK), MLA_Q_LORA ** -0.5),
        "g_kv_lora": gain(ks[6], (DEPTH, MLA_KV_LORA)),
        "w_ukv": nrm(ks[7], (DEPTH, MLA_KV_LORA, MLA_HEADS * (MLA_NOPE + MLA_V)), MLA_KV_LORA ** -0.5),
        "g_qk_q": gain(ks[8], (DEPTH, MLA_QK)),
        "g_qk_k": gain(ks[9], (DEPTH, MLA_QK)),
        "w_mla_out": nrm(ks[10], (DEPTH, MLA_HEADS * MLA_V, D_MODEL), (MLA_HEADS * MLA_V) ** -0.5),
        "g_ret_gn": gain(ks[11], (DEPTH, RET_HEADS * RET_DV)),
        "w_ret_out": nrm(ks[12], (DEPTH, RET_HEADS * RET_DV, D_MODEL), (RET_HEADS * RET_DV) ** -0.5),
        "w_mix_out": nrm(ks[13], (DEPTH, D_MODEL, D_MODEL), D_MODEL ** -0.5),
        "g_ffn": gain(ks[14], (DEPTH, D_MODEL)),
        "w_peer_q": nrm(ks[15], (DEPTH, D_MODEL, PEER_HEADS * PEER_DQ), D_MODEL ** -0.5),
        "peer_keys_1": nrm(ks[16], (DEPTH, PEER_NKEYS, PEER_DQ // 2), (PEER_DQ // 2) ** -0.5),
        "peer_keys_2": nrm(ks[17], (DEPTH, PEER_NKEYS, PEER_DQ // 2), (PEER_DQ // 2) ** -0.5),
        "peer_u": nrm(ks[18], (DEPTH, PEER_EXPERTS, D_MODEL), D_MODEL ** -0.5),
        "peer_v": nrm(ks[19], (DEPTH, PEER_EXPERTS, D_MODEL), PEER_HEADS ** -0.5),
    }

def first_block(x, meta_tokens, g_mix, w_in, g_q_lora, w_uq, g_kv_lora, w_ukv, g_qk_q, g_qk_k,
              w_mla_out, g_ret_gn, w_ret_out, w_mix_out, g_ffn, w_peer_q, peer_keys_1,
              peer_keys_2, peer_u, peer_v):
    B = x.shape[0]
    meta = jnp.broadcast_to(meta_tokens.astype(x.dtype)[None], (B, N_META, x.shape[-1]))
    h = jnp.concatenate([meta, x], axis=1)
    pos = jnp.arange(h.shape[1])
    for layer in range(DEPTH):
        h = h + mixer_sublayer(h, pos, g_mix[layer], w_in[layer], g_q_lora[layer], w_uq[layer],
                               g_kv_lora[layer], w_ukv[layer], g_qk_q[layer], g_qk_k[layer],
                               w_mla_out[layer], g_ret_gn[layer], w_ret_out[layer], w_mix_out[layer])
        if layer == DEPTH - 1:
            h = h[:, N_META:]
        h = h + peer_sublayer(h, g_ffn[layer], w_peer_q[layer], peer_keys_1[layer], peer_keys_2[layer],
                              peer_u[layer], peer_v[layer])
    return h


POOL_WINDOWS = (2, 4, 8, 16)
POOL_GROUPS = len(POOL_WINDOWS)
POOL_WIDTH = D_MODEL // 2
POOL_GW = POOL_WIDTH // POOL_GROUPS
N_HEADS = 16
HEAD_DIM = 64
N_KV_GROUPS = 2
HPG = N_HEADS // N_KV_GROUPS
NSA_WIDTH = N_HEADS * HEAD_DIM
KV_WIDTH = N_KV_GROUPS * HEAD_DIM
CMP_LEN = 32
CMP_STRIDE = 16
CMP_HIDDEN = 256
SEL_BLOCK = 64
N_SEL = 16
WINDOW = 512
Q_BLOCK = 64
SEL_BONUS = 1e4
NEG_INF = -1e30
ROPE_THETA = 10000.0
D_FF = 4 * D_MODEL
RMS_EPS = 1e-6
IN_SIZES_2 = (POOL_WIDTH, NSA_WIDTH, KV_WIDTH, KV_WIDTH, KV_WIDTH, KV_WIDTH, KV_WIDTH, KV_WIDTH, 3 * N_HEADS, 2 * D_MODEL)
N_IN = sum(IN_SIZES_2)
IN_SPLITS = tuple(int(v) for v in np.cumsum(IN_SIZES_2)[:-1])


def rms_norm(x, g):
    xf = x.astype(jnp.float32)
    y = xf * lax.rsqrt(jnp.mean(xf * xf, axis=-1, keepdims=True) + RMS_EPS)
    return (y * g.astype(jnp.float32)).astype(x.dtype)

def rope_tables(pos):
    inv = ROPE_THETA ** (-jnp.arange(0, HEAD_DIM, 2, dtype=jnp.float32) / HEAD_DIM)
    ang = pos.astype(jnp.float32)[:, None] * inv[None, :]
    ang = jnp.concatenate([ang, ang], axis=-1)
    return jnp.cos(ang), jnp.sin(ang)

def apply_rope(x, cos, sin):
    x1, x2 = jnp.split(x, 2, axis=-1)
    rot = jnp.concatenate([-x2, x1], axis=-1)
    y = x.astype(jnp.float32) * cos[:, None, :] + rot.astype(jnp.float32) * sin[:, None, :]
    return y.astype(x.dtype)

def masked_softmax(s, mask):
    s = jnp.where(mask, s.astype(jnp.float32), NEG_INF)
    return jnp.where(mask, jax.nn.softmax(s, axis=-1), 0.0)

def pool_mixer(u, w_pool, pool_scale):
    B, S, _ = u.shape
    uf = u.astype(jnp.float32)
    csum = jnp.pad(jnp.cumsum(uf, axis=1), ((0, 0), (1, 0), (0, 0)))
    t = jnp.arange(S)
    diffs = []
    for g, w in enumerate(POOL_WINDOWS):
        c = csum[:, :, g * POOL_GW:(g + 1) * POOL_GW]
        upper = c[:, 1:]
        lower = jnp.pad(c, ((0, 0), (w - 1, 0), (0, 0)))[:, :S]
        count = jnp.minimum(t + 1, w).astype(jnp.float32)[None, :, None]
        diffs.append((upper - lower) / count - uf[:, :, g * POOL_GW:(g + 1) * POOL_GW])
    d = jnp.stack(diffs, axis=2)
    y = jnp.einsum('bsgc,gcd->bsgd', d, w_pool.astype(jnp.float32)).reshape(B, S, POOL_WIDTH)
    return (y * pool_scale.astype(jnp.float32)).astype(u.dtype)

def compress(k, pe, w1, w2):
    B, S, G, dh = k.shape
    r = CMP_LEN // CMP_STRIDE
    n_chunks = S // CMP_STRIDE
    n_cmp = n_chunks - r + 1
    ch = k.reshape(B, n_chunks, CMP_STRIDE, G, dh)
    blocks = jnp.concatenate([ch[:, j:j + n_cmp] for j in range(r)], axis=2)
    blocks = blocks + pe[None, None, :, None, :]
    flat = blocks.transpose(0, 1, 3, 2, 4).reshape(B, n_cmp, G, CMP_LEN * dh)
    return jax.nn.gelu(flat @ w1) @ w2

def nsa_mixer(q, kc, vc, ks, vs, kw, vw, g_nsa, pe_k, pe_v, w_ck1, w_ck2, w_cv1, w_cv2):
    B, S = q.shape[:2]
    G, dh = N_KV_GROUPS, HEAD_DIM
    cos, sin = rope_tables(jnp.arange(S))
    q = apply_rope(q.reshape(B, S, N_HEADS, dh), cos, sin).reshape(B, S, G, HPG, dh)
    ks = apply_rope(ks.reshape(B, S, G, dh), cos, sin)
    kw = apply_rope(kw.reshape(B, S, G, dh), cos, sin)
    vs = vs.reshape(B, S, G, dh)
    vw = vw.reshape(B, S, G, dh)
    k_cmp = compress(kc.reshape(B, S, G, dh), pe_k, w_ck1, w_ck2)
    v_cmp = compress(vc.reshape(B, S, G, dh), pe_v, w_cv1, w_cv2)
    n_cmp = k_cmp.shape[1]
    cmp_start = jnp.arange(n_cmp) * CMP_STRIDE
    cmp_end = cmp_start + CMP_LEN - 1
    ccos, csin = rope_tables(cmp_end)
    k_cmp = apply_rope(k_cmp, ccos, csin)
    n_slc = S // SEL_BLOCK
    k_blk = ks.reshape(B, n_slc, SEL_BLOCK, G, dh).transpose(0, 3, 1, 2, 4)
    v_blk = vs.reshape(B, n_slc, SEL_BLOCK, G, dh).transpose(0, 3, 1, 2, 4)
    slc_start = jnp.arange(n_slc) * SEL_BLOCK
    slc_idx = jnp.arange(n_slc)
    overlap = ((cmp_start[:, None] <= slc_start[None, :] + SEL_BLOCK - 1)
               & (cmp_end[:, None] >= slc_start[None, :])).astype(jnp.float32)
    n_pick = min(N_SEL, n_slc)
    gather_blocks = jax.vmap(jax.vmap(lambda kb, i: kb[i]))
    win_len = Q_BLOCK + WINDOW - 1
    kw_pad = jnp.pad(kw, ((0, 0), (WINDOW - 1, 0), (0, 0), (0, 0)))
    vw_pad = jnp.pad(vw, ((0, 0), (WINDOW - 1, 0), (0, 0), (0, 0)))
    scale = HEAD_DIM ** -0.5
    gates = jax.nn.sigmoid(g_nsa.astype(jnp.float32)).reshape(B, S, G, HPG, 3)

    def block(s0):
        t = s0 + jnp.arange(Q_BLOCK)
        qb = lax.dynamic_slice_in_dim(q, s0, Q_BLOCK, axis=1)
        gb = lax.dynamic_slice_in_dim(gates, s0, Q_BLOCK, axis=1)
        s_c = jnp.einsum('bqghd,bngd->bghqn', qb, k_cmp) * scale
        p_c = masked_softmax(s_c, cmp_end[None, :] <= t[:, None])
        o_c = jnp.einsum('bghqn,bngd->bqghd', p_c, v_cmp)
        imp = jnp.einsum('bghqn,nj->bgqj', p_c, overlap)
        causal = slc_start[None, :] <= t[:, None]
        cur = t // SEL_BLOCK
        forced = causal & ((slc_idx[None, :] == 0) | (slc_idx[None, :] >= cur[:, None] - 1))
        score = jnp.where(forced, SEL_BONUS, jnp.where(causal, imp, NEG_INF))
        top_v, idx = lax.top_k(score, n_pick)
        sel_ok = top_v > 0.5 * NEG_INF
        idx_flat = idx.reshape(B, G, Q_BLOCK * n_pick)
        k_sel = gather_blocks(k_blk, idx_flat).reshape(B, G, Q_BLOCK, n_pick * SEL_BLOCK, dh)
        v_sel = gather_blocks(v_blk, idx_flat).reshape(B, G, Q_BLOCK, n_pick * SEL_BLOCK, dh)
        key_pos = idx[..., None] * SEL_BLOCK + jnp.arange(SEL_BLOCK)
        ok = (sel_ok[..., None] & (key_pos <= t[:, None, None])).reshape(B, G, Q_BLOCK, n_pick * SEL_BLOCK)
        s_s = jnp.einsum('bqghd,bgqkd->bghqk', qb, k_sel) * scale
        p_s = masked_softmax(s_s, ok[:, :, None])
        o_s = jnp.einsum('bghqk,bgqkd->bqghd', p_s, v_sel)
        kwb = lax.dynamic_slice_in_dim(kw_pad, s0, win_len, axis=1)
        vwb = lax.dynamic_slice_in_dim(vw_pad, s0, win_len, axis=1)
        kpos = s0 - (WINDOW - 1) + jnp.arange(win_len)
        wmask = (kpos[None, :] <= t[:, None]) & (kpos[None, :] > t[:, None] - WINDOW) & (kpos[None, :] >= 0)
        s_w = jnp.einsum('bqghd,bkgd->bghqk', qb, kwb) * scale
        p_w = masked_softmax(s_w, wmask)
        o_w = jnp.einsum('bghqk,bkgd->bqghd', p_w, vwb)
        o = gb[..., 0:1] * o_c + gb[..., 1:2] * o_s + gb[..., 2:3] * o_w
        return o.reshape(B, Q_BLOCK, NSA_WIDTH)

    out = lax.map(block, jnp.arange(S // Q_BLOCK) * Q_BLOCK)
    return out.transpose(1, 0, 2, 3).reshape(B, S, NSA_WIDTH)

def second_inputs(seed: int = 0) -> dict:
    key = jax.random.key(seed)
    ks = jax.random.split(key, 20)
    f32 = jnp.float32

    def nrm(k, shape, fan_in):
        return jax.random.normal(k, shape, f32) * (fan_in ** -0.5)

    return {
        'x': jax.random.normal(ks[0], (BATCH, SEQ, D_MODEL), f32),
        'norm_mix': 1.0 + 0.05 * jax.random.normal(ks[1], (DEPTH, D_MODEL), f32),
        'w_in': nrm(ks[2], (DEPTH, D_MODEL, N_IN), D_MODEL),
        'w_pool': nrm(ks[3], (DEPTH, POOL_GROUPS, POOL_GW, POOL_GW), POOL_GW),
        'pool_scale': 1.0 + 0.1 * jax.random.normal(ks[4], (DEPTH, POOL_WIDTH), f32),
        'pe_k': 0.1 * jax.random.normal(ks[5], (DEPTH, CMP_LEN, HEAD_DIM), f32),
        'pe_v': 0.1 * jax.random.normal(ks[6], (DEPTH, CMP_LEN, HEAD_DIM), f32),
        'w_ck1': nrm(ks[7], (DEPTH, CMP_LEN * HEAD_DIM, CMP_HIDDEN), CMP_LEN * HEAD_DIM),
        'w_ck2': nrm(ks[8], (DEPTH, CMP_HIDDEN, HEAD_DIM), CMP_HIDDEN),
        'w_cv1': nrm(ks[9], (DEPTH, CMP_LEN * HEAD_DIM, CMP_HIDDEN), CMP_LEN * HEAD_DIM),
        'w_cv2': nrm(ks[10], (DEPTH, CMP_HIDDEN, HEAD_DIM), CMP_HIDDEN),
        'w_proj_pool': nrm(ks[11], (DEPTH, POOL_WIDTH, D_MODEL), POOL_WIDTH),
        'w_proj_nsa': nrm(ks[12], (DEPTH, NSA_WIDTH, D_MODEL), NSA_WIDTH),
        'w_out': nrm(ks[13], (DEPTH, D_MODEL, D_MODEL), D_MODEL),
        'norm_mlp': 1.0 + 0.05 * jax.random.normal(ks[14], (DEPTH, D_MODEL), f32),
        'w_ff1': nrm(ks[15], (DEPTH, D_MODEL, D_FF), D_MODEL),
        'w_ff2': nrm(ks[16], (DEPTH, D_FF, D_MODEL), D_FF),
        'norm_final': 1.0 + 0.05 * jax.random.normal(ks[17], (D_MODEL,), f32),
    }

def second_block(x, norm_mix, w_in, w_pool, pool_scale, pe_k, pe_v, w_ck1, w_ck2, w_cv1, w_cv2,
              w_proj_pool, w_proj_nsa, w_out, norm_mlp, w_ff1, w_ff2, norm_final):
    for l in range(DEPTH):
        h = rms_norm(x, norm_mix[l])
        proj = h @ w_in[l]
        u, q, kc, vc, ksl, vsl, kwn, vwn, g_nsa, g_merge = jnp.split(proj, IN_SPLITS, axis=-1)
        y_pool = pool_mixer(u, w_pool[l], pool_scale[l])
        y_nsa = nsa_mixer(q, kc, vc, ksl, vsl, kwn, vwn, g_nsa, pe_k[l], pe_v[l],
                          w_ck1[l], w_ck2[l], w_cv1[l], w_cv2[l]).astype(x.dtype)
        g_a, g_b = jnp.split(jax.nn.sigmoid(g_merge.astype(jnp.float32)).astype(x.dtype), 2, axis=-1)
        merged = g_a * (y_pool @ w_proj_pool[l]) + g_b * (y_nsa @ w_proj_nsa[l])
        x = x + merged @ w_out[l]
        h = rms_norm(x, norm_mlp[l])
        x = x + jnp.square(jax.nn.relu(h @ w_ff1[l])) @ w_ff2[l]
    return rms_norm(x, norm_final)


def setup_inputs(seed=0):
    out = dict(first_inputs(seed))
    for name, value in second_inputs(seed + 1).items():
        if name != "x":
            out[name + "_2"] = value
    return out


def reference(
    x, meta_tokens, g_mix, w_in, g_q_lora, w_uq, g_kv_lora, w_ukv, g_qk_q, g_qk_k, w_mla_out,
    g_ret_gn, w_ret_out, w_mix_out, g_ffn, w_peer_q, peer_keys_1, peer_keys_2, peer_u, peer_v,
    norm_mix_2, w_in_2, w_pool_2, pool_scale_2, pe_k_2, pe_v_2, w_ck1_2, w_ck2_2, w_cv1_2,
    w_cv2_2, w_proj_pool_2, w_proj_nsa_2, w_out_2, norm_mlp_2, w_ff1_2, w_ff2_2, norm_final_2,
):
    x = first_block(
        x, meta_tokens, g_mix, w_in, g_q_lora, w_uq, g_kv_lora, w_ukv, g_qk_q, g_qk_k,
        w_mla_out, g_ret_gn, w_ret_out, w_mix_out, g_ffn, w_peer_q, peer_keys_1, peer_keys_2,
        peer_u, peer_v,
    )
    return second_block(
        x, norm_mix_2, w_in_2, w_pool_2, pool_scale_2, pe_k_2, pe_v_2, w_ck1_2, w_ck2_2,
        w_cv1_2, w_cv2_2, w_proj_pool_2, w_proj_nsa_2, w_out_2, norm_mlp_2, w_ff1_2, w_ff2_2,
        norm_final_2,
    )


_drawn_inputs = setup_inputs


def setup_inputs(seed=0):
    import zlib

    import numpy as np

    out = dict(_drawn_inputs(seed))
    spreads = {}
    factors = {'g_q_lora': 7.112,
     'g_kv_lora': 6.195,
     'g_qk_q': 7.521,
     'g_qk_k': 6.839,
     'g_ret_gn': 24.659,
     'pe_k_2': 57.013,
     'pe_v_2': 36.078,
     'g_ffn': 7.332,
     'norm_mix_2': 7.263,
     'pool_scale_2': 4.249,
     'w_ck1_2': 5.246,
     'w_ck2_2': 5.031,
     'norm_mlp_2': 3.056}
    for name, (base, spread) in spreads.items():
        noise = np.random.default_rng([zlib.crc32(name.encode()), seed]).standard_normal(out[name].shape)
        drawn = base * np.exp(spread * noise) if base else spread * noise
        out[name] = __import__('jax').numpy.asarray(drawn.astype(out[name].dtype))
    for name, factor in factors.items():
        out[name] = (out[name] * factor).astype(out[name].dtype)
    return out
```

```python
from contextlib import ExitStack

import numpy as np

import concourse.bass as bass
from concourse import mybir

F32 = mybir.dt.float32
U32 = mybir.dt.uint32
ALU = mybir.AluOpType
ACT = mybir.ActivationFunctionType
AX_X = mybir.AxisListType.X

P = 128
D = 1024
S = 512
NT = S // P
META = 16
L = META + S
KT = D // P
EPS = 1e-6
NEG = -1e30
LOWEST = -3.0e38

Q_LORA, KV_LORA, MH, NOPE, MROPE, MV = 384, 256, 8, 64, 32, 64
QK = NOPE + MROPE
RH, RDK, RDV = 8, 64, 128
PH, PK, TOPK = 8, 128, 16
PICKS = PH * TOPK
C_Q, C_KV, C_RQ, C_RK = 0, Q_LORA, Q_LORA + KV_LORA + MROPE, Q_LORA + KV_LORA + MROPE + RH * RDK
C_RV = C_RK + RH * RDK
C_RG = C_RV + RH * RDV
C_ZA = C_RG + RH * RDV
C_ZR = C_ZA + D

POOL_W, WINDOWS = 512, (2, 4, 8, 16)
NH, HD, NG = 16, 64, 2
HPG = NH // NG
KVW = NG * HD
CMP_LEN, CMP_STRIDE, CMP_HID = 32, 16, 256
NCMP = S // CMP_STRIDE - CMP_LEN // CMP_STRIDE + 1
WINDOW, SEL_BLOCK, N_SEL = 512, 64, 16
D_FF = 4 * D
E_Q = POOL_W
E_KC = E_Q + NH * HD
E_KS = E_KC + 2 * KVW
E_GN = E_KS + 4 * KVW
E_GM = E_GN + 3 * NH

RING = 4
SLAB = KT * 512
BANKS = 8
GATHERS = 8
PAD = 16


def constants():
    def rope(pos, half):
        inv = (10000.0 ** (-np.arange(half, dtype=np.float32) / half)).astype(np.float32)
        ang = (np.asarray(pos, np.float32)[:, None] * inv[None]).astype(np.float32)
        return np.stack([np.cos(ang), np.sin(ang)], 1).astype(np.float32)

    def tiles(a, tiles_with_meta):
        out = np.zeros((P, NT + tiles_with_meta) + a.shape[1:], np.float32)
        if tiles_with_meta:
            out[:META, 0] = a[:META]
            a = a[META:]
        out[:, tiles_with_meta:] = a.reshape((NT, P) + a.shape[1:]).swapaxes(0, 1)
        return out

    r = np.arange(P)
    gamma = 1.0 - 2.0 ** (-5.0 - np.arange(RH))
    steps = np.arange(L)[None, :] - r[:, None]
    decay = np.where(steps[:, None] >= 0, gamma[None, :, None] ** np.maximum(steps, 0)[:, None] * RDK ** -0.5, 0.0)
    t = np.arange(S)
    ends = np.arange(NCMP) * CMP_STRIDE + CMP_LEN - 1
    seen = (ends[None] <= t[:, None]).astype(np.float32)
    counts = np.stack([1.0 / np.minimum(t + 1, w) for w in WINDOWS])
    c = {
        "identity": np.eye(P),
        "rope_mla": tiles(rope(np.arange(L), MROPE // 2), 1),
        "rope_ret": tiles(rope(np.arange(L), RDK // 2), 1),
        "rope_nsa": tiles(rope(t, HD // 2), 0),
        "rope_cmp": rope(ends, HD // 2),
        "decay": decay,
        "causal": np.where(r[None, :] <= r[:, None], 0.0, NEG),
        "cmp_bias": tiles(np.where(seen > 0, 0.0, NEG), 0),
        "cmp_seen": tiles(seen, 0),
        "inv_count": np.broadcast_to(counts[None], (P,) + counts.shape),
        "iota": np.broadcast_to(np.arange(TOPK)[None], (P, TOPK)),
    }
    return {k: np.ascontiguousarray(v, dtype=np.float32) for k, v in c.items()}


class Core:

    def __init__(self, nc):
        self.nc = nc
        self.w = self.psum = self.h = self.identity = self.gain = self.semaphore = None


class Item:

    def __init__(self, q, keys, columns, biases, blocks, seen, gate, out, add):
        self.q, self.keys, self.columns, self.biases = q, keys, columns, biases
        self.blocks, self.seen, self.gate, self.out, self.add = blocks, seen, gate, out, add


def linker(eng, sem):
    count = [0]

    def link(ins):
        count[0] += 1
        ins.then_inc(sem, 1)
        eng.wait_ge(sem, count[0])
    return link


def weight_plan(a):
    def cols(w, c0, n, kt=KT, k0=0):
        return w.rearrange("(k p) n -> p k n", p=P)[:, k0:k0 + kt, c0:c0 + n]

    plan = [("cq", cols(a["w_in"], C_Q, Q_LORA), NT), ("ckv", cols(a["w_in"], C_KV, KV_LORA + MROPE), NT + 1)]
    plan += [(("uq", b), cols(a["w_uq"], 384 * b, 384, 3), NT) for b in range(2)]
    plan += [(("ukv", b), cols(a["w_ukv"], 512 * b, 512, 2), NT + 1) for b in range(2)]
    plan += [("rq", cols(a["w_in"], C_RQ, 512), NT), ("rk", cols(a["w_in"], C_RK, 512), NT + 1)]
    plan += [(("rv", b), cols(a["w_in"], C_RV + 512 * b, 512), NT + 1) for b in range(2)]
    plan += [(("rg", b), cols(a["w_in"], C_RG + 512 * b, 512), 4) for b in range(2)]
    for b in range(2):
        plan += [(("za", b), cols(a["w_in"], C_ZA + 512 * b, 512), 4), (("ya", b), cols(a["w_mla_out"], 512 * b, 512, 4), 4),
                 (("zr", b), cols(a["w_in"], C_ZR + 512 * b, 512), 4), (("yr", b), cols(a["w_ret_out"], 512 * b, 512), 4)]
    plan += [(("mix", b), cols(a["w_mix_out"], 512 * b, 512), NT) for b in range(2)]
    plan += [(("pq", b), cols(a["w_peer_q"], 512 * b, 512), 4) for b in range(2)]
    plan += [("u", cols(a["w_in2"], 0, 512), 4)]
    plan += [(("q", b), cols(a["w_in2"], E_Q + 512 * b, 512), NT) for b in range(2)]
    plan += [("kcvc", a["w_kcvc"].rearrange("(k p) n -> p k n", p=P), 4), ("kv", cols(a["w_in2"], E_KS, 512), NT),
             ("gn", cols(a["w_in2"], E_GN, 3 * NH), NT)]
    plan += [("ck1", a["w_ck1"], 2), ("cv1", a["w_cv1"], 2)]
    for b in range(2):
        plan += [(("ga", b), cols(a["w_in2"], E_GM + 512 * b, 512), 4), (("yp", b), cols(a["w_proj_pool"], 512 * b, 512, 4), 4),
                 (("gb", b), cols(a["w_in2"], E_GM + D + 512 * b, 512), 4), (("yn", b), cols(a["w_proj_nsa"], 512 * b, 512), 4)]
    plan += [(("out", b), cols(a["w_out"], 512 * b, 512), NT) for b in range(2)]
    plan += [(("ff1", b), cols(a["w_ff1"], 512 * b, 512), 4) for b in range(D_FF // 512)]
    plan += [(("ff2", b, k), cols(a["w_ff2"], 512 * b, 512, KT, KT * k), NT) for b in range(2) for k in range(4)]
    return plan


class Weights:

    def __init__(self, nc, ctx, plan):
        self.nc, self.plan = nc, plan
        self.ring = ctx.enter_context(nc.sbuf_tensor("weight_ring", [P, RING, SLAB], F32))
        self.landed = [ctx.enter_context(nc.semaphore(f"slab_landed{r}")) for r in range(RING)]
        self.products_done = ctx.enter_context(nc.semaphore("products_done"))
        self.number = {name: i for i, (name, _, _) in enumerate(plan)}
        self.products = [0]
        for _, _, n in plan:
            self.products.append(self.products[-1] + n)
        self.loaded = 0

    def view(self, name):
        i = self.number[name]
        _, kt, n = self.plan[i][1].shape
        return self.ring[:, i % RING, 0:kt * n].rearrange("p (k n) -> p k n", k=kt)

    def load_through(self, sp, name):
        last = -1 if name is None else self.number[name]
        while self.loaded < min(last + 1 + RING, len(self.plan)):
            i = self.loaded
            if i >= RING:
                sp.wait_ge(self.products_done, self.products[i - RING + 1])
            sp.dma_start(self.view(self.plan[i][0]), self.plan[i][1]).then_inc(self.landed[i % RING], 16)
            self.loaded += 1

    def arrived(self, pe, name):
        i = self.number[name]
        pe.wait_ge(self.landed[i % RING], 16 * (i // RING + 1))

    def product(self, name, j):
        return self.products[self.number[name]] + j + 1


def row_tile(t):
    return (META, slice(0, META)) if t == 0 else (P, slice(META + P * (t - 1), META + P * t))


def evacuations(owners, n):
    return owners[:n + 1].count(owners[n])


def token_major(g, name, t, xT, columns, rows):
    w = g.w.view(name)
    return (name, t, rows, w.shape[2], [(xT[:, k, columns], w[:, k, :]) for k in range(w.shape[1])])


def feature_major(g, name, j, xT, columns):
    w = g.w.view(name)
    return (name, j, P, S, [(w[:, k, P * j:P * j + P], xT[:, k, columns]) for k in range(w.shape[1])])


def multiply(g, pe, products, owners, drained):
    for n, (name, j, rows, cols, pairs) in enumerate(products):
        if j == 0:
            g.w.arrived(pe, name)
        if n >= BANKS:
            pe.wait_ge(drained[owners[n - BANKS]], evacuations(owners, n - BANKS))
        for k, (lhsT, rhs) in enumerate(pairs):
            mm = g.nc.tensor.matmul(g.psum[0:rows, n % BANKS, 0:cols], lhsT, rhs, start=(k == 0),
                                    stop=(k == len(pairs) - 1))
        mm.then_inc(g.w.products_done, 1)


def product_stage(g, tag, products, outputs, last_slab, functions=None):
    nc = g.nc
    functions = functions or [None] * len(products)
    owners = ["act" if functions[n] or n % 2 else "dve" for n in range(len(products))]
    with ExitStack() as ctx:
        drained = {e: g.semaphore(f"{tag}_drained_{e}") for e in ("act", "dve")}
        block = ctx.enter_context(nc.Block())

        @block.sync
        def _(sp):
            g.w.load_through(sp, last_slab)

        @block.tensor
        def _(pe):
            multiply(g, pe, products, owners, drained)

        @block.scalar
        def _(act):
            for n, (name, j, rows, cols, _) in enumerate(products):
                if owners[n] == "act":
                    act.wait_ge(g.w.products_done, g.w.product(name, j))
                    nc.scalar.activation(outputs[n], g.psum[0:rows, n % BANKS, 0:cols],
                                         functions[n] or ACT.Copy).then_inc(drained["act"], 1)

        @block.vector
        def _(dve):
            for n, (name, j, rows, cols, _) in enumerate(products):
                if owners[n] == "dve":
                    dve.wait_ge(g.w.products_done, g.w.product(name, j))
                    nc.vector.tensor_copy(outputs[n], g.psum[0:rows, n % BANKS, 0:cols]).then_inc(drained["dve"], 1)


def residual_stage(g, tag, names, xT, last_slab):
    nc = g.nc
    products = [token_major(g, names[b], t, xT, slice(P * t, P * t + P), P) for b in range(2) for t in range(NT)]
    with ExitStack() as ctx:
        drained = {"dve": g.semaphore(f"{tag}_drained")}
        block = ctx.enter_context(nc.Block())

        @block.sync
        def _(sp):
            g.w.load_through(sp, last_slab)

        @block.tensor
        def _(pe):
            multiply(g, pe, products, ["dve"] * len(products), drained)

        @block.vector
        def _(dve):
            for n, (name, t, rows, cols, _) in enumerate(products):
                h = g.h[:, t, 512 * (n // NT):512 * (n // NT) + 512]
                dve.wait_ge(g.w.products_done, g.w.product(name, t))
                nc.vector.tensor_tensor(h, h, g.psum[:, n % BANKS, :], ALU.add).then_inc(drained["dve"], 1)


def norm_stage(g, tag, sources, width, outT=None, gain_columns=None, token_out=None, gain_rows=None, loads=None,
               store=None):
    nc = g.nc
    n, chunks = len(sources), width // P
    with ExitStack() as ctx:
        sb = lambda name, shape: ctx.enter_context(nc.sbuf_tensor(f"{tag}_{name}", shape, F32))
        sem = lambda name: g.semaphore(f"{tag}_{name}")
        junk = sb("squares", [P, width])
        sums, mean, root, inverse = (sb(x, [P, n]) for x in ("sums", "mean", "root", "inverse"))
        scaled = token_out if token_out is not None else sb("scaled", [P, 2, width])
        s_in, s_zero, s_sq, s_mean, s_root, s_inv = (sem(x) for x in ("in", "zero", "sq", "mean_ready", "root_ready", "inv"))
        s_scaled, s_turned, s_drained, s_out = (sem(x) for x in ("scaled_ready", "turned", "drained", "out"))
        n_loads = len(loads) if loads else 0
        block = ctx.enter_context(nc.Block())

        def buffer(t):
            return scaled[:, t if token_out is not None else t % 2, :]

        @block.sync
        def _(sp):
            for dst, src in loads or ():
                sp.dma_start(dst, src).then_inc(s_in, 16)
            if loads:
                g.w.load_through(sp, None)
            if store is not None:
                for t in range(n):
                    sp.wait_ge(s_scaled, t + 1)
                    sp.dma_start(store[:, t, :], token_out[:, t, :]).then_inc(s_out, 16)
                sp.wait_ge(s_out, 16 * n)

        @block.scalar
        def _(act):
            act.wait_ge(s_zero, 1)
            if loads:
                act.wait_ge(s_in, 16 * n_loads)
            for t, (src, rows, _) in enumerate(sources):
                if t:
                    act.wait_ge(s_sq, t)
                nc.scalar.activation(junk[0:rows], src, ACT.Square, accum_out=sums[0:rows, t:t + 1]).then_inc(s_sq, 1)
            act.wait_ge(s_mean, 1)
            nc.scalar.activation(root[:], mean[:], ACT.Sqrt).then_inc(s_root, 1)

        def drain(dve, t):
            _, rows, columns = sources[t]
            dve.wait_ge(s_turned, t + 1)
            for c in range(0, chunks, 4):
                m = min(4, chunks - c)
                src = g.psum[:, 2 * (t % 2) + c // 4, :].rearrange("p (c r) -> p c r", c=4)[:, 0:m, 0:rows]
                if gain_columns is None:
                    ins = nc.vector.tensor_copy(outT[:, c:c + m, columns], src)
                else:
                    ins = nc.vector.tensor_tensor(outT[:, c:c + m, columns], src,
                                                  gain_columns[:, c:c + m].unsqueeze(2).to_broadcast([P, m, rows]), ALU.mult)
            ins.then_inc(s_drained, 1)

        @block.vector
        def _(dve):
            nc.vector.memset(sums[:], 1.0).then_inc(s_zero, 1)
            dve.wait_ge(s_sq, n)
            nc.vector.tensor_scalar(mean[:], sums[:], 1.0 / width, EPS, ALU.mult, ALU.add).then_inc(s_mean, 1)
            dve.wait_ge(s_root, 1)
            nc.vector.reciprocal(inverse[:], root[:]).then_inc(s_inv, 1)
            dve.wait_ge(s_inv, 1)
            for t, (src, rows, _) in enumerate(sources):
                if token_out is not None:
                    nc.vector.scalar_tensor_tensor(out=buffer(t)[0:rows], in0=src, scalar=inverse[0:rows, t:t + 1],
                                                   in1=gain_rows, op0=ALU.mult, op1=ALU.mult).then_inc(s_scaled, 1)
                else:
                    if t >= 2:
                        dve.wait_ge(s_turned, t - 1)
                    nc.vector.tensor_scalar(buffer(t)[0:rows], src, inverse[0:rows, t:t + 1], None,
                                            ALU.mult).then_inc(s_scaled, 1)
                if outT is not None and t >= 1:
                    drain(dve, t - 1)
            if outT is not None:
                drain(dve, n - 1)

        if outT is not None:
            @block.tensor
            def _(pe):
                for t, (_, rows, _) in enumerate(sources):
                    pe.wait_ge(s_scaled, t + 1)
                    if t >= 2:
                        pe.wait_ge(s_drained, t - 1)
                    for c in range(chunks):
                        mm = nc.tensor.transpose(g.psum[:, 2 * (t % 2) + c // 4, P * (c % 4):P * (c % 4) + rows],
                                                 buffer(t)[0:rows, P * c:P * c + P], g.identity[0:rows, 0:rows])
                    mm.then_inc(s_turned, 1)


def turn_stage(g, tag, sources, rows_out, scale=1.0):
    nc = g.nc
    with ExitStack() as ctx:
        s_turned = g.semaphore(f"{tag}_turned")
        s_drained = [g.semaphore(f"{tag}_drained{e}") for e in range(2)]
        block = ctx.enter_context(nc.Block())

        def bank(n, m, rows):
            return g.psum[0:rows_out, n % BANKS, :].rearrange("p (c r) -> p c r", c=4)[:, 0:m, 0:rows]

        @block.tensor
        def _(pe):
            for n, (blocks, rows, _) in enumerate(sources):
                if n >= BANKS:
                    pe.wait_ge(s_drained[n % 2], (n - BANKS) // 2 + 1)
                for c, src in enumerate(blocks):
                    mm = nc.tensor.transpose(g.psum[0:rows_out, n % BANKS, P * c:P * c + rows], src,
                                             g.identity[0:rows, 0:rows])
                mm.then_inc(s_turned, 1)

        @block.scalar
        def _(act):
            for n, (blocks, rows, dst) in enumerate(sources):
                if n % 2 == 0:
                    act.wait_ge(s_turned, n + 1)
                    nc.scalar.activation(dst, bank(n, len(blocks), rows), ACT.Copy, scale=scale).then_inc(s_drained[0], 1)

        @block.vector
        def _(dve):
            for n, (blocks, rows, dst) in enumerate(sources):
                if n % 2 == 1:
                    dve.wait_ge(s_turned, n + 1)
                    nc.vector.tensor_scalar(dst, bank(n, len(blocks), rows), scale, None, ALU.mult).then_inc(s_drained[1], 1)


def rope(nc, link, dst, src, table, tmp):
    shape = list(src.shape)
    cos = table[:, 0, :].unsqueeze(1).unsqueeze(1).to_broadcast(shape)
    sin = table[:, 1, :].unsqueeze(1).unsqueeze(1).to_broadcast(shape)
    nc.vector.tensor_tensor(tmp[0], src, cos, ALU.mult)
    link(nc.vector.tensor_tensor(tmp[1], src, sin, ALU.mult))
    nc.vector.tensor_tensor(dst[:, :, 0, :], tmp[0][:, :, 0, :], tmp[1][:, :, 1, :], ALU.subtract)
    link(nc.vector.tensor_tensor(dst[:, :, 1, :], tmp[1][:, :, 0, :], tmp[0][:, :, 1, :], ALU.add))


def rope_stage(g, tag, jobs, width):
    nc = g.nc
    with ExitStack() as ctx:
        tmp = [ctx.enter_context(nc.sbuf_tensor(f"{tag}_tmp{i}", [P, width], F32)) for i in range(2)]
        s_link = g.semaphore(f"{tag}_link")
        block = ctx.enter_context(nc.Block())

        @block.vector
        def _(dve):
            link = linker(dve, s_link)
            for dst, src, table in jobs:
                rows, heads, _, half = src.shape
                views = [x[0:rows, 0:heads * 2 * half].rearrange("p (h a b) -> p h a b", h=heads, a=2) for x in tmp]
                rope(nc, link, dst, src, table, views)


def mla_qk_stage(g, q, kv, k_pe, q_gain, k_gain, rope_table, k_heads):
    nc = g.nc
    with ExitStack() as ctx:
        sb = lambda name, shape: ctx.enter_context(nc.sbuf_tensor(f"mla_{name}", shape, F32))
        sem = lambda name: g.semaphore(f"mla_{name}")
        n = 2 * NT + 1
        squares = sb("head_squares", [P, MH, QK])
        sums, mean, root, inverse = (sb(x, [P, n, MH]) for x in ("head_sums", "head_mean", "head_root", "head_inverse"))
        tmp = [sb(f"rope_tmp{i}", [P, MH * MROPE]) for i in range(2)]
        s_link, s_mean, s_root = sem("qk_link"), sem("qk_mean"), sem("qk_root")
        block = ctx.enter_context(nc.Block())
        units = []
        for t in range(NT):
            x = q[:, t, :].rearrange("p (h d) -> p h d", h=MH)
            units.append((P, x[:, :, 0:NOPE], x[:, :, NOPE:QK], x, q_gain, t + 1))
        for t in range(NT + 1):
            rows, _ = row_tile(t)
            nope = kv[0:rows, t, :].rearrange("p (h d) -> p h d", h=MH)[:, :, 0:NOPE]
            pe_part = k_pe[0:rows, t, :].unsqueeze(1).to_broadcast([rows, MH, MROPE])
            units.append((rows, nope, pe_part, k_heads[0:rows, t, :].rearrange("p (h d) -> p h d", h=MH), k_gain, t))

        @block.scalar
        def _(act):
            act.wait_ge(s_mean, 1)
            nc.scalar.activation(root[:], mean[:], ACT.Sqrt).then_inc(s_root, 1)

        @block.vector
        def _(dve):
            link = linker(dve, s_link)
            link(nc.vector.memset(sums[:], 1.0))
            for i, (rows, nope, roped, _, _, _) in enumerate(units):
                nc.vector.tensor_tensor(squares[0:rows, :, 0:NOPE], nope, nope, ALU.mult)
                link(nc.vector.tensor_tensor(squares[0:rows, :, NOPE:QK], roped, roped, ALU.mult))
                link(nc.vector.tensor_reduce(sums[0:rows, i, :], squares[0:rows], AX_X, ALU.add))
            nc.vector.tensor_scalar(mean[:], sums[:], 1.0 / QK, EPS, ALU.mult, ALU.add).then_inc(s_mean, 1)
            dve.wait_ge(s_root, 1)
            link(nc.vector.reciprocal(inverse[:], root[:]))
            for i, (rows, nope, roped, dst, gain, t) in enumerate(units):
                scale = inverse[0:rows, i, :].unsqueeze(2)
                nc.vector.tensor_tensor(dst[:, :, 0:NOPE], nope, scale.to_broadcast([rows, MH, NOPE]), ALU.mult)
                link(nc.vector.tensor_tensor(dst[:, :, NOPE:QK], roped, scale.to_broadcast([rows, MH, MROPE]), ALU.mult))
                link(nc.vector.tensor_tensor(dst, dst, gain[0:rows].unsqueeze(1).to_broadcast([rows, MH, QK]), ALU.mult))
                x = dst[:, :, NOPE:QK].rearrange("p h (a b) -> p h a b", a=2)
                views = [v[0:rows].rearrange("p (h a b) -> p h a b", h=MH, a=2) for v in tmp]
                rope(nc, link, x, x, rope_table[0:rows, t, :, :], views)


def attention_stage(g, tag, items, head_dim, last_slab=None):
    nc = g.nc
    n_items = len(items)
    with ExitStack() as ctx:
        sb = lambda name, shape: ctx.enter_context(nc.sbuf_tensor(f"{tag}_{name}", shape, F32))
        sem = lambda name: g.semaphore(f"{tag}_{name}")
        probs = sb("probs", [P, 2, 1024])
        probsT = sb("probsT", [P, 2, 5 * P])
        negmax, rowsum, factor = sb("negmax", [P, 4]), sb("rowsum", [P, 8]), sb("factor", [P, 8])
        s_scores, s_max, s_exp, s_seen, s_turned = (sem(x) for x in ("scores", "max", "exp", "seen_done", "turned"))
        s_copied = [sem("copied_by_act"), sem("copied_by_dve")]
        s_values, s_out, s_link = sem("values"), sem("out_done"), sem("link")
        block = ctx.enter_context(nc.Block())
        with_mask = [it.seen is not None for it in items]

        def scores(i):
            return g.psum[:, 2 * (i % 2):2 * (i % 2) + 2, :].rearrange("p a b -> p (a b)")

        def turned(i, m, keys):
            if m < 4:
                return g.psum[0:keys, 4 + i % 2, P * m:P * m + P]
            return g.psum[0:keys, 6 + i % 2, P:2 * P]

        def values(i):
            return g.psum[:, 6 + i % 2, 0:head_dim]

        @block.sync
        def _(sp):
            if last_slab:
                g.w.load_through(sp, last_slab)

        @block.tensor
        def _(pe):
            for i in range(n_items + 2):
                if i < n_items:
                    it = items[i]
                    if i >= 2:
                        pe.wait_ge(s_exp, i - 1)
                    for (kT, col) in it.keys:
                        mine = [(b, c) for b, c in it.biases if col <= c < col + kT.shape[1]]
                        mm = nc.tensor.matmul(scores(i)[:, col:col + kT.shape[1]], it.q, kT, start=True, stop=not mine)
                        for b, c in mine:
                            mm = nc.tensor.matmul(scores(i)[:, c:c + b.shape[1]], g.identity[:], b, start=False, stop=True)
                    mm.then_inc(s_scores, 1)
                if i >= 2:
                    j, it = i - 2, items[i - 2]
                    pe.wait_ge(s_copied[j % 2], j // 2 + 1)
                    if j >= 2:
                        pe.wait_ge(s_out, j - 1)
                    for m, (_, keys, v) in enumerate(it.blocks):
                        mm = nc.tensor.matmul(values(j), probsT[0:keys, j % 2, P * m:P * m + P], v, start=(m == 0),
                                              stop=(m == len(it.blocks) - 1))
                    mm.then_inc(s_values, 1)
                if 1 <= i <= n_items:
                    j, it = i - 1, items[i - 1]
                    pe.wait_ge(s_exp, j + 1)
                    if it.seen is not None:
                        pe.wait_ge(s_seen, sum(with_mask[:j + 1]))
                    if j >= 2:
                        pe.wait_ge(s_copied[j % 2], (j - 2) // 2 + 1)
                    if j >= 2 and len(it.blocks) > 4:
                        pe.wait_ge(s_out, j - 1)
                    for m, (col, keys, _) in enumerate(it.blocks):
                        mm = nc.tensor.transpose(turned(j, m, keys), probs[:, j % 2, col:col + keys], g.identity[:])
                    mm.then_inc(s_turned, 1)

        def copy_turned(copy, j):
            blocks = items[j].blocks
            full = [m for m, b in enumerate(blocks) if m < 4 and b[1] == P]
            last = None
            if full:
                last = copy(probsT[:, j % 2, 0:P * len(full)], g.psum[:, 4 + j % 2, 0:P * len(full)])
            for m, (_, keys, _) in enumerate(blocks):
                if m not in full:
                    last = copy(probsT[0:keys, j % 2, P * m:P * m + P], turned(j, m, keys))
            last.then_inc(s_copied[j % 2], 1)

        @block.scalar
        def _(act):
            for i in range(n_items + 1):
                if i < n_items:
                    lo, hi = items[i].columns
                    act.wait_ge(s_max, i + 1)
                    if i >= 2:
                        act.wait_ge(s_turned, i - 1)
                    nc.scalar.activation(probs[:, i % 2, lo:hi], scores(i)[:, lo:hi], ACT.Exp, bias=negmax[:, i % 4:i % 4 + 1],
                                         accum_out=rowsum[:, i % 8:i % 8 + 1]).then_inc(s_exp, 1)
                if i >= 1 and (i - 1) % 2 == 0:
                    act.wait_ge(s_turned, i)
                    if i >= 3:
                        act.wait_ge(s_values, i - 2)
                    copy_turned(nc.scalar.copy, i - 1)

        @block.vector
        def _(dve):
            link = linker(dve, s_link)
            for i in range(n_items + 3):
                if i < n_items:
                    lo, hi = items[i].columns
                    dve.wait_ge(s_scores, i + 1)
                    nc.vector.tensor_reduce(negmax[:, i % 4:i % 4 + 1], scores(i)[:, lo:hi], AX_X, ALU.max,
                                            negate=True).then_inc(s_max, 1)
                if i >= 3:
                    j, it = i - 3, items[i - 3]
                    f = factor[:, j % 8:j % 8 + 1]
                    link(nc.vector.reciprocal(f, rowsum[:, j % 8:j % 8 + 1]))
                    if it.gate is not None:
                        link(nc.vector.tensor_tensor(f, f, it.gate, ALU.mult))
                    dve.wait_ge(s_values, j + 1)
                    if it.add:
                        dve.wait_ge(s_out, j)
                        ins = nc.vector.scalar_tensor_tensor(out=it.out, in0=values(j), scalar=f, in1=it.out, op0=ALU.mult,
                                                             op1=ALU.add)
                    else:
                        ins = nc.vector.tensor_scalar(it.out, values(j), f, None, ALU.mult)
                    ins.then_inc(s_out, 1)
                if 1 <= i <= n_items and items[i - 1].seen is not None:
                    j = i - 1
                    lo, hi = items[j].columns
                    dve.wait_ge(s_exp, j + 1)
                    p = probs[:, j % 2, lo:hi]
                    nc.vector.tensor_tensor(p, p, items[j].seen, ALU.mult).then_inc(s_seen, 1)
                if 1 <= i <= n_items and (i - 1) % 2 == 1:
                    dve.wait_ge(s_turned, i)
                    if i >= 3:
                        dve.wait_ge(s_values, i - 2)
                    copy_turned(nc.vector.tensor_copy, i - 1)


RET_Q0 = [0] + [P * t for t in range(NT)]
RET_OFF = [0, S, 2 * S, 3 * S - P, 4 * S - 3 * P]
RET_WIDTH = RET_OFF[-1] + P


def retention_stage(g, rqT, rkT, rv, decay, y, last_slab):
    nc = g.nc
    n_m = NT + 1
    with ExitStack() as ctx:
        sem = lambda name: g.semaphore(f"ret_{name}")
        decayed = ctx.enter_context(nc.sbuf_tensor("ret_decayed", [P, 2, RET_WIDTH], F32))
        s_scores, s_decayed, s_y, s_copied = (sem(x) for x in ("scores", "decayed_ready", "y_ready", "y_copied"))
        block = ctx.enter_context(nc.Block())

        @block.sync
        def _(sp):
            g.w.load_through(sp, last_slab)

        @block.tensor
        def _(pe):
            for h in range(RH + 1):
                if h < RH:
                    part = slice(RDK * (h % 2), RDK * (h % 2) + RDK)
                    for m in range(n_m):
                        n = n_m * h + m
                        rows, columns = row_tile(m)
                        if n >= 4:
                            pe.wait_ge(s_decayed, n - 3)
                        nc.tensor.matmul(g.psum[0:rows, n % 4, 0:S - RET_Q0[m]], rkT[part, h // 2, columns],
                                         rqT[part, h // 2, RET_Q0[m]:S], start=True, stop=True).then_inc(s_scores, 1)
                if h >= 1:
                    j = h - 1
                    pe.wait_ge(s_decayed, n_m * h)
                    if j >= 4:
                        pe.wait_ge(s_copied, j - 3)
                    for t in range(NT):
                        for m in range(t + 2):
                            rows, _ = row_tile(m)
                            at = RET_OFF[m] + P * t - RET_Q0[m]
                            mm = nc.tensor.matmul(g.psum[:, 4 + j % 4, RDV * t:RDV * t + RDV], decayed[0:rows, j % 2, at:at + P],
                                                  rv[0:rows, m, RDV * j:RDV * j + RDV], start=(m == 0), stop=(m == t + 1))
                    mm.then_inc(s_y, 1)

        @block.vector
        def _(dve):
            for h in range(RH):
                for m in range(n_m):
                    n = n_m * h + m
                    rows, _ = row_tile(m)
                    width = S - RET_Q0[m]
                    dve.wait_ge(s_scores, n + 1)
                    if m == 0 and h >= 2:
                        dve.wait_ge(s_y, h - 1)
                    d = decay[0:rows, h, META:L] if m == 0 else decay[0:rows, h, 0:width]
                    nc.vector.tensor_tensor(decayed[0:rows, h % 2, RET_OFF[m]:RET_OFF[m] + width],
                                            g.psum[0:rows, n % 4, 0:width], d, ALU.mult).then_inc(s_decayed, 1)

        @block.scalar
        def _(act):
            for h in range(RH):
                act.wait_ge(s_y, h + 1)
                nc.scalar.copy(y[:, h, :], g.psum[:, 4 + h % 4, :]).then_inc(s_copied, 1)


def group_norm_stage(g, y, gains, ynT):
    nc = g.nc
    with ExitStack() as ctx:
        sb = lambda name, shape: ctx.enter_context(nc.sbuf_tensor(f"gn_{name}", shape, F32))
        sem = lambda name: g.semaphore(f"gn_{name}")
        n = RH * NT
        stats, moments = sb("stats", [P, n, 6]), sb("moments", [P, n, 2])
        root, inverse = sb("root", [P, n]), sb("inverse", [P, n])
        s_link, s_var, s_root, s_normed, s_turned, s_drained = (
            sem(x) for x in ("link", "var", "root_ready", "normed", "turned", "drained"))
        block = ctx.enter_context(nc.Block())

        @block.vector
        def _(dve):
            link = linker(dve, s_link)
            for i in range(n):
                ins = nc.vector.bn_stats(stats[:, i, :], y[:, i // NT, RDV * (i % NT):RDV * (i % NT) + RDV])
            link(ins)
            for i in range(n):
                ins = nc.vector.bn_aggr(moments[:, i, :], stats[:, i, :])
            link(ins)
            nc.vector.tensor_scalar(inverse[:], moments[:, :, 1], EPS, None, ALU.add).then_inc(s_var, 1)
            dve.wait_ge(s_root, 1)
            link(nc.vector.reciprocal(inverse[:], root[:]))
            for i in range(n):
                yi = y[:, i // NT, RDV * (i % NT):RDV * (i % NT) + RDV]
                nc.vector.tensor_scalar(yi, yi, moments[:, i, 0:1], inverse[:, i:i + 1], ALU.subtract,
                                        ALU.mult).then_inc(s_normed, 1)

        @block.tensor
        def _(pe):
            for h in range(RH):
                pe.wait_ge(s_normed, NT * (h + 1))
                if h >= 4:
                    pe.wait_ge(s_drained, h - 3)
                for t in range(NT):
                    mm = nc.tensor.transpose(g.psum[:, h % 4, P * t:P * t + P], y[:, h, RDV * t:RDV * t + RDV], g.identity[:])
                mm.then_inc(s_turned, 1)

        @block.scalar
        def _(act):
            act.wait_ge(s_var, 1)
            nc.scalar.activation(root[:], inverse[:], ACT.Sqrt).then_inc(s_root, 1)
            for h in range(RH):
                act.wait_ge(s_turned, h + 1)
                nc.scalar.activation(ynT[:, h, :], g.psum[:, h % 4, :], ACT.Copy, scale=gains[:, h:h + 1]).then_inc(s_drained, 1)


def retention_gate_stage(g, hnT, ynT, last_slab):
    nc = g.nc
    products = [feature_major(g, ("rg", b), j, hnT, slice(META, L)) for b in range(2) for j in range(4)]
    with ExitStack() as ctx:
        gate = ctx.enter_context(nc.sbuf_tensor("rg_silu", [P, 2, S], F32))
        drained = {"act": g.semaphore("rg_drained")}
        s_used = g.semaphore("rg_used")
        block = ctx.enter_context(nc.Block())

        @block.sync
        def _(sp):
            g.w.load_through(sp, last_slab)

        @block.tensor
        def _(pe):
            multiply(g, pe, products, ["act"] * 8, drained)

        @block.scalar
        def _(act):
            for n, (name, j, _, _, _) in enumerate(products):
                act.wait_ge(g.w.products_done, g.w.product(name, j))
                if n >= 2:
                    act.wait_ge(s_used, n - 1)
                nc.scalar.activation(gate[:, n % 2, :], g.psum[:, n % BANKS, :], ACT.Silu).then_inc(drained["act"], 1)

        @block.vector
        def _(dve):
            for n in range(8):
                dve.wait_ge(drained["act"], n + 1)
                nc.vector.tensor_tensor(ynT[:, n, :], ynT[:, n, :], gate[:, n % 2, :], ALU.mult).then_inc(s_used, 1)


def merge_stage(g, tag, names, gate_input, gate_columns, inputs, mergedT, last_slab):
    nc = g.nc
    gate_a, prod_a, gate_b, prod_b = names
    products, owners = [], []
    for b in range(2):
        for gate, prod, x in ((gate_a, prod_a, inputs[0]), (gate_b, prod_b, inputs[1])):
            products += [feature_major(g, (gate, b), j, gate_input, gate_columns) for j in range(4)]
            products += [feature_major(g, (prod, b), j, x, slice(0, S)) for j in range(4)]
            owners += ["act"] * 4 + ["dve"] * 4
    with ExitStack() as ctx:
        gates = ctx.enter_context(nc.sbuf_tensor(f"{tag}_gates", [P, 8, S], F32))
        term = ctx.enter_context(nc.sbuf_tensor(f"{tag}_term", [P, 2, S], F32))
        drained = {e: g.semaphore(f"{tag}_drained_{e}") for e in ("act", "dve")}
        s_merged = g.semaphore(f"{tag}_merged")
        block = ctx.enter_context(nc.Block())

        @block.sync
        def _(sp):
            g.w.load_through(sp, last_slab)

        @block.tensor
        def _(pe):
            multiply(g, pe, products, owners, drained)

        @block.scalar
        def _(act):
            done = 0
            for n, (name, j, _, _, _) in enumerate(products):
                if owners[n] != "act":
                    continue
                act.wait_ge(g.w.products_done, g.w.product(name, j))
                if done >= 8:
                    act.wait_ge(drained["dve"], done - 7)
                nc.scalar.activation(gates[:, done % 8, :], g.psum[:, n % BANKS, :], ACT.Sigmoid).then_inc(drained["act"], 1)
                done += 1

        @block.vector
        def _(dve):
            done = 0
            for n, (name, j, _, _, _) in enumerate(products):
                if owners[n] != "dve":
                    continue
                second = (n // 8) % 2
                out = mergedT[:, 4 * (n // 16) + j, :]
                dve.wait_ge(g.w.products_done, g.w.product(name, j))
                dve.wait_ge(drained["act"], done + 1)
                nc.vector.tensor_tensor(term[:, j % 2, :] if second else out, g.psum[:, n % BANKS, :],
                                        gates[:, done % 8, :], ALU.mult).then_inc(drained["dve"], 1)
                done += 1
                if second:
                    dve.wait_ge(drained["dve"], done)
                    nc.vector.tensor_tensor(out, out, term[:, j % 2, :], ALU.add).then_inc(s_merged, 1)


def peer_select_stage(g, pqT, keysT, iota, expert, gates):
    nc = g.nc
    with ExitStack() as ctx:
        sb = lambda name, shape, dt=F32: ctx.enter_context(nc.sbuf_tensor(f"sel_{name}", shape, dt))
        sem = lambda name: g.semaphore(f"sel_{name}")
        rest = sb("rest", [P, PK])
        best = sb("best", [P, PH, 2, TOPK])
        at = sb("at", [P, PH, 2, TOPK], U32)
        at_f = sb("at_f", [P, PH, 2, TOPK])
        cand, cand_rest = sb("cand", [P, TOPK, TOPK]), sb("cand_rest", [P, TOPK * TOPK])
        top, pick = sb("top", [P, PH, TOPK]), sb("pick", [P, PH, TOPK], U32)
        part, part_f = sb("part", [P, 2, PH, TOPK], U32), sb("part_f", [P, 2, PH, TOPK])
        equal = sb("equal", [P, PH, TOPK, TOPK])
        number = sb("number", [P, 2, PH, TOPK])
        over, weight = sb("over", [P, PH, TOPK]), sb("weight", [P, PH, TOPK])
        total, inverse = sb("total", [P, PH]), sb("inverse", [P, PH])
        s_scores, s_taken, s_over, s_exp, s_link = (sem(x) for x in ("scores", "taken", "over_ready", "exp", "link"))
        block = ctx.enter_context(nc.Block())

        def scores(n):
            t, h, half = n // 16, n % 16 // 2, n % 2
            return g.psum[:, 4 * (t % 2) + 2 * half + h // 4, PK * (h % 4):PK * (h % 4) + PK]

        @block.tensor
        def _(pe):
            for t in range(NT):
                if t >= 2:
                    pe.wait_ge(s_taken, t - 1)
                for h in range(PH):
                    for half in range(2):
                        rows = slice(64 * half, 64 * half + 64)
                        mm = nc.tensor.matmul(scores(16 * t + 2 * h + half), pqT[rows, h, P * t:P * t + P], keysT[rows, :],
                                              start=True, stop=True)
                mm.then_inc(s_scores, 1)

        @block.scalar
        def _(act):
            for t in range(NT):
                act.wait_ge(s_over, t + 1)
                nc.scalar.activation(weight[:], over[:], ACT.Exp).then_inc(s_exp, 1)

        @block.vector
        def _(dve):
            link = linker(dve, s_link)

            def top16(values, numbers, src, scratch):
                link(nc.vector.max(values[:, 0:8], src))
                nc.vector.max_index(numbers[:, 0:8], values[:, 0:8], src)
                link(nc.vector.match_replace(scratch, values[:, 0:8], src, LOWEST))
                link(nc.vector.max(values[:, 8:16], scratch))
                return nc.vector.max_index(numbers[:, 8:16], values[:, 8:16], scratch)

            for t in range(NT):
                dve.wait_ge(s_scores, t + 1)
                for h in range(PH):
                    for half in range(2):
                        ins = top16(best[:, h, half, :], at[:, h, half, :], scores(16 * t + 2 * h + half), rest[:])
                ins.then_inc(s_taken, 1)
                dve.wait_ge(s_taken, t + 1)
                link(nc.vector.tensor_copy(at_f[:], at[:]))
                for h in range(PH):
                    link(nc.vector.tensor_tensor(cand[:], best[:, h, 0, :].unsqueeze(2).to_broadcast([P, TOPK, TOPK]),
                                                 best[:, h, 1, :].unsqueeze(1).to_broadcast([P, TOPK, TOPK]), ALU.add))
                    ins = top16(top[:, h, :], pick[:, h, :], cand[:].rearrange("p a b -> p (a b)"), cand_rest[:])
                link(ins)
                nc.vector.tensor_tensor(over[:], top[:], top[:, :, 0:1].to_broadcast([P, PH, TOPK]),
                                        ALU.subtract).then_inc(s_over, 1)
                nc.vector.tensor_scalar(part[:, 0], pick[:], 4, None, ALU.logical_shift_right)
                link(nc.vector.tensor_scalar(part[:, 1], pick[:], TOPK - 1, None, ALU.bitwise_and))
                link(nc.vector.tensor_copy(part_f[:], part[:]))
                for half in range(2):
                    shape = [P, PH, TOPK, TOPK]
                    link(nc.vector.tensor_tensor(equal[:], part_f[:, half].unsqueeze(3).to_broadcast(shape),
                                                 iota.unsqueeze(1).unsqueeze(1).to_broadcast(shape), ALU.is_equal))
                    link(nc.vector.tensor_tensor(equal[:], equal[:], at_f[:, :, half, :].unsqueeze(2).to_broadcast(shape),
                                                 ALU.mult))
                    link(nc.vector.tensor_reduce(number[:, half], equal[:], AX_X, ALU.add))
                link(nc.vector.scalar_tensor_tensor(out=expert[:, t, :], in0=number[:, 0].rearrange("p h k -> p (h k)"),
                                                    scalar=float(PK), in1=number[:, 1].rearrange("p h k -> p (h k)"),
                                                    op0=ALU.mult, op1=ALU.add))
                dve.wait_ge(s_exp, t + 1)
                link(nc.vector.tensor_reduce(total[:], weight[:], AX_X, ALU.add))
                link(nc.vector.reciprocal(inverse[:], total[:]))
                link(nc.vector.tensor_tensor(gates[:, t, :].rearrange("p (h k) -> p h k", h=PH), weight[:],
                                             inverse[:].unsqueeze(2).to_broadcast([P, PH, TOPK]), ALU.mult))


def peer_expert_stage(g, xn, expert, gates, peer_u, peer_v, last_slab):
    nc = g.nc
    with ExitStack() as ctx:
        sb = lambda name, shape, dt=F32: ctx.enter_context(nc.sbuf_tensor(f"peer_{name}", shape, dt))
        sem = lambda name: g.semaphore(f"peer_{name}")
        rows = sb("rows", [P, GATHERS, D])
        junk = sb("junk", [P, D])
        round_dots = sb("round_dots", [P, GATHERS])
        dots, active, weight = sb("dots", [P, PICKS]), sb("active", [P, PICKS]), sb("weight", [P, PICKS])
        landed = [sem(f"landed{r}") for r in range(GATHERS)]
        s_used, s_active, s_weight, s_kept = (sem(x) for x in ("used", "active_ready", "weight_ready", "kept"))
        block = ctx.enter_context(nc.Block())
        rounds = PICKS // GATHERS

        @block.sync
        def _(sp):
            g.w.load_through(sp, last_slab)

        @block.gpsimd
        def _(pool):
            n = 0
            for t in range(NT):
                for table in (peer_u, peer_v):
                    for k in range(PICKS):
                        if n >= GATHERS:
                            pool.wait_ge(s_used, n - GATHERS + 1)
                        pool.indirect_dma_start(
                            out=rows[:, n % GATHERS, :], out_offset=None, in_=table,
                            in_offset=bass.IndirectOffsetOnAxis(ap=expert[:, t, k:k + 1], axis=0),
                        ).then_inc(landed[n % GATHERS], 16)
                        n += 1

        @block.scalar
        def _(act):
            for t in range(NT):
                act.wait_ge(s_kept, rounds * (t + 1))
                nc.scalar.activation(active[:], dots[:], ACT.Gelu).then_inc(s_active, 1)

        @block.vector
        def _(dve):
            for t in range(NT):
                with dve.Fori(0, rounds) as i:
                    for r in range(GATHERS):
                        n = i * GATHERS + r
                        dve.wait_ge(landed[r], (i + rounds * 2 * t + 1) * 16)
                        if r:
                            dve.wait_ge(s_used, n + PICKS * 2 * t)
                        nc.vector.tensor_tensor_reduce(out=junk[:], in0=rows[:, r, :], in1=xn[:, t, :], scale=1.0, scalar=0.0,
                                                       op0=ALU.mult, op1=ALU.add,
                                                       accum_out=round_dots[:, r:r + 1]).then_inc(s_used, 1)
                    dve.wait_ge(s_used, (i + 1) * GATHERS + PICKS * 2 * t)
                    nc.vector.tensor_copy(dots[:, bass.ds(i * GATHERS, GATHERS)], round_dots[:]).then_inc(s_kept, 1)
                    dve.wait_ge(s_kept, i + 1 + rounds * t)
                dve.wait_ge(s_active, t + 1)
                nc.vector.tensor_tensor(weight[:], active[:], gates[:, t, :], ALU.mult).then_inc(s_weight, 1)
                dve.wait_ge(s_weight, t + 1)
                with dve.Fori(0, rounds) as i:
                    for r in range(GATHERS):
                        n = i * GATHERS + r
                        dve.wait_ge(landed[r], (i + rounds * (2 * t + 1) + 1) * 16)
                        dve.wait_ge(s_used, n + PICKS * (2 * t + 1))
                        nc.vector.scalar_tensor_tensor(out=g.h[:, t, :], in0=rows[:, r, :], scalar=weight[:, bass.ds(n, 1)],
                                                       in1=g.h[:, t, :], op0=ALU.mult, op1=ALU.add).then_inc(s_used, 1)


def compress_input_stage(g, h2T, pe_table, kc, last_slab):
    nc = g.nc
    products = [feature_major(g, "kcvc", j, h2T, slice(0, S)) for j in range(4)]
    n = NCMP * CMP_STRIDE
    with ExitStack() as ctx:
        drained = {"dve": g.semaphore("kc_drained")}
        block = ctx.enter_context(nc.Block())

        @block.sync
        def _(sp):
            g.w.load_through(sp, last_slab)

        @block.tensor
        def _(pe):
            multiply(g, pe, products, ["dve"] * 4, drained)

        @block.vector
        def _(dve):
            for j in range(4):
                dve.wait_ge(g.w.products_done, g.w.product("kcvc", j))
                for half in range(2):
                    rows, c0 = slice(HD * half, HD * half + HD), CMP_STRIDE * half
                    ins = nc.vector.tensor_tensor(
                        kc[rows, j // 2, j % 2, 0:n].rearrange("p (n l) -> p n l", l=CMP_STRIDE),
                        g.psum[rows, j, c0:c0 + n].rearrange("p (n l) -> p n l", l=CMP_STRIDE),
                        pe_table[rows, j // 2, :].unsqueeze(1).to_broadcast([HD, NCMP, CMP_STRIDE]), ALU.add)
                ins.then_inc(drained["dve"], 1)


def compress_stage(g, kc, w2, rope_cmp, k_cmpT, v_cmp, last_slab):
    nc = g.nc
    with ExitStack() as ctx:
        sb = lambda name, shape: ctx.enter_context(nc.sbuf_tensor(f"cmp_{name}", shape, F32))
        sem = lambda name: g.semaphore(f"cmp_{name}")
        hidden = sb("hidden", [P, 2, 2, NG * NCMP])
        k_tok, k_roped = sb("k_tok", [NCMP, NG * HD]), sb("k_roped", [NCMP, NG * HD])
        tmp = [sb(f"tmp{i}", [NCMP, NG * HD]) for i in range(2)]
        s_hidden, s_out, s_copied, s_link, s_roped, s_turned = (
            sem(x) for x in ("hidden_ready", "out_ready", "copied", "link", "roped", "turned"))
        block = ctx.enter_context(nc.Block())

        @block.sync
        def _(sp):
            g.w.load_through(sp, last_slab)

        @block.tensor
        def _(pe):
            for x, name in enumerate(("ck1", "cv1")):
                g.w.arrived(pe, name)
                w1 = g.w.view(name)
                for j in range(2):
                    for l in range(CMP_STRIDE):
                        rhs = kc[:, x, :, :].rearrange("p g (n l) -> p g n l", l=CMP_STRIDE)[:, :, 0:NCMP, l]
                        mm = nc.tensor.matmul(g.psum[:, 2 * x + j, 0:NG * NCMP].rearrange("p (g n) -> p g n", g=NG),
                                              w1[:, l, P * j:P * j + P], rhs, start=(l == 0), stop=(l == CMP_STRIDE - 1))
                    mm.then_inc(g.w.products_done, 1)
            for x in range(2):
                pe.wait_ge(s_hidden, 2 * x + 2)
                for grp in range(NG):
                    for j in range(2):
                        mm = nc.tensor.matmul(g.psum[0:NCMP, 4 + x, HD * grp:HD * grp + HD],
                                              hidden[:, x, j, NCMP * grp:NCMP * grp + NCMP], w2[:, x, j, :],
                                              start=(j == 0), stop=(j == 1))
                mm.then_inc(s_out, 1)
            pe.wait_ge(s_roped, 1)
            for grp in range(NG):
                mm = nc.tensor.transpose(g.psum[0:HD, 6, P * grp:P * grp + NCMP], k_roped[:, HD * grp:HD * grp + HD],
                                         g.identity[0:NCMP, 0:NCMP])
            mm.then_inc(s_turned, 1)

        @block.scalar
        def _(act):
            for x, name in enumerate(("ck1", "cv1")):
                for j in range(2):
                    act.wait_ge(g.w.products_done, g.w.product(name, j))
                    nc.scalar.activation(hidden[:, x, j, :], g.psum[:, 2 * x + j, 0:NG * NCMP],
                                         ACT.Gelu_apprx_tanh).then_inc(s_hidden, 1)

        @block.vector
        def _(dve):
            link = linker(dve, s_link)
            dve.wait_ge(s_out, 1)
            link(nc.vector.tensor_copy(k_tok[:], g.psum[0:NCMP, 4, 0:NG * HD]))
            view = lambda x: x[:].rearrange("p (h a b) -> p h a b", h=NG, a=2)
            rope(nc, link, view(k_roped), view(k_tok), rope_cmp, [view(x) for x in tmp])
            nc.vector.memset(k_tok[:, 0:1], 0.0).then_inc(s_roped, 1)
            dve.wait_ge(s_out, 2)
            nc.vector.tensor_copy(v_cmp, g.psum[0:NCMP, 5, 0:NG * HD])
            dve.wait_ge(s_turned, 1)
            link(nc.vector.tensor_copy(k_cmpT, g.psum[0:HD, 6, :].rearrange("p (g n) -> p g n", g=4)[:, 0:NG, 0:NCMP]))


def pool_stage(g, uT, inv_count, w_pool, pool_scale, ypT):
    nc = g.nc
    n = len(WINDOWS)
    with ExitStack() as ctx:
        sb = lambda name, shape: ctx.enter_context(nc.sbuf_tensor(f"pool_{name}", shape, F32))
        sem = lambda name: g.semaphore(f"pool_{name}")
        sums = [sb(f"sums{i}", [P, n, PAD + S]) for i in range(2)]
        s_link, s_diff, s_y = sem("link"), sem("diff"), sem("y")
        block = ctx.enter_context(nc.Block())

        @block.vector
        def _(dve):
            link = linker(dve, s_link)
            for x in (uT, sums[0], sums[1]):
                ins = nc.vector.memset(x[:, :, 0:PAD], 0.0)
            link(ins)
            src = uT
            for j in range(n):
                dst = sums[j % 2]
                step = 2 ** j
                link(nc.vector.tensor_tensor(dst[:, j:n, PAD:], src[:, j:n, PAD:], src[:, j:n, PAD - step:PAD + S - step],
                                             ALU.add))
                link(nc.vector.tensor_tensor(dst[:, j, PAD:], dst[:, j, PAD:], inv_count[:, j, :], ALU.mult)
                     if j == n - 1 else nc.vector.tensor_tensor(ypT[:, j, :], dst[:, j, PAD:], inv_count[:, j, :], ALU.mult))
                mean = dst[:, j, PAD:] if j == n - 1 else ypT[:, j, :]
                link(nc.vector.tensor_tensor(ypT[:, j, :], mean, uT[:, j, PAD:], ALU.subtract))
                src = dst
            nc.vector.memset(sums[0][:, 0, 0:1], 0.0).then_inc(s_diff, 1)

        @block.tensor
        def _(pe):
            pe.wait_ge(s_diff, 1)
            for j in range(n):
                nc.tensor.matmul(g.psum[:, j, :], w_pool[:, j, :], ypT[:, j, :], start=True, stop=True).then_inc(s_y, 1)

        @block.scalar
        def _(act):
            for j in range(n):
                act.wait_ge(s_y, j + 1)
                nc.scalar.activation(ypT[:, j, :], g.psum[:, j, :], ACT.Copy, scale=pool_scale[:, j:j + 1])


def mlp_up_stage(g, h2T, aT, last_slab):
    nc = g.nc
    n_slabs = D_FF // 512
    products = [feature_major(g, ("ff1", b), j, h2T, slice(0, S)) for b in range(n_slabs) for j in range(4)]
    with ExitStack() as ctx:
        drained = {"act": g.semaphore("ff1_drained")}
        positive = ctx.enter_context(nc.sbuf_tensor("ff1_positive", [P, 4, S], F32))
        s_squared = g.semaphore("ff1_squared")
        block = ctx.enter_context(nc.Block())

        @block.sync
        def _(sp):
            g.w.load_through(sp, last_slab)

        @block.tensor
        def _(pe):
            multiply(g, pe, products, ["act"] * len(products), drained)

        @block.scalar
        def _(act):
            for n, (name, j, _, _, _) in enumerate(products):
                act.wait_ge(g.w.products_done, g.w.product(name, j))
                if n >= 4:
                    act.wait_ge(s_squared, n - 3)
                nc.scalar.activation(positive[:, n % 4, :], g.psum[:, n % BANKS, :], ACT.Relu).then_inc(drained["act"], 1)

        @block.vector
        def _(dve):
            for n in range(len(products)):
                dve.wait_ge(drained["act"], n + 1)
                x = positive[:, n % 4, :]
                nc.vector.tensor_tensor(aT[:, n, :], x, x, ALU.mult).then_inc(s_squared, 1)


def mlp_down_stage(g, aT, last_slab):
    nc = g.nc
    groups = D_FF // P // KT
    with ExitStack() as ctx:
        s_added = g.semaphore("ff2_added")
        block = ctx.enter_context(nc.Block())

        @block.sync
        def _(sp):
            g.w.load_through(sp, last_slab)

        @block.tensor
        def _(pe):
            for b in range(2):
                for k in range(groups):
                    name = ("ff2", b, k)
                    g.w.arrived(pe, name)
                    w = g.w.view(name)
                    for t in range(NT):
                        for i in range(KT):
                            mm = nc.tensor.matmul(g.psum[:, 4 * b + t, :], aT[:, KT * k + i, P * t:P * t + P], w[:, i, :],
                                                  start=(k == 0 and i == 0), stop=(k == groups - 1 and i == KT - 1))
                        mm.then_inc(g.w.products_done, 1)

        @block.vector
        def _(dve):
            for b in range(2):
                for t in range(NT):
                    h = g.h[:, t, 512 * b:512 * b + 512]
                    dve.wait_ge(g.w.products_done, g.w.product(("ff2", b, groups - 1), t))
                    nc.vector.tensor_tensor(h, h, g.psum[:, 4 * b + t, :], ALU.add).then_inc(s_added, 1)


def load_stage(g, tag, pairs):
    with ExitStack() as ctx:
        s = g.semaphore(f"{tag}_loaded")
        block = ctx.enter_context(g.nc.Block())

        @block.sync
        def _(sp):
            for dst, src in pairs:
                sp.dma_start(dst, src).then_inc(s, 16)
            sp.wait_ge(s, 16 * len(pairs))


def build(nc, a):
    with ExitStack() as whole:
        g = Core(nc)
        alloc = lambda ctx, name, shape, dt=F32: ctx.enter_context(nc.sbuf_tensor(name, shape, dt))
        stage_semaphores = []

        def semaphore(name):
            stage_semaphores.append(nc.alloc_semaphore(name=name))
            return stage_semaphores[-1]

        def clear_semaphores():
            nc.clear_and_free_semaphores(stage_semaphores)
            nc.all_engine_barrier()
            stage_semaphores.clear()

        g.semaphore = semaphore
        g.psum = whole.enter_context(nc.psum_tensor("psum", [P, BANKS, 512], F32))
        g.w = Weights(nc, whole, weight_plan(a))
        g.h = alloc(whole, "h", [P, NT, D])
        g.identity = alloc(whole, "identity_sb", [P, P])
        gains = alloc(whole, "gains", [P, 96])
        names = [("g_mix", 8), ("g_q_lora", 3), ("g_kv_lora", 2), ("g_ret_gn", 8), ("norm_mix", 8), ("norm_mlp", 8),
                 ("pool_scale", 4)]
        g.gain, at, gain_loads = {}, 0, []
        for name, n in names:
            g.gain[name] = gains[:, at:at + n]
            gain_loads.append((g.gain[name], a[name]))
            at += n
        x_tiles = a["x"].rearrange("(t p) d -> p t d", p=P)

        with ExitStack() as first:
            hnT = alloc(first, "hnT", [P, KT, L])
            o_tok = alloc(first, "mla_o", [P, NT, MH * MV])
            with ExitStack() as s:
                meta = alloc(s, "meta", [META, D])
                loads = [(meta[:], a["meta_tokens"]), (g.h[:], x_tiles), (g.identity[:], a["identity"])] + gain_loads
                sources = [(meta[:], META, row_tile(0)[1])] + [(g.h[:, t, :], P, row_tile(t + 1)[1]) for t in range(NT)]
                norm_stage(g, "n1", sources, D, outT=hnT, gain_columns=g.gain["g_mix"], loads=loads)

            with ExitStack() as mla:
                qT, kT = alloc(mla, "qT", [QK, MH, S]), alloc(mla, "kT", [QK, MH, L])
                kv = alloc(mla, "kv", [P, NT + 1, MH * (NOPE + MV)])
                with ExitStack() as s:
                    ckv = alloc(s, "ckv", [P, NT + 1, KV_LORA + MROPE])
                    q = alloc(s, "q", [P, NT, MH * QK])
                    with ExitStack() as lat:
                        cq = alloc(lat, "cq", [P, NT, Q_LORA])
                        cqT, ckvT = alloc(lat, "cqT", [P, 3, S]), alloc(lat, "ckvT", [P, 2, L])
                        products = [token_major(g, "cq", t, hnT, row_tile(t + 1)[1], P) for t in range(NT)]
                        outputs = [cq[:, t, :] for t in range(NT)]
                        for t in range(NT + 1):
                            rows, columns = row_tile(t)
                            products.append(token_major(g, "ckv", t, hnT, columns, rows))
                            outputs.append(ckv[0:rows, t, :])
                        product_stage(g, "lat", products, outputs, "ckv")
                        norm_stage(g, "nq", [(cq[:, t, :], P, slice(P * t, P * t + P)) for t in range(NT)], Q_LORA,
                                   outT=cqT, gain_columns=g.gain["g_q_lora"])
                        norm_stage(g, "nkv", [(ckv[0:row_tile(t)[0], t, 0:KV_LORA],) + row_tile(t) for t in range(NT + 1)],
                                   KV_LORA, outT=ckvT, gain_columns=g.gain["g_kv_lora"])
                        products, outputs = [], []
                        for b in range(2):
                            for t in range(NT):
                                products.append(token_major(g, ("uq", b), t, cqT, slice(P * t, P * t + P), P))
                                outputs.append(q[:, t, 384 * b:384 * b + 384])
                        for b in range(2):
                            for t in range(NT + 1):
                                rows, columns = row_tile(t)
                                products.append(token_major(g, ("ukv", b), t, ckvT, columns, rows))
                                outputs.append(kv[0:rows, t, 512 * b:512 * b + 512])
                        product_stage(g, "up", products, outputs, ("ukv", 1))
                    with ExitStack() as heads:
                        k_heads = alloc(heads, "k_heads", [P, NT + 1, MH * QK])
                        q_gain, k_gain = alloc(heads, "q_gain", [P, QK]), alloc(heads, "k_gain", [P, QK])
                        table = alloc(heads, "rope_mla_sb", [P, NT + 1, 2, MROPE // 2])
                        load_stage(g, "mla", [(q_gain[:], a["g_qk_q"].partition_broadcast(P)),
                                              (k_gain[:], a["g_qk_k"].partition_broadcast(P)), (table[:], a["rope_mla"])])
                        mla_qk_stage(g, q, kv, ckv[:, :, KV_LORA:], q_gain, k_gain, table, k_heads)
                        sources = []
                        for t in range(NT):
                            for h0 in (0, 4):
                                sources.append(([q[:, t, QK * h:QK * h + QK] for h in range(h0, h0 + 4)], P,
                                                qT[:, h0:h0 + 4, P * t:P * t + P]))
                        turn_stage(g, "tq", sources, QK, scale=QK ** -0.5)
                        sources = []
                        for t in range(NT + 1):
                            rows, columns = row_tile(t)
                            for h0 in (0, 4):
                                sources.append(([k_heads[0:rows, t, QK * h:QK * h + QK] for h in range(h0, h0 + 4)], rows,
                                                kT[:, h0:h0 + 4, columns]))
                        turn_stage(g, "tk", sources, QK)
                with ExitStack() as s:
                    causal = alloc(s, "causal_sb", [P, P])
                    load_stage(g, "causal", [(causal[:], a["causal"])])
                    items = []
                    for t in range(NT):
                        for h in range(MH):
                            lo = 512 - P * (t + 1)
                            v = kv[:, :, 128 * h + NOPE:128 * h + 128]
                            items.append(Item(
                                q=qT[:, h, P * t:P * t + P], columns=(lo, 512 + META),
                                keys=[(kT[:, h, META:META + P * (t + 1)], lo), (kT[:, h, 0:META], 512)],
                                biases=[(causal[:], 512 - P)], seen=None, gate=None, add=False,
                                blocks=[(lo + P * m, P, v[:, m + 1, :]) for m in range(t + 1)] + [(512, META, v[0:META, 0, :])],
                                out=o_tok[:, t, MV * h:MV * h + MV]))
                    attention_stage(g, "ma", items, MV)

            clear_semaphores()
            ynT = alloc(first, "ynT", [P, RH, S])
            with ExitStack() as ret:
                rqT, rkT = alloc(ret, "rqT", [P, RH // 2, S]), alloc(ret, "rkT", [P, RH // 2, L])
                rv = alloc(ret, "rv", [P, NT + 1, RH * RDV])
                with ExitStack() as s:
                    rq, rk = alloc(s, "rq", [P, NT, RH * RDK]), alloc(s, "rk", [P, NT + 1, RH * RDK])
                    table = alloc(s, "rope_ret_sb", [P, NT + 1, 2, RDK // 2])
                    products = [token_major(g, "rq", t, hnT, row_tile(t + 1)[1], P) for t in range(NT)]
                    outputs = [rq[:, t, :] for t in range(NT)]
                    for name, dst, c0 in (("rk", rk, 0), (("rv", 0), rv, 0), (("rv", 1), rv, 512)):
                        for t in range(NT + 1):
                            rows, columns = row_tile(t)
                            products.append(token_major(g, name, t, hnT, columns, rows))
                            outputs.append(dst[0:rows, t, c0:c0 + 512])
                    product_stage(g, "rp", products, outputs, ("rv", 1))
                    load_stage(g, "ropret", [(table[:], a["rope_ret"])])
                    jobs = []
                    for x, t, i in [(rq, t, t + 1) for t in range(NT)] + [(rk, t, t) for t in range(NT + 1)]:
                        rows, _ = row_tile(i)
                        view = x[0:rows, t, :].rearrange("p (h a b) -> p h a b", h=RH, a=2)
                        jobs.append((view, view, table[0:rows, i, :, :]))
                    rope_stage(g, "rr", jobs, RH * RDK)
                    sources = [([rq[:, t, P * c:P * c + P] for c in range(4)], P, rqT[:, :, P * t:P * t + P])
                               for t in range(NT)]
                    for t in range(NT + 1):
                        rows, columns = row_tile(t)
                        sources.append(([rk[0:rows, t, P * c:P * c + P] for c in range(4)], rows, rkT[:, :, columns]))
                    turn_stage(g, "tr", sources, P)
                y = alloc(ret, "ret_y", [P, RH, NT * RDV])
                with ExitStack() as s:
                    decay = alloc(s, "decay_sb", [P, RH, L])
                    load_stage(g, "decay", [(decay[:], a["decay"])])
                    retention_stage(g, rqT, rkT, rv, decay, y, ("rv", 1))
                group_norm_stage(g, y, g.gain["g_ret_gn"], ynT)
            retention_gate_stage(g, hnT, ynT, ("rg", 1))

            with ExitStack() as s:
                oT, mergedT = alloc(s, "oT", [P, 4, S]), alloc(s, "mergedT", [P, KT, S])
                turn_stage(g, "to", [([o_tok[:, t, P * c:P * c + P] for c in range(4)], P, oT[:, :, P * t:P * t + P])
                                     for t in range(NT)], P)
                merge_stage(g, "m1", ("za", "ya", "zr", "yr"), hnT, slice(META, L), (oT, ynT), mergedT, ("yr", 1))
                residual_stage(g, "mix", [("mix", 0), ("mix", 1)], mergedT, ("mix", 1))

        clear_semaphores()
        with ExitStack() as peer:
            xn = alloc(peer, "xn", [P, NT, D])
            expert, gates = alloc(peer, "expert", [P, NT, PICKS], U32), alloc(peer, "gates_sb", [P, NT, PICKS])
            with ExitStack() as s:
                g_ffn = alloc(s, "g_ffn_sb", [P, D])
                keysT, iota = alloc(s, "keysT_sb", [P, PK]), alloc(s, "iota_sb", [P, TOPK])
                xnT, pqT = alloc(s, "xnT", [P, KT, S]), alloc(s, "pqT", [P, PH, S])
                load_stage(g, "peer", [(g_ffn[:], a["g_ffn"].partition_broadcast(P)), (keysT[:], a["keysT"]), (iota[:], a["iota"])])
                norm_stage(g, "np", [(g.h[:, t, :], P, slice(P * t, P * t + P)) for t in range(NT)], D, outT=xnT,
                           token_out=xn, gain_rows=g_ffn[:])
                products = [feature_major(g, ("pq", b), j, xnT, slice(0, S)) for b in range(2) for j in range(4)]
                product_stage(g, "pq", products, [pqT[:, h, :] for h in range(PH)], ("pq", 1))
                peer_select_stage(g, pqT, keysT, iota[:], expert, gates)
            peer_expert_stage(g, xn, expert, gates, a["peer_u"], a["peer_v"], ("pq", 1))

        with ExitStack() as second:
            h2T = alloc(second, "h2T", [P, KT, S])
            ypT = alloc(second, "ypT", [P, 4, S])
            norm_stage(g, "n2", [(g.h[:, t, :], P, slice(P * t, P * t + P)) for t in range(NT)], D, outT=h2T,
                       gain_columns=g.gain["norm_mix"])
            with ExitStack() as s:
                uT = alloc(s, "uT", [P, 4, PAD + S])
                inv_count, w_pool = alloc(s, "inv_count_sb", [P, 4, S]), alloc(s, "w_pool_sb", [P, 4, P])
                load_stage(g, "pool", [(inv_count[:], a["inv_count"]), (w_pool[:], a["w_pool"].rearrange("g c d -> c g d"))])
                product_stage(g, "u", [feature_major(g, "u", j, h2T, slice(0, S)) for j in range(4)],
                              [uT[:, j, PAD:] for j in range(4)], "u")
                pool_stage(g, uT, inv_count, w_pool, g.gain["pool_scale"], ypT)

            clear_semaphores()
            o = alloc(second, "nsa_o", [P, NT, NH * HD])
            with ExitStack() as nsa:
                qT, kT = alloc(nsa, "nsa_qT", [HD, NH, S]), alloc(nsa, "nsa_kT", [HD, 4, S])
                kv = alloc(nsa, "nsa_kv", [P, NT, 512])
                branch_gates = alloc(nsa, "branch_gates", [P, NT, 3 * NH])
                k_cmpT, v_cmp = alloc(nsa, "k_cmpT", [HD, NG, NCMP]), alloc(nsa, "v_cmp", [NCMP, NG * HD])
                with ExitStack() as s:
                    q = alloc(s, "nsa_q", [P, NT, NH * HD])
                    kc = alloc(s, "kc", [P, 2, NG, S])
                    pe_table = alloc(s, "pe_sb", [P, 2, CMP_STRIDE])
                    w2 = alloc(s, "w2_sb", [P, 2, 2, HD])
                    table = alloc(s, "rope_nsa_sb", [P, NT, 2, HD // 2])
                    table_cmp = alloc(s, "rope_cmp_sb", [NCMP, 2, HD // 2])
                    load_stage(g, "nsa", [(pe_table[:], a["pe_table"]), (w2[:, 0], a["w_ck2"].rearrange("(j p) d -> p j d", p=P)),
                                          (w2[:, 1], a["w_cv2"].rearrange("(j p) d -> p j d", p=P)), (table[:], a["rope_nsa"]),
                                          (table_cmp[:], a["rope_cmp"])])
                    products, outputs = [], []
                    for b in range(2):
                        for t in range(NT):
                            products.append(token_major(g, ("q", b), t, h2T, slice(P * t, P * t + P), P))
                            outputs.append(q[:, t, 512 * b:512 * b + 512])
                    product_stage(g, "nq2", products, outputs, ("q", 1))
                    compress_input_stage(g, h2T, pe_table, kc, "kcvc")
                    products, outputs = [], []
                    for t in range(NT):
                        products.append(token_major(g, "kv", t, h2T, slice(P * t, P * t + P), P))
                        outputs.append(kv[:, t, :])
                    for t in range(NT):
                        products.append(token_major(g, "gn", t, h2T, slice(P * t, P * t + P), P))
                        outputs.append(branch_gates[:, t, :])
                    product_stage(g, "nkv2", products, outputs, "gn", functions=[None] * NT + [ACT.Sigmoid] * NT)
                    compress_stage(g, kc, w2, table_cmp, k_cmpT[:], v_cmp[:], "cv1")
                    jobs = []
                    for t in range(NT):
                        view = q[:, t, :].rearrange("p (h a b) -> p h a b", h=NH, a=2)
                        jobs.append((view, view, table[:, t, :, :]))
                        for c0 in (0, 2 * KVW):
                            view = kv[:, t, c0:c0 + KVW].rearrange("p (h a b) -> p h a b", h=NG, a=2)
                            jobs.append((view, view, table[:, t, :, :]))
                    rope_stage(g, "nr", jobs, NH * HD)
                    sources = []
                    for t in range(NT):
                        for h0 in range(0, NH, 4):
                            sources.append(([q[:, t, HD * h:HD * h + HD] for h in range(h0, h0 + 4)], P,
                                            qT[:, h0:h0 + 4, P * t:P * t + P]))
                    turn_stage(g, "tq2", sources, HD, scale=HD ** -0.5)
                    turn_stage(g, "tk2", [([kv[:, t, c:c + HD] for c in (0, HD, 2 * KVW, 2 * KVW + HD)], P,
                                           kT[:, :, P * t:P * t + P]) for t in range(NT)], HD)
                with ExitStack() as s:
                    causal = alloc(s, "causal2_sb", [P, P])
                    bias, seen = alloc(s, "cmp_bias_sb", [P, NT, NCMP]), alloc(s, "cmp_seen_sb", [P, NT, NCMP])
                    load_stage(g, "masks", [(causal[:], a["causal"]), (bias[:], a["cmp_bias"]), (seen[:], a["cmp_seen"])])
                    assert S // SEL_BLOCK <= N_SEL and WINDOW >= S
                    items = []
                    for t in range(NT):
                        for h in range(NH):
                            grp = h // HPG
                            common = dict(q=qT[:, h, P * t:P * t + P], out=o[:, t, HD * h:HD * h + HD])
                            gate = lambda x: branch_gates[:, t, 3 * h + x:3 * h + x + 1]
                            items.append(Item(
                                keys=[(k_cmpT[:, grp, :], 0)], columns=(0, NCMP), biases=[(bias[:, t, :], 0)],
                                blocks=[(0, NCMP, v_cmp[:, HD * grp:HD * grp + HD])], seen=seen[:, t, :], gate=gate(0),
                                add=False, **common))
                            for x in range(2):
                                n = P * (t + 1)
                                v0 = 2 * KVW * x + KVW + HD * grp
                                items.append(Item(
                                    keys=[(kT[:, 2 * x + grp, 0:n], 0)], columns=(0, n), biases=[(causal[:], n - P)],
                                    blocks=[(P * m, P, kv[:, m, v0:v0 + HD]) for m in range(t + 1)], seen=None,
                                    gate=gate(1 + x), add=True, **common))
                    attention_stage(g, "na", items, HD)
            oT = alloc(second, "nsa_oT", [P, KT, S])
            turn_stage(g, "to2", [([o[:, t, P * c:P * c + P] for c in range(c0, c0 + 4)], P,
                                   oT[:, c0:c0 + 4, P * t:P * t + P]) for t in range(NT) for c0 in (0, 4)], P)
            mergedT = alloc(second, "mergedT2", [P, KT, S])
            merge_stage(g, "m2", ("ga", "yp", "gb", "yn"), h2T, slice(0, S), (ypT, oT), mergedT, ("yn", 1))
            residual_stage(g, "out", [("out", 0), ("out", 1)], mergedT, ("out", 1))

        clear_semaphores()
        with ExitStack() as mlp:
            aT = alloc(mlp, "aT", [P, D_FF // P, S])
            with ExitStack() as s:
                h3T = alloc(s, "h3T", [P, KT, S])
                norm_stage(g, "n3", [(g.h[:, t, :], P, slice(P * t, P * t + P)) for t in range(NT)], D, outT=h3T,
                           gain_columns=g.gain["norm_mlp"])
                mlp_up_stage(g, h3T, aT, ("ff1", D_FF // 512 - 1))
            mlp_down_stage(g, aT, ("ff2", 1, 3))
        with ExitStack() as s:
            final, g_final = alloc(s, "final", [P, NT, D]), alloc(s, "g_final", [P, D])
            load_stage(g, "final", [(g_final[:], a["norm_final"].partition_broadcast(P))])
            norm_stage(g, "nf", [(g.h[:, t, :], P, None) for t in range(NT)], D, token_out=final, gain_rows=g_final[:],
                       store=a["out"].rearrange("(t p) d -> p t d", p=P))


def arrays(inputs):
    def columns(v):
        return v.reshape(-1, P).T

    one = {k: np.asarray(v)[0] for k, v in inputs.items() if k not in ("meta_tokens", "norm_final_2")}
    w2 = one["w_in_2"]
    kc_vc = w2[:, E_KC:E_KS].reshape(D, 2 * NG, 1, HD)
    first_w = lambda w: w.reshape(2, CMP_STRIDE, HD, CMP_HID).transpose(0, 2, 1, 3).reshape(P, CMP_STRIDE, CMP_HID)
    pe = lambda x: x.reshape(2, CMP_STRIDE, HD).transpose(0, 2, 1).reshape(P, CMP_STRIDE)
    out = {
        "x": one["x"], "meta_tokens": np.asarray(inputs["meta_tokens"]),
        "g_mix": columns(one["g_mix"]), "g_q_lora": columns(one["g_q_lora"]), "g_kv_lora": columns(one["g_kv_lora"]),
        "g_ret_gn": columns(one["g_ret_gn"]), "norm_mix": columns(one["norm_mix_2"]),
        "norm_mlp": columns(one["norm_mlp_2"]), "pool_scale": columns(one["pool_scale_2"]),
        "g_qk_q": one["g_qk_q"], "g_qk_k": one["g_qk_k"], "g_ffn": one["g_ffn"], "norm_final": np.asarray(inputs["norm_final_2"]),
        "w_in": one["w_in"], "w_uq": one["w_uq"], "w_ukv": one["w_ukv"], "w_mla_out": one["w_mla_out"],
        "w_ret_out": one["w_ret_out"], "w_mix_out": one["w_mix_out"], "w_peer_q": one["w_peer_q"],
        "keysT": np.concatenate([one["peer_keys_1"].T, one["peer_keys_2"].T]),
        "peer_u": one["peer_u"], "peer_v": one["peer_v"],
        "w_in2": w2, "w_kcvc": np.broadcast_to(kc_vc, (D, 2 * NG, 2, HD)).reshape(D, 4 * P),
        "w_ck1": first_w(one["w_ck1_2"]), "w_cv1": first_w(one["w_cv1_2"]), "w_ck2": one["w_ck2_2"], "w_cv2": one["w_cv2_2"],
        "pe_table": np.stack([pe(one["pe_k_2"]), pe(one["pe_v_2"])], 1),
        "w_pool": one["w_pool_2"], "w_proj_pool": one["w_proj_pool_2"], "w_proj_nsa": one["w_proj_nsa_2"],
        "w_out": one["w_out_2"], "w_ff1": one["w_ff1_2"], "w_ff2": one["w_ff2_2"],
    }
    return {k: np.ascontiguousarray(v) for k, v in out.items()} | constants()


def kernel(**inputs):
    import concourse.bacc as bacc
    from concourse.bass_utils import run_bass_kernel_spmd

    nc = bacc.Bacc("TRN2", target_bir_lowering=False, num_devices=1)
    data = arrays(inputs)
    views = {k: nc.dram_tensor(f"{k}_dram", v.shape, mybir.dt.from_np(v.dtype), kind="ExternalInput").ap()
             for k, v in data.items()}
    views["out"] = nc.dram_tensor("out_dram", (S, D), F32, kind="ExternalOutput").ap()
    build(nc, views)
    r = run_bass_kernel_spmd(nc, [{f"{k}_dram": v for k, v in data.items()}], core_ids=[0])
    return r.results[0]["out_dram"].reshape(1, S, D)
```

```python
from contextlib import ExitStack

import numpy as np

import concourse.bass as bass
from concourse import mybir

F32 = mybir.dt.float32
U32 = mybir.dt.uint32
ALU = mybir.AluOpType
ACT = mybir.ActivationFunctionType
AX_X = mybir.AxisListType.X

P = 128
D = 1024
S = 512
NT = S // P
META = 16
L = META + S
KT = D // P
EPS = 1e-6
NEG = -1e30
LOWEST = -3.0e38

Q_LORA, KV_LORA, MH, NOPE, MROPE, MV = 384, 256, 8, 64, 32, 64
QK = NOPE + MROPE
RH, RDK, RDV = 8, 64, 128
PH, PK, TOPK = 8, 128, 16
PICKS = PH * TOPK
C_Q, C_KV, C_RQ, C_RK = 0, Q_LORA, Q_LORA + KV_LORA + MROPE, Q_LORA + KV_LORA + MROPE + RH * RDK
C_RV = C_RK + RH * RDK
C_RG = C_RV + RH * RDV
C_ZA = C_RG + RH * RDV
C_ZR = C_ZA + D

HALVES = ((0, NT // 2), (NT // 2, NT))

POOL_W, WINDOWS = 512, (2, 4, 8, 16)
NH, HD, NG = 16, 64, 2
HPG = NH // NG
KVW = NG * HD
CMP_LEN, CMP_STRIDE, CMP_HID = 32, 16, 256
NCMP = S // CMP_STRIDE - CMP_LEN // CMP_STRIDE + 1
WINDOW, SEL_BLOCK, N_SEL = 512, 64, 16
D_FF = 4 * D
E_Q = POOL_W
E_KC = E_Q + NH * HD
E_KS = E_KC + 2 * KVW
E_GN = E_KS + 4 * KVW
E_GM = E_GN + 3 * NH

RING = 3
SLAB = KT * 512
BANKS = 8
SHARES = {"sel1": 128, "sel2": 128, "sel3": 128, "values1": 128,
          "n2_0": 8, "u_0": 12, "pool_0": 10, "nq2_0": 18, "kc_0": 8, "nkv2_0": 12, "cmp_0": 14, "nr_0": 12, "tq2_0": 4,
          "tk2_0": 2, "na_0": 220, "to2_0": 4, "m2_0": 44, "out_0": 16, "n3_0": 4, "ff1_0": 56, "ff2_0": 68}
GATHERS = 8
PAD = 16


def constants():
    def rope(pos, half):
        inv = (10000.0 ** (-np.arange(half, dtype=np.float32) / half)).astype(np.float32)
        ang = (np.asarray(pos, np.float32)[:, None] * inv[None]).astype(np.float32)
        return np.stack([np.cos(ang), np.sin(ang)], 1).astype(np.float32)

    def tiles(a, tiles_with_meta):
        out = np.zeros((P, NT + tiles_with_meta) + a.shape[1:], np.float32)
        if tiles_with_meta:
            out[:META, 0] = a[:META]
            a = a[META:]
        out[:, tiles_with_meta:] = a.reshape((NT, P) + a.shape[1:]).swapaxes(0, 1)
        return out

    r = np.arange(P)
    gamma = 1.0 - 2.0 ** (-5.0 - np.arange(RH))
    steps = np.arange(L)[None, :] - r[:, None]
    decay = np.where(steps[:, None] >= 0, gamma[None, :, None] ** np.maximum(steps, 0)[:, None] * RDK ** -0.5, 0.0)
    t = np.arange(S)
    ends = np.arange(NCMP) * CMP_STRIDE + CMP_LEN - 1
    seen = (ends[None] <= t[:, None]).astype(np.float32)
    counts = np.stack([1.0 / np.minimum(t + 1, w) for w in WINDOWS])
    c = {
        "identity": np.eye(P),
        "rope_mla": tiles(rope(np.arange(L), MROPE // 2), 1),
        "rope_ret": tiles(rope(np.arange(L), RDK // 2), 1),
        "rope_nsa": tiles(rope(t, HD // 2), 0),
        "rope_cmp": rope(ends, HD // 2),
        "decay": decay,
        "causal": np.where(r[None, :] <= r[:, None], 0.0, NEG),
        "cmp_bias": tiles(np.where(seen > 0, 0.0, NEG), 0),
        "cmp_seen": tiles(seen, 0),
        "inv_count": np.broadcast_to(counts[None], (P,) + counts.shape),
        "iota": np.broadcast_to(np.arange(TOPK)[None], (P, TOPK)),
    }
    return {k: np.ascontiguousarray(v, dtype=np.float32) for k, v in c.items()}


class Core:

    def __init__(self, nc):
        self.nc = nc
        self.w = self.picks = self.psum = self.h = self.identity = self.gain = self.semaphore = None


class Item:

    def __init__(self, q, keys, columns, biases, blocks, seen, gate, out, add):
        self.q, self.keys, self.columns, self.biases = q, keys, columns, biases
        self.blocks, self.seen, self.gate, self.out, self.add = blocks, seen, gate, out, add


def linker(eng, sem):
    count = [0]

    def link(ins):
        count[0] += 1
        ins.then_inc(sem, 1)
        eng.wait_ge(sem, count[0])
    return link


def weight_plan(a):
    def cols(w, c0, n, kt=KT, k0=0):
        return w.rearrange("(k p) n -> p k n", p=P)[:, k0:k0 + kt, c0:c0 + n]

    plan = [("cq", cols(a["w_in"], C_Q, Q_LORA), NT), ("ckv", cols(a["w_in"], C_KV, KV_LORA + MROPE), NT + 1)]
    plan += [(("uq", b), cols(a["w_uq"], 384 * b, 384, 3), NT) for b in range(2)]
    plan += [(("ukv", b), cols(a["w_ukv"], 512 * b, 512, 2), NT + 1) for b in range(2)]
    plan += [("rq", cols(a["w_in"], C_RQ, 512), NT), ("rk", cols(a["w_in"], C_RK, 512), NT + 1)]
    plan += [(("rv", b), cols(a["w_in"], C_RV + 512 * b, 512), NT + 1) for b in range(2)]
    plan += [(("rg", b), cols(a["w_in"], C_RG + 512 * b, 512), 4) for b in range(2)]
    for b in range(2):
        plan += [(("za", b), cols(a["w_in"], C_ZA + 512 * b, 512), 4), (("ya", b), cols(a["w_mla_out"], 512 * b, 512, 4), 4),
                 (("zr", b), cols(a["w_in"], C_ZR + 512 * b, 512), 4), (("yr", b), cols(a["w_ret_out"], 512 * b, 512), 4)]
    plan += [(("mix", b), cols(a["w_mix_out"], 512 * b, 512), NT) for b in range(2)]
    plan += [(("pq", b), cols(a["w_peer_q"], 512 * b, 512), 4) for b in range(2)]
    for half in range(len(HALVES)):
        n = HALVES[half][1] - HALVES[half][0]
        second = [("u", cols(a["w_in2"], 0, 512), 4)]
        second += [(("q", b), cols(a["w_in2"], E_Q + 512 * b, 512), n) for b in range(2)]
        second += [("kcvc", a["w_kcvc"].rearrange("(k p) n -> p k n", p=P), 4), ("kv", cols(a["w_in2"], E_KS, 512), n),
                   ("gn", cols(a["w_in2"], E_GN, 3 * NH), n)]
        second += [("ck1", a["w_ck1"], 2), ("cv1", a["w_cv1"], 2)]
        for b in range(2):
            second += [(("ga", b), cols(a["w_in2"], E_GM + 512 * b, 512), 4), (("yp", b), cols(a["w_proj_pool"], 512 * b, 512, 4), 4),
                       (("gb", b), cols(a["w_in2"], E_GM + D + 512 * b, 512), 4), (("yn", b), cols(a["w_proj_nsa"], 512 * b, 512), 4)]
        second += [(("out", b), cols(a["w_out"], 512 * b, 512), n) for b in range(2)]
        second += [(("ff1", b), cols(a["w_ff1"], 512 * b, 512), 4) for b in range(D_FF // 512)]
        second += [(("ff2", b, k), cols(a["w_ff2"], 512 * b, 512, KT, KT * k), n) for b in range(2) for k in range(4)]
        plan += [((name, half), view, products) for name, view, products in second]
    return plan


class Weights:

    def __init__(self, nc, ctx, plan):
        self.nc, self.plan = nc, plan
        self.ring = ctx.enter_context(nc.sbuf_tensor("weight_ring", [P, RING, SLAB], F32))
        self.landed = [ctx.enter_context(nc.semaphore(f"slab_landed{r}")) for r in range(RING)]
        self.products_done = ctx.enter_context(nc.semaphore("products_done"))
        self.number = {name: i for i, (name, _, _) in enumerate(plan)}
        self.products = [0]
        for _, _, n in plan:
            self.products.append(self.products[-1] + n)
        self.loaded = 0

    def view(self, name):
        i = self.number[name]
        _, kt, n = self.plan[i][1].shape
        return self.ring[:, i % RING, 0:kt * n].rearrange("p (k n) -> p k n", k=kt)

    def load_through(self, sp, name):
        last = -1 if name is None else self.number[name]
        while self.loaded < min(last + 1 + RING, len(self.plan)):
            i = self.loaded
            if i >= RING:
                sp.wait_ge(self.products_done, self.products[i - RING + 1])
            sp.dma_start(self.view(self.plan[i][0]), self.plan[i][1]).then_inc(self.landed[i % RING], 16)
            self.loaded += 1

    def arrived(self, pe, name):
        i = self.number[name]
        pe.wait_ge(self.landed[i % RING], 16 * (i // RING + 1))

    def product(self, name, j):
        return self.products[self.number[name]] + j + 1


class Picks:

    def __init__(self, g, ctx, peer_u, peer_v, expert, gates, x, shares):
        nc, self.g = g.nc, g
        sb = lambda name, shape: ctx.enter_context(nc.sbuf_tensor(f"picks_{name}", shape, F32))
        self.expert, self.gates, self.x, self.shares = expert, gates, x, shares
        self.rows = sb("rows", [P, GATHERS, D])
        self.product = sb("product", [P, D])
        self.dots, self.active, self.weight = (sb(x, [P, PICKS]) for x in ("dots", "active", "weight"))
        self.landed = [ctx.enter_context(nc.semaphore(f"picks_landed{r}")) for r in range(GATHERS)]
        self.rows_used = ctx.enter_context(nc.semaphore("picks_rows_used"))
        self.steps = [(t, table, k) for t in range(NT) for table in (peer_u, peer_v) for k in range(PICKS)]
        self.peer_u = peer_u
        self.issued = self.used = self.first = self.last = 0
        self.turn = self.turns = 0
        self.weights = 0
        self.active_ready = ctx.enter_context(nc.semaphore("picks_active_ready"))
        self.weight_ready = ctx.enter_context(nc.semaphore("picks_weight_ready"))

    def share(self, tag, turns):
        self.first, self.last = self.last, self.last + self.shares.get(tag, 0)
        self.turn, self.turns = 0, turns

    def issue(self, pool):
        if self.last == self.first:
            return
        while self.issued < min(self.last + GATHERS, len(self.steps)):
            n = self.issued
            t, table, k = self.steps[n]
            if n >= GATHERS:
                pool.wait_ge(self.rows_used, n - GATHERS + 1)
            pool.indirect_dma_start(
                out=self.rows[:, n % GATHERS, :], out_offset=None, in_=table,
                in_offset=bass.IndirectOffsetOnAxis(ap=self.expert[:, t, k:k + 1], axis=0),
            ).then_inc(self.landed[n % GATHERS], 16)
            self.issued += 1

    def after(self, turn):
        return self.first + (self.last - self.first) * min(turn, self.turns) // self.turns

    def activate(self, act, turn=None):
        for t in range(NT):
            dots_end = (2 * t + 1) * PICKS
            if (turn is None and self.last == dots_end) or (
                    turn is not None and self.after(turn - 1) < dots_end <= self.after(turn)):
                act.wait_ge(self.rows_used, dots_end)
                self.g.nc.scalar.activation(self.active[:], self.dots[:], ACT.Gelu).then_inc(self.active_ready, 1)

    def make_weights(self, dve, t):
        dve.wait_ge(self.active_ready, t + 1)
        if t:
            dve.wait_ge(self.rows_used, 2 * t * PICKS)
        self.g.nc.vector.tensor_tensor(self.weight[:], self.active[:], self.gates[:, t, :],
                                       ALU.mult).then_inc(self.weight_ready, 1)
        dve.wait_ge(self.weight_ready, t + 1)
        self.weights = t + 1

    def use(self, dve):
        nc = self.g.nc
        self.turn += 1
        while self.used < self.after(self.turn):
            n = self.used
            t, table, k = self.steps[n]
            if table is not self.peer_u and self.weights == t:
                self.make_weights(dve, t)
            row = self.rows[:, n % GATHERS, :]
            dve.wait_ge(self.landed[n % GATHERS], 16 * (n // GATHERS + 1))
            if n:
                dve.wait_ge(self.rows_used, n)
            if table is self.peer_u:
                ins = nc.vector.tensor_tensor_reduce(out=self.product[:], in0=row, in1=self.x[t], scale=1.0, scalar=0.0,
                                                     op0=ALU.mult, op1=ALU.add, accum_out=self.dots[:, k:k + 1])
            else:
                h = self.g.h[:, t, :]
                ins = nc.vector.scalar_tensor_tensor(out=h, in0=row, scalar=self.weight[:, k:k + 1], in1=h, op0=ALU.mult,
                                                     op1=ALU.add)
            ins.then_inc(self.rows_used, 1)
            self.used += 1


class NoPicks:

    def share(self, tag, turns):
        pass

    def issue(self, pool):
        pass

    def use(self, dve):
        pass

    def activate(self, act, turn):
        pass


def row_tile(t):
    return (META, slice(0, META)) if t == 0 else (P, slice(META + P * (t - 1), META + P * t))


def evacuations(owners, n):
    return owners[:n + 1].count(owners[n])


def token_major(g, name, t, xT, columns, rows):
    w = g.w.view(name)
    return (name, t, rows, w.shape[2], [(xT[:, k, columns], w[:, k, :]) for k in range(w.shape[1])])


def feature_major(g, name, j, xT, columns):
    w = g.w.view(name)
    return (name, j, P, columns.stop - columns.start,
            [(w[:, k, P * j:P * j + P], xT[:, k, columns]) for k in range(w.shape[1])])


def multiply(g, pe, products, owners, drained):
    for n, (name, j, rows, cols, pairs) in enumerate(products):
        if j == 0:
            g.w.arrived(pe, name)
        if n >= BANKS:
            pe.wait_ge(drained[owners[n - BANKS]], evacuations(owners, n - BANKS))
        for k, (lhsT, rhs) in enumerate(pairs):
            mm = g.nc.tensor.matmul(g.psum[0:rows, n % BANKS, 0:cols], lhsT, rhs, start=(k == 0),
                                    stop=(k == len(pairs) - 1))
        mm.then_inc(g.w.products_done, 1)


def product_stage(g, tag, products, outputs, last_slab, functions=None):
    nc = g.nc
    functions = functions or [None] * len(products)
    owners = ["act" if functions[n] or n % 2 else "dve" for n in range(len(products))]
    with ExitStack() as ctx:
        drained = {e: g.semaphore(f"{tag}_drained_{e}") for e in ("act", "dve")}
        g.picks.share(tag, len(products))
        block = ctx.enter_context(nc.Block())

        @block.gpsimd
        def _(pool):
            g.picks.issue(pool)

        @block.sync
        def _(sp):
            g.w.load_through(sp, last_slab)

        @block.tensor
        def _(pe):
            multiply(g, pe, products, owners, drained)

        @block.scalar
        def _(act):
            for n, (name, j, rows, cols, _) in enumerate(products):
                if owners[n] == "act":
                    act.wait_ge(g.w.products_done, g.w.product(name, j))
                    nc.scalar.activation(outputs[n], g.psum[0:rows, n % BANKS, 0:cols],
                                         functions[n] or ACT.Copy).then_inc(drained["act"], 1)

        @block.vector
        def _(dve):
            for n, (name, j, rows, cols, _) in enumerate(products):
                if owners[n] == "dve":
                    dve.wait_ge(g.w.products_done, g.w.product(name, j))
                    nc.vector.tensor_copy(outputs[n], g.psum[0:rows, n % BANKS, 0:cols]).then_inc(drained["dve"], 1)
                g.picks.use(dve)


def residual_stage(g, tag, names, xT, tiles, last_slab):
    nc = g.nc
    n_tiles = tiles[1] - tiles[0]
    products = [token_major(g, names[b], t, xT, slice(P * t, P * t + P), P) for b in range(2) for t in range(n_tiles)]
    with ExitStack() as ctx:
        drained = {"dve": g.semaphore(f"{tag}_drained")}
        g.picks.share(tag, len(products))
        block = ctx.enter_context(nc.Block())

        @block.gpsimd
        def _(pool):
            g.picks.issue(pool)

        @block.sync
        def _(sp):
            g.w.load_through(sp, last_slab)

        @block.tensor
        def _(pe):
            multiply(g, pe, products, ["dve"] * len(products), drained)

        @block.vector
        def _(dve):
            for n, (name, t, rows, cols, _) in enumerate(products):
                b = n // n_tiles
                h = g.h[:, tiles[0] + t, 512 * b:512 * b + 512]
                g.picks.use(dve)
                dve.wait_ge(g.w.products_done, g.w.product(name, t))
                nc.vector.tensor_tensor(h, h, g.psum[:, n % BANKS, :], ALU.add).then_inc(drained["dve"], 1)


def norm_stage(g, tag, sources, width, outT=None, gain_columns=None, token_out=None, gain_rows=None, loads=None,
               store=None):
    nc = g.nc
    n, chunks = len(sources), width // P
    with ExitStack() as ctx:
        sb = lambda name, shape: ctx.enter_context(nc.sbuf_tensor(f"{tag}_{name}", shape, F32))
        sem = lambda name: g.semaphore(f"{tag}_{name}")
        junk = sb("squares", [P, width])
        sums, mean, root, inverse = (sb(x, [P, n]) for x in ("sums", "mean", "root", "inverse"))
        scaled = None if token_out is not None else sb("scaled", [P, 2, width])
        s_in, s_zero, s_sq, s_mean, s_root, s_inv = (sem(x) for x in ("in", "zero", "sq", "mean_ready", "root_ready", "inv"))
        s_scaled, s_turned, s_drained, s_out = (sem(x) for x in ("scaled_ready", "turned", "drained", "out"))
        n_loads = len(loads) if loads else 0
        g.picks.share(tag, n)
        block = ctx.enter_context(nc.Block())

        @block.gpsimd
        def _(pool):
            g.picks.issue(pool)

        def buffer(t):
            return token_out[t] if token_out is not None else scaled[:, t % 2, :]

        @block.sync
        def _(sp):
            for dst, src in loads or ():
                sp.dma_start(dst, src).then_inc(s_in, 16)
            if loads:
                g.w.load_through(sp, None)
            if store is not None:
                for t in range(n):
                    sp.wait_ge(s_scaled, t + 1)
                    sp.dma_start(store[:, t, :], token_out[t]).then_inc(s_out, 16)
                sp.wait_ge(s_out, 16 * n)

        @block.scalar
        def _(act):
            act.wait_ge(s_zero, 1)
            if loads:
                act.wait_ge(s_in, 16 * n_loads)
            for t, (src, rows, _) in enumerate(sources):
                if t:
                    act.wait_ge(s_sq, t)
                nc.scalar.activation(junk[0:rows], src, ACT.Square, accum_out=sums[0:rows, t:t + 1]).then_inc(s_sq, 1)
            act.wait_ge(s_mean, 1)
            nc.scalar.activation(root[:], mean[:], ACT.Sqrt).then_inc(s_root, 1)

        def drain(dve, t):
            _, rows, columns = sources[t]
            dve.wait_ge(s_turned, t + 1)
            for c in range(0, chunks, 4):
                m = min(4, chunks - c)
                src = g.psum[:, 2 * (t % 2) + c // 4, :].rearrange("p (c r) -> p c r", c=4)[:, 0:m, 0:rows]
                if gain_columns is None:
                    ins = nc.vector.tensor_copy(outT[:, c:c + m, columns], src)
                else:
                    ins = nc.vector.tensor_tensor(outT[:, c:c + m, columns], src,
                                                  gain_columns[:, c:c + m].unsqueeze(2).to_broadcast([P, m, rows]), ALU.mult)
            ins.then_inc(s_drained, 1)

        @block.vector
        def _(dve):
            nc.vector.memset(sums[:], 1.0).then_inc(s_zero, 1)
            dve.wait_ge(s_sq, n)
            nc.vector.tensor_scalar(mean[:], sums[:], 1.0 / width, EPS, ALU.mult, ALU.add).then_inc(s_mean, 1)
            dve.wait_ge(s_root, 1)
            nc.vector.reciprocal(inverse[:], root[:]).then_inc(s_inv, 1)
            dve.wait_ge(s_inv, 1)
            for t, (src, rows, _) in enumerate(sources):
                g.picks.use(dve)
                if token_out is not None:
                    nc.vector.scalar_tensor_tensor(out=buffer(t)[0:rows], in0=src, scalar=inverse[0:rows, t:t + 1],
                                                   in1=gain_rows, op0=ALU.mult, op1=ALU.mult).then_inc(s_scaled, 1)
                else:
                    if t >= 2:
                        dve.wait_ge(s_turned, t - 1)
                    nc.vector.tensor_scalar(buffer(t)[0:rows], src, inverse[0:rows, t:t + 1], None,
                                            ALU.mult).then_inc(s_scaled, 1)
                if outT is not None and t >= 1:
                    drain(dve, t - 1)
            if outT is not None:
                drain(dve, n - 1)

        if outT is not None:
            @block.tensor
            def _(pe):
                for t, (_, rows, _) in enumerate(sources):
                    pe.wait_ge(s_scaled, t + 1)
                    if t >= 2:
                        pe.wait_ge(s_drained, t - 1)
                    for c in range(chunks):
                        mm = nc.tensor.transpose(g.psum[:, 2 * (t % 2) + c // 4, P * (c % 4):P * (c % 4) + rows],
                                                 buffer(t)[0:rows, P * c:P * c + P], g.identity[0:rows, 0:rows])
                    mm.then_inc(s_turned, 1)


def turn_stage(g, tag, sources, rows_out, scale=1.0):
    nc = g.nc
    with ExitStack() as ctx:
        s_turned = g.semaphore(f"{tag}_turned")
        s_drained = [g.semaphore(f"{tag}_drained{e}") for e in range(2)]
        g.picks.share(tag, len(sources))
        block = ctx.enter_context(nc.Block())

        @block.gpsimd
        def _(pool):
            g.picks.issue(pool)

        def bank(n, m, rows):
            return g.psum[0:rows_out, n % BANKS, :].rearrange("p (c r) -> p c r", c=4)[:, 0:m, 0:rows]

        @block.tensor
        def _(pe):
            for n, (blocks, rows, _) in enumerate(sources):
                if n >= BANKS:
                    pe.wait_ge(s_drained[n % 2], (n - BANKS) // 2 + 1)
                for c, src in enumerate(blocks):
                    mm = nc.tensor.transpose(g.psum[0:rows_out, n % BANKS, P * c:P * c + rows], src,
                                             g.identity[0:rows, 0:rows])
                mm.then_inc(s_turned, 1)

        @block.scalar
        def _(act):
            for n, (blocks, rows, dst) in enumerate(sources):
                if n % 2 == 0:
                    act.wait_ge(s_turned, n + 1)
                    nc.scalar.activation(dst, bank(n, len(blocks), rows), ACT.Copy, scale=scale).then_inc(s_drained[0], 1)

        @block.vector
        def _(dve):
            for n, (blocks, rows, dst) in enumerate(sources):
                if n % 2 == 1:
                    dve.wait_ge(s_turned, n + 1)
                    nc.vector.tensor_scalar(dst, bank(n, len(blocks), rows), scale, None, ALU.mult).then_inc(s_drained[1], 1)
                g.picks.use(dve)


def rope(nc, link, dst, src, table, tmp):
    shape = list(src.shape)
    cos = table[:, 0, :].unsqueeze(1).unsqueeze(1).to_broadcast(shape)
    sin = table[:, 1, :].unsqueeze(1).unsqueeze(1).to_broadcast(shape)
    nc.vector.tensor_tensor(tmp[0], src, cos, ALU.mult)
    link(nc.vector.tensor_tensor(tmp[1], src, sin, ALU.mult))
    nc.vector.tensor_tensor(dst[:, :, 0, :], tmp[0][:, :, 0, :], tmp[1][:, :, 1, :], ALU.subtract)
    link(nc.vector.tensor_tensor(dst[:, :, 1, :], tmp[1][:, :, 0, :], tmp[0][:, :, 1, :], ALU.add))


def rope_stage(g, tag, jobs, width):
    nc = g.nc
    with ExitStack() as ctx:
        tmp = [ctx.enter_context(nc.sbuf_tensor(f"{tag}_tmp{i}", [P, width], F32)) for i in range(2)]
        s_link = g.semaphore(f"{tag}_link")
        g.picks.share(tag, len(jobs))
        block = ctx.enter_context(nc.Block())

        @block.gpsimd
        def _(pool):
            g.picks.issue(pool)

        @block.vector
        def _(dve):
            link = linker(dve, s_link)
            for dst, src, table in jobs:
                rows, heads, _, half = src.shape
                views = [x[0:rows, 0:heads * 2 * half].rearrange("p (h a b) -> p h a b", h=heads, a=2) for x in tmp]
                rope(nc, link, dst, src, table, views)
                g.picks.use(dve)


def mla_qk_stage(g, q, kv, k_pe, q_gain, k_gain, rope_table, k_heads):
    nc = g.nc
    with ExitStack() as ctx:
        sb = lambda name, shape: ctx.enter_context(nc.sbuf_tensor(f"mla_{name}", shape, F32))
        sem = lambda name: g.semaphore(f"mla_{name}")
        n = 2 * NT + 1
        squares = sb("head_squares", [P, MH, QK])
        sums, mean, root, inverse = (sb(x, [P, n, MH]) for x in ("head_sums", "head_mean", "head_root", "head_inverse"))
        tmp = [sb(f"rope_tmp{i}", [P, MH * MROPE]) for i in range(2)]
        s_link, s_mean, s_root = sem("qk_link"), sem("qk_mean"), sem("qk_root")
        block = ctx.enter_context(nc.Block())
        units = []
        for t in range(NT):
            x = q[:, t, :].rearrange("p (h d) -> p h d", h=MH)
            units.append((P, x[:, :, 0:NOPE], x[:, :, NOPE:QK], x, q_gain, t + 1))
        for t in range(NT + 1):
            rows, _ = row_tile(t)
            nope = kv[0:rows, t, :].rearrange("p (h d) -> p h d", h=MH)[:, :, 0:NOPE]
            pe_part = k_pe[0:rows, t, :].unsqueeze(1).to_broadcast([rows, MH, MROPE])
            units.append((rows, nope, pe_part, k_heads[0:rows, t, :].rearrange("p (h d) -> p h d", h=MH), k_gain, t))

        @block.scalar
        def _(act):
            act.wait_ge(s_mean, 1)
            nc.scalar.activation(root[:], mean[:], ACT.Sqrt).then_inc(s_root, 1)

        @block.vector
        def _(dve):
            link = linker(dve, s_link)
            link(nc.vector.memset(sums[:], 1.0))
            for i, (rows, nope, roped, _, _, _) in enumerate(units):
                nc.vector.tensor_tensor(squares[0:rows, :, 0:NOPE], nope, nope, ALU.mult)
                link(nc.vector.tensor_tensor(squares[0:rows, :, NOPE:QK], roped, roped, ALU.mult))
                link(nc.vector.tensor_reduce(sums[0:rows, i, :], squares[0:rows], AX_X, ALU.add))
            nc.vector.tensor_scalar(mean[:], sums[:], 1.0 / QK, EPS, ALU.mult, ALU.add).then_inc(s_mean, 1)
            dve.wait_ge(s_root, 1)
            link(nc.vector.reciprocal(inverse[:], root[:]))
            for i, (rows, nope, roped, dst, gain, t) in enumerate(units):
                scale = inverse[0:rows, i, :].unsqueeze(2)
                nc.vector.tensor_tensor(dst[:, :, 0:NOPE], nope, scale.to_broadcast([rows, MH, NOPE]), ALU.mult)
                link(nc.vector.tensor_tensor(dst[:, :, NOPE:QK], roped, scale.to_broadcast([rows, MH, MROPE]), ALU.mult))
                link(nc.vector.tensor_tensor(dst, dst, gain[0:rows].unsqueeze(1).to_broadcast([rows, MH, QK]), ALU.mult))
                x = dst[:, :, NOPE:QK].rearrange("p h (a b) -> p h a b", a=2)
                views = [v[0:rows].rearrange("p (h a b) -> p h a b", h=MH, a=2) for v in tmp]
                rope(nc, link, x, x, rope_table[0:rows, t, :, :], views)


def attention_stage(g, tag, items, head_dim, last_slab=None):
    nc = g.nc
    n_items = len(items)
    widest = max(it.columns[1] for it in items)
    depth = 4 if widest <= 512 else 2
    lag, late = (2, 3) if depth == 4 else (1, 2)
    score_width = 4 * 512 // depth
    with ExitStack() as ctx:
        sb = lambda name, shape: ctx.enter_context(nc.sbuf_tensor(f"{tag}_{name}", shape, F32))
        sem = lambda name: g.semaphore(f"{tag}_{name}")
        probs = sb("probs", [P, depth, widest])
        probsT = sb("probsT", [P, 2, (widest + P - 1) // P * P])
        negmax, rowsum, factor = sb("negmax", [P, 4]), sb("rowsum", [P, 8]), sb("factor", [P, 8])
        s_scores, s_max, s_exp, s_seen, s_turned, s_copied = (
            sem(x) for x in ("scores", "max", "exp", "seen_done", "turned", "copied"))
        s_values, s_out, s_link = sem("values"), sem("out_done"), sem("link")
        g.picks.share(tag, n_items)
        block = ctx.enter_context(nc.Block())

        @block.gpsimd
        def _(pool):
            g.picks.issue(pool)
        with_mask = [it.seen is not None for it in items]

        def scores(i):
            at = (i % depth) * score_width
            return g.psum[:, 0:4, :].rearrange("p a b -> p (a b)")[:, at:at + score_width]

        def turned(i, m, keys):
            if m < 4:
                return g.psum[0:keys, 4 + i % 2, P * m:P * m + P]
            return g.psum[0:keys, 6 + i % 2, P:2 * P]

        def values(i):
            return g.psum[:, 6 + i % 2, 0:head_dim]

        @block.sync
        def _(sp):
            if last_slab:
                g.w.load_through(sp, last_slab)

        @block.tensor
        def _(pe):
            for i in range(n_items + late):
                if i < n_items:
                    it = items[i]
                    if i >= depth:
                        pe.wait_ge(s_exp, i - depth + 1)
                    for (kT, col) in it.keys:
                        mine = [(b, c) for b, c in it.biases if col <= c < col + kT.shape[1]]
                        mm = nc.tensor.matmul(scores(i)[:, col:col + kT.shape[1]], it.q, kT, start=True, stop=not mine)
                        for b, c in mine:
                            mm = nc.tensor.matmul(scores(i)[:, c:c + b.shape[1]], g.identity[:], b, start=False, stop=True)
                    mm.then_inc(s_scores, 1)
                if i >= late:
                    j, it = i - late, items[i - late]
                    pe.wait_ge(s_copied, j + 1)
                    if j >= 2:
                        pe.wait_ge(s_out, j - 1)
                    for m, (_, keys, v) in enumerate(it.blocks):
                        mm = nc.tensor.matmul(values(j), probsT[0:keys, j % 2, P * m:P * m + P], v, start=(m == 0),
                                              stop=(m == len(it.blocks) - 1))
                    mm.then_inc(s_values, 1)
                if lag <= i < n_items + lag:
                    j, it = i - lag, items[i - lag]
                    pe.wait_ge(s_exp, j + 1)
                    if it.seen is not None:
                        pe.wait_ge(s_seen, sum(with_mask[:j + 1]))
                    if j >= 2:
                        pe.wait_ge(s_copied, j - 1)
                    if j >= 2 and len(it.blocks) > 4:
                        pe.wait_ge(s_out, j - 1)
                    for m, (col, keys, _) in enumerate(it.blocks):
                        mm = nc.tensor.transpose(turned(j, m, keys), probs[:, j % depth, col:col + keys], g.identity[:])
                    mm.then_inc(s_turned, 1)

        @block.scalar
        def _(act):
            for i in range(n_items + lag):
                if i < n_items:
                    lo, hi = items[i].columns
                    act.wait_ge(s_max, i + 1)
                    if i >= depth:
                        act.wait_ge(s_turned, i - depth + 1)
                    nc.scalar.activation(probs[:, i % depth, lo:hi], scores(i)[:, lo:hi], ACT.Exp, bias=negmax[:, i % 4:i % 4 + 1],
                                         accum_out=rowsum[:, i % 8:i % 8 + 1]).then_inc(s_exp, 1)
                if i >= lag:
                    j = i - lag
                    act.wait_ge(s_turned, j + 1)
                    if j >= 2:
                        act.wait_ge(s_values, j - 1)
                    blocks = items[j].blocks
                    full = [m for m, b in enumerate(blocks) if m < 4 and b[1] == P]
                    if full:
                        ins = nc.scalar.copy(probsT[:, j % 2, 0:P * len(full)], g.psum[:, 4 + j % 2, 0:P * len(full)])
                    for m, (_, keys, _) in enumerate(blocks):
                        if m not in full:
                            ins = nc.scalar.copy(probsT[0:keys, j % 2, P * m:P * m + P], turned(j, m, keys))
                    ins.then_inc(s_copied, 1)
                g.picks.activate(act, i + 1)

        @block.vector
        def _(dve):
            link = linker(dve, s_link)
            for i in range(n_items + late + 1):
                if i < n_items:
                    lo, hi = items[i].columns
                    dve.wait_ge(s_scores, i + 1)
                    nc.vector.tensor_reduce(negmax[:, i % 4:i % 4 + 1], scores(i)[:, lo:hi], AX_X, ALU.max,
                                            negate=True).then_inc(s_max, 1)
                if 1 <= i <= n_items and items[i - 1].seen is not None:
                    j = i - 1
                    lo, hi = items[j].columns
                    dve.wait_ge(s_exp, j + 1)
                    p = probs[:, j % depth, lo:hi]
                    nc.vector.tensor_tensor(p, p, items[j].seen, ALU.mult).then_inc(s_seen, 1)
                if i >= late + 1:
                    j, it = i - late - 1, items[i - late - 1]
                    f = factor[:, j % 8:j % 8 + 1]
                    link(nc.vector.reciprocal(f, rowsum[:, j % 8:j % 8 + 1]))
                    if it.gate is not None:
                        link(nc.vector.tensor_tensor(f, f, it.gate, ALU.mult))
                    dve.wait_ge(s_values, j + 1)
                    if it.add:
                        dve.wait_ge(s_out, j)
                        ins = nc.vector.scalar_tensor_tensor(out=it.out, in0=values(j), scalar=f, in1=it.out, op0=ALU.mult,
                                                             op1=ALU.add)
                    else:
                        ins = nc.vector.tensor_scalar(it.out, values(j), f, None, ALU.mult)
                    ins.then_inc(s_out, 1)
                g.picks.use(dve)


RET_Q0 = [0] + [P * t for t in range(NT)]
RET_OFF = [0, S, 2 * S, 3 * S - P, 4 * S - 3 * P]
RET_WIDTH = RET_OFF[-1] + P


def retention_stage(g, rqT, rkT, rv, decay, y, last_slab):
    nc = g.nc
    n_m = NT + 1
    with ExitStack() as ctx:
        sem = lambda name: g.semaphore(f"ret_{name}")
        decayed = ctx.enter_context(nc.sbuf_tensor("ret_decayed", [P, 2, RET_WIDTH], F32))
        s_scores, s_decayed, s_y, s_copied = (sem(x) for x in ("scores", "decayed_ready", "y_ready", "y_copied"))
        block = ctx.enter_context(nc.Block())

        @block.sync
        def _(sp):
            g.w.load_through(sp, last_slab)

        @block.tensor
        def _(pe):
            for h in range(RH + 1):
                if h < RH:
                    part = slice(RDK * (h % 2), RDK * (h % 2) + RDK)
                    for m in range(n_m):
                        n = n_m * h + m
                        rows, columns = row_tile(m)
                        if n >= 4:
                            pe.wait_ge(s_decayed, n - 3)
                        nc.tensor.matmul(g.psum[0:rows, n % 4, 0:S - RET_Q0[m]], rkT[part, h // 2, columns],
                                         rqT[part, h // 2, RET_Q0[m]:S], start=True, stop=True).then_inc(s_scores, 1)
                if h >= 1:
                    j = h - 1
                    pe.wait_ge(s_decayed, n_m * h)
                    if j >= 4:
                        pe.wait_ge(s_copied, j - 3)
                    for t in range(NT):
                        for m in range(t + 2):
                            rows, _ = row_tile(m)
                            at = RET_OFF[m] + P * t - RET_Q0[m]
                            mm = nc.tensor.matmul(g.psum[:, 4 + j % 4, RDV * t:RDV * t + RDV], decayed[0:rows, j % 2, at:at + P],
                                                  rv[0:rows, m, RDV * j:RDV * j + RDV], start=(m == 0), stop=(m == t + 1))
                    mm.then_inc(s_y, 1)

        @block.vector
        def _(dve):
            for h in range(RH):
                for m in range(n_m):
                    n = n_m * h + m
                    rows, _ = row_tile(m)
                    width = S - RET_Q0[m]
                    dve.wait_ge(s_scores, n + 1)
                    if m == 0 and h >= 2:
                        dve.wait_ge(s_y, h - 1)
                    d = decay[0:rows, h, META:L] if m == 0 else decay[0:rows, h, 0:width]
                    nc.vector.tensor_tensor(decayed[0:rows, h % 2, RET_OFF[m]:RET_OFF[m] + width],
                                            g.psum[0:rows, n % 4, 0:width], d, ALU.mult).then_inc(s_decayed, 1)

        @block.scalar
        def _(act):
            for h in range(RH):
                act.wait_ge(s_y, h + 1)
                nc.scalar.copy(y[:, h, :], g.psum[:, 4 + h % 4, :]).then_inc(s_copied, 1)


def group_norm_stage(g, y, gains, ynT):
    nc = g.nc
    with ExitStack() as ctx:
        sb = lambda name, shape: ctx.enter_context(nc.sbuf_tensor(f"gn_{name}", shape, F32))
        sem = lambda name: g.semaphore(f"gn_{name}")
        n = RH * NT
        stats, moments = sb("stats", [P, n, 6]), sb("moments", [P, n, 2])
        root, inverse = sb("root", [P, n]), sb("inverse", [P, n])
        s_link, s_var, s_root, s_normed, s_turned, s_drained = (
            sem(x) for x in ("link", "var", "root_ready", "normed", "turned", "drained"))
        block = ctx.enter_context(nc.Block())

        @block.vector
        def _(dve):
            link = linker(dve, s_link)
            for i in range(n):
                ins = nc.vector.bn_stats(stats[:, i, :], y[:, i // NT, RDV * (i % NT):RDV * (i % NT) + RDV])
            link(ins)
            for i in range(n):
                ins = nc.vector.bn_aggr(moments[:, i, :], stats[:, i, :])
            link(ins)
            nc.vector.tensor_scalar(inverse[:], moments[:, :, 1], EPS, None, ALU.add).then_inc(s_var, 1)
            dve.wait_ge(s_root, 1)
            link(nc.vector.reciprocal(inverse[:], root[:]))
            for i in range(n):
                yi = y[:, i // NT, RDV * (i % NT):RDV * (i % NT) + RDV]
                nc.vector.tensor_scalar(yi, yi, moments[:, i, 0:1], inverse[:, i:i + 1], ALU.subtract,
                                        ALU.mult).then_inc(s_normed, 1)

        @block.tensor
        def _(pe):
            for h in range(RH):
                pe.wait_ge(s_normed, NT * (h + 1))
                if h >= 4:
                    pe.wait_ge(s_drained, h - 3)
                for t in range(NT):
                    mm = nc.tensor.transpose(g.psum[:, h % 4, P * t:P * t + P], y[:, h, RDV * t:RDV * t + RDV], g.identity[:])
                mm.then_inc(s_turned, 1)

        @block.scalar
        def _(act):
            act.wait_ge(s_var, 1)
            nc.scalar.activation(root[:], inverse[:], ACT.Sqrt).then_inc(s_root, 1)
            for h in range(RH):
                act.wait_ge(s_turned, h + 1)
                nc.scalar.activation(ynT[:, h, :], g.psum[:, h % 4, :], ACT.Copy, scale=gains[:, h:h + 1]).then_inc(s_drained, 1)


def retention_gate_stage(g, hnT, ynT, last_slab):
    nc = g.nc
    products = [feature_major(g, ("rg", b), j, hnT, slice(META, L)) for b in range(2) for j in range(4)]
    with ExitStack() as ctx:
        gate = ctx.enter_context(nc.sbuf_tensor("rg_silu", [P, 2, S], F32))
        drained = {"act": g.semaphore("rg_drained")}
        s_used = g.semaphore("rg_used")
        block = ctx.enter_context(nc.Block())

        @block.sync
        def _(sp):
            g.w.load_through(sp, last_slab)

        @block.tensor
        def _(pe):
            multiply(g, pe, products, ["act"] * 8, drained)

        @block.scalar
        def _(act):
            for n, (name, j, _, _, _) in enumerate(products):
                act.wait_ge(g.w.products_done, g.w.product(name, j))
                if n >= 2:
                    act.wait_ge(s_used, n - 1)
                nc.scalar.activation(gate[:, n % 2, :], g.psum[:, n % BANKS, :], ACT.Silu).then_inc(drained["act"], 1)

        @block.vector
        def _(dve):
            for n in range(8):
                dve.wait_ge(drained["act"], n + 1)
                nc.vector.tensor_tensor(ynT[:, n, :], ynT[:, n, :], gate[:, n % 2, :], ALU.mult).then_inc(s_used, 1)


def merge_stage(g, tag, names, gate_input, gate_columns, inputs, mergedT, last_slab, half=None):
    nc = g.nc
    gate_a, prod_a, gate_b, prod_b = names
    slab = lambda name, b: (name, b) if half is None else ((name, b), half)
    products, owners = [], []
    width = gate_columns.stop - gate_columns.start
    for b in range(2):
        for gate, prod, x in ((gate_a, prod_a, inputs[0]), (gate_b, prod_b, inputs[1])):
            products += [feature_major(g, slab(gate, b), j, gate_input, gate_columns) for j in range(4)]
            products += [feature_major(g, slab(prod, b), j, x, slice(0, width)) for j in range(4)]
            owners += ["act"] * 4 + ["dve"] * 4
    with ExitStack() as ctx:
        gates = ctx.enter_context(nc.sbuf_tensor(f"{tag}_gates", [P, 8, width], F32))
        term = ctx.enter_context(nc.sbuf_tensor(f"{tag}_term", [P, 2, width], F32))
        drained = {e: g.semaphore(f"{tag}_drained_{e}") for e in ("act", "dve")}
        s_merged = g.semaphore(f"{tag}_merged")
        g.picks.share(tag, 16)
        block = ctx.enter_context(nc.Block())

        @block.gpsimd
        def _(pool):
            g.picks.issue(pool)

        @block.sync
        def _(sp):
            g.w.load_through(sp, last_slab)

        @block.tensor
        def _(pe):
            multiply(g, pe, products, owners, drained)

        @block.scalar
        def _(act):
            done = 0
            for n, (name, j, _, _, _) in enumerate(products):
                if owners[n] != "act":
                    continue
                act.wait_ge(g.w.products_done, g.w.product(name, j))
                if done >= 8:
                    act.wait_ge(drained["dve"], done - 7)
                nc.scalar.activation(gates[:, done % 8, :], g.psum[:, n % BANKS, 0:width], ACT.Sigmoid).then_inc(drained["act"], 1)
                done += 1

        @block.vector
        def _(dve):
            done = 0
            for n, (name, j, _, _, _) in enumerate(products):
                if owners[n] != "dve":
                    continue
                second = (n // 8) % 2
                out = mergedT[:, 4 * (n // 16) + j, :]
                dve.wait_ge(g.w.products_done, g.w.product(name, j))
                dve.wait_ge(drained["act"], done + 1)
                nc.vector.tensor_tensor(term[:, j % 2, :] if second else out, g.psum[:, n % BANKS, 0:width],
                                        gates[:, done % 8, :], ALU.mult).then_inc(drained["dve"], 1)
                done += 1
                if second:
                    dve.wait_ge(drained["dve"], done)
                    nc.vector.tensor_tensor(out, out, term[:, j % 2, :], ALU.add).then_inc(s_merged, 1)
                g.picks.use(dve)


def peer_select_stage(g, tag, t, pqT, keysT, iota, expert, gates):
    nc = g.nc
    with ExitStack() as ctx:
        sb = lambda name, shape, dt=F32: ctx.enter_context(nc.sbuf_tensor(f"{tag}_{name}", shape, dt))
        sem = lambda name: g.semaphore(f"{tag}_{name}")
        rest = sb("rest", [P, PK])
        best = sb("best", [P, PH, 2, TOPK])
        at = sb("at", [P, PH, 2, TOPK], U32)
        at_f = sb("at_f", [P, PH, 2, TOPK])
        cand, cand_rest = sb("cand", [P, TOPK, TOPK]), sb("cand_rest", [P, TOPK * TOPK])
        top, pick = sb("top", [P, PH, TOPK]), sb("pick", [P, PH, TOPK], U32)
        part, part_f = sb("part", [P, 2, PH, TOPK], U32), sb("part_f", [P, 2, PH, TOPK])
        equal = sb("equal", [P, PH, TOPK, TOPK])
        number = sb("number", [P, 2, PH, TOPK])
        over, weight = sb("over", [P, PH, TOPK]), sb("weight", [P, PH, TOPK])
        total, inverse = sb("total", [P, PH]), sb("inverse", [P, PH])
        s_scores, s_taken, s_over, s_exp, s_link = (sem(x) for x in ("scores", "taken", "over_ready", "exp", "link"))
        g.picks.share(tag, 2 * PH - 1)
        block = ctx.enter_context(nc.Block())

        def scores(n):
            h, half = n // 2, n % 2
            return g.psum[:, 2 * half + h // 4, PK * (h % 4):PK * (h % 4) + PK]

        @block.gpsimd
        def _(pool):
            g.picks.issue(pool)

        @block.tensor
        def _(pe):
            for h in range(PH):
                for half in range(2):
                    rows = slice(64 * half, 64 * half + 64)
                    mm = nc.tensor.matmul(scores(2 * h + half), pqT[rows, h, P * t:P * t + P], keysT[rows, :],
                                          start=True, stop=True)
            mm.then_inc(s_scores, 1)

        @block.scalar
        def _(act):
            act.wait_ge(s_over, 1)
            nc.scalar.activation(weight[:], over[:], ACT.Exp).then_inc(s_exp, 1)

        @block.vector
        def _(dve):
            link = linker(dve, s_link)

            def top16(values, numbers, src, scratch):
                link(nc.vector.max(values[:, 0:8], src))
                nc.vector.max_index(numbers[:, 0:8], values[:, 0:8], src)
                link(nc.vector.match_replace(scratch, values[:, 0:8], src, LOWEST))
                link(nc.vector.max(values[:, 8:16], scratch))
                return nc.vector.max_index(numbers[:, 8:16], values[:, 8:16], scratch)

            dve.wait_ge(s_scores, 1)
            for h in range(PH):
                for half in range(2):
                    ins = top16(best[:, h, half, :], at[:, h, half, :], scores(2 * h + half), rest[:])
                if h < PH - 1:
                    g.picks.use(dve)
            ins.then_inc(s_taken, 1)
            dve.wait_ge(s_taken, 1)
            link(nc.vector.tensor_copy(at_f[:], at[:]))
            for h in range(PH):
                link(nc.vector.tensor_tensor(cand[:], best[:, h, 0, :].unsqueeze(2).to_broadcast([P, TOPK, TOPK]),
                                             best[:, h, 1, :].unsqueeze(1).to_broadcast([P, TOPK, TOPK]), ALU.add))
                ins = top16(top[:, h, :], pick[:, h, :], cand[:].rearrange("p a b -> p (a b)"), cand_rest[:])
                g.picks.use(dve)
            link(ins)
            nc.vector.tensor_tensor(over[:], top[:], top[:, :, 0:1].to_broadcast([P, PH, TOPK]),
                                    ALU.subtract).then_inc(s_over, 1)
            nc.vector.tensor_scalar(part[:, 0], pick[:], 4, None, ALU.logical_shift_right)
            link(nc.vector.tensor_scalar(part[:, 1], pick[:], TOPK - 1, None, ALU.bitwise_and))
            link(nc.vector.tensor_copy(part_f[:], part[:]))
            for half in range(2):
                shape = [P, PH, TOPK, TOPK]
                link(nc.vector.tensor_tensor(equal[:], part_f[:, half].unsqueeze(3).to_broadcast(shape),
                                             iota.unsqueeze(1).unsqueeze(1).to_broadcast(shape), ALU.is_equal))
                link(nc.vector.tensor_tensor(equal[:], equal[:], at_f[:, :, half, :].unsqueeze(2).to_broadcast(shape),
                                             ALU.mult))
                link(nc.vector.tensor_reduce(number[:, half], equal[:], AX_X, ALU.add))
            link(nc.vector.scalar_tensor_tensor(out=expert[:, t, :], in0=number[:, 0].rearrange("p h k -> p (h k)"),
                                                scalar=float(PK), in1=number[:, 1].rearrange("p h k -> p (h k)"),
                                                op0=ALU.mult, op1=ALU.add))
            dve.wait_ge(s_exp, 1)
            link(nc.vector.tensor_reduce(total[:], weight[:], AX_X, ALU.add))
            link(nc.vector.reciprocal(inverse[:], total[:]))
            link(nc.vector.tensor_tensor(gates[:, t, :].rearrange("p (h k) -> p h k", h=PH), weight[:],
                                         inverse[:].unsqueeze(2).to_broadcast([P, PH, TOPK]), ALU.mult))


def picks_stage(g, tag):
    with ExitStack() as ctx:
        g.picks.share(tag, 1)
        block = ctx.enter_context(g.nc.Block())

        @block.gpsimd
        def _(pool):
            g.picks.issue(pool)

        @block.vector
        def _(dve):
            g.picks.use(dve)


def picks_weight_stage(g):
    with ExitStack() as ctx:
        block = ctx.enter_context(g.nc.Block())

        @block.scalar
        def _(act):
            g.picks.activate(act)

        @block.vector
        def _(dve):
            g.picks.make_weights(dve, g.picks.weights)


def compress_input_stage(g, tag, h2T, half, pe_table, kc, last_slab):
    nc = g.nc
    first, last = (P * t // CMP_STRIDE for t in HALVES[half])
    name = ("kcvc", half)
    products = [feature_major(g, name, j, h2T, slice(0, CMP_STRIDE * (last - first))) for j in range(4)]
    with ExitStack() as ctx:
        drained = {"dve": g.semaphore(f"{tag}_drained")}
        g.picks.share(tag, 4)
        block = ctx.enter_context(nc.Block())

        @block.gpsimd
        def _(pool):
            g.picks.issue(pool)

        @block.sync
        def _(sp):
            g.w.load_through(sp, last_slab)

        @block.tensor
        def _(pe):
            multiply(g, pe, products, ["dve"] * 4, drained)

        @block.vector
        def _(dve):
            for j in range(4):
                dve.wait_ge(g.w.products_done, g.w.product(name, j))
                for part in range(2):
                    rows = slice(HD * part, HD * part + HD)
                    n0, n1 = max(first - part, 0), min(last - part, NCMP)
                    at = CMP_STRIDE * (n0 + part - first)
                    ins = nc.vector.tensor_tensor(
                        kc[rows, j // 2, j % 2, CMP_STRIDE * n0:CMP_STRIDE * n1].rearrange("p (n l) -> p n l", l=CMP_STRIDE),
                        g.psum[rows, j, at:at + CMP_STRIDE * (n1 - n0)].rearrange("p (n l) -> p n l", l=CMP_STRIDE),
                        pe_table[rows, j // 2, :].unsqueeze(1).to_broadcast([HD, n1 - n0, CMP_STRIDE]), ALU.add)
                ins.then_inc(drained["dve"], 1)
                g.picks.use(dve)


def compress_stage(g, tag, half, n, kc, w2, rope_cmp, k_cmpT, v_cmp, last_slab):
    nc = g.nc
    with ExitStack() as ctx:
        sb = lambda name, shape: ctx.enter_context(nc.sbuf_tensor(f"{tag}_{name}", shape, F32))
        sem = lambda name: g.semaphore(f"{tag}_{name}")
        hidden = sb("hidden", [P, 2, 2, NG * n])
        k_tok, k_roped = sb("k_tok", [n, NG * HD]), sb("k_roped", [n, NG * HD])
        tmp = [sb(f"tmp{i}", [n, NG * HD]) for i in range(2)]
        s_hidden, s_out, s_copied, s_link, s_roped, s_turned = (
            sem(x) for x in ("hidden_ready", "out_ready", "copied", "link", "roped", "turned"))
        g.picks.share(tag, 3)
        block = ctx.enter_context(nc.Block())

        @block.gpsimd
        def _(pool):
            g.picks.issue(pool)

        @block.sync
        def _(sp):
            g.w.load_through(sp, last_slab)

        @block.tensor
        def _(pe):
            for x, name in enumerate((("ck1", half), ("cv1", half))):
                g.w.arrived(pe, name)
                w1 = g.w.view(name)
                for j in range(2):
                    for l in range(CMP_STRIDE):
                        rhs = kc[:, x, :, :].rearrange("p g (n l) -> p g n l", l=CMP_STRIDE)[:, :, 0:n, l]
                        mm = nc.tensor.matmul(g.psum[:, 2 * x + j, 0:NG * n].rearrange("p (g n) -> p g n", g=NG),
                                              w1[:, l, P * j:P * j + P], rhs, start=(l == 0), stop=(l == CMP_STRIDE - 1))
                    mm.then_inc(g.w.products_done, 1)
            for x in range(2):
                pe.wait_ge(s_hidden, 2 * x + 2)
                for grp in range(NG):
                    for j in range(2):
                        mm = nc.tensor.matmul(g.psum[0:n, 4 + x, HD * grp:HD * grp + HD],
                                              hidden[:, x, j, n * grp:n * grp + n], w2[:, x, j, :],
                                              start=(j == 0), stop=(j == 1))
                mm.then_inc(s_out, 1)
            pe.wait_ge(s_roped, 1)
            for grp in range(NG):
                mm = nc.tensor.transpose(g.psum[0:HD, 6, P * grp:P * grp + n], k_roped[:, HD * grp:HD * grp + HD],
                                         g.identity[0:n, 0:n])
            mm.then_inc(s_turned, 1)

        @block.scalar
        def _(act):
            for x, name in enumerate((("ck1", half), ("cv1", half))):
                for j in range(2):
                    act.wait_ge(g.w.products_done, g.w.product(name, j))
                    nc.scalar.activation(hidden[:, x, j, :], g.psum[:, 2 * x + j, 0:NG * n],
                                         ACT.Gelu_apprx_tanh).then_inc(s_hidden, 1)

        @block.vector
        def _(dve):
            link = linker(dve, s_link)
            g.picks.use(dve)
            dve.wait_ge(s_out, 1)
            link(nc.vector.tensor_copy(k_tok[:], g.psum[0:n, 4, 0:NG * HD]))
            view = lambda x: x[:].rearrange("p (h a b) -> p h a b", h=NG, a=2)
            rope(nc, link, view(k_roped), view(k_tok), rope_cmp, [view(x) for x in tmp])
            nc.vector.memset(k_tok[:, 0:1], 0.0).then_inc(s_roped, 1)
            g.picks.use(dve)
            dve.wait_ge(s_out, 2)
            nc.vector.tensor_copy(v_cmp, g.psum[0:n, 5, 0:NG * HD])
            g.picks.use(dve)
            dve.wait_ge(s_turned, 1)
            link(nc.vector.tensor_copy(k_cmpT, g.psum[0:HD, 6, :].rearrange("p (g n) -> p g n", g=4)[:, 0:NG, 0:n]))


def pool_stage(g, tag, uT, tokens, inv_count, w_pool, pool_scale, ypT):
    nc = g.nc
    n = len(WINDOWS)
    lo, hi = tokens
    width = hi - lo
    with ExitStack() as ctx:
        sem = lambda name: g.semaphore(f"{tag}_{name}")
        sums = [ctx.enter_context(nc.sbuf_tensor(f"{tag}_sums{i}", [P, n, PAD + width], F32)) for i in range(2)]
        s_link, s_diff, s_y = sem("link"), sem("diff"), sem("y")
        g.picks.share(tag, n)
        block = ctx.enter_context(nc.Block())

        @block.gpsimd
        def _(pool):
            g.picks.issue(pool)

        @block.vector
        def _(dve):
            link = linker(dve, s_link)
            if lo == 0:
                link(nc.vector.memset(uT[:, :, 0:PAD], 0.0))
            mine = uT[:, :, lo:PAD + hi]
            src = mine
            for j in range(n):
                dst = sums[j % 2]
                step = 2 ** j
                at = 2 * step
                link(nc.vector.tensor_tensor(dst[:, j:n, at:], src[:, j:n, at:], src[:, j:n, at - step:PAD + width - step],
                                             ALU.add))
                link(nc.vector.tensor_tensor(ypT[:, j, :], dst[:, j, PAD:], inv_count[:, j, lo:hi], ALU.mult))
                ins = nc.vector.tensor_tensor(ypT[:, j, :], ypT[:, j, :], mine[:, j, PAD:], ALU.subtract)
                if j < n - 1:
                    link(ins)
                else:
                    ins.then_inc(s_diff, 1)
                src = dst
                g.picks.use(dve)

        @block.tensor
        def _(pe):
            pe.wait_ge(s_diff, 1)
            for j in range(n):
                nc.tensor.matmul(g.psum[:, j, 0:width], w_pool[:, j, :], ypT[:, j, :], start=True, stop=True).then_inc(s_y, 1)

        @block.scalar
        def _(act):
            for j in range(n):
                act.wait_ge(s_y, j + 1)
                nc.scalar.activation(ypT[:, j, :], g.psum[:, j, 0:width], ACT.Copy, scale=pool_scale[:, j:j + 1])


def mlp_up_stage(g, tag, half, h2T, aT, last_slab):
    nc = g.nc
    n_slabs = D_FF // 512
    width = P * (HALVES[half][1] - HALVES[half][0])
    products = [feature_major(g, (("ff1", b), half), j, h2T, slice(0, width)) for b in range(n_slabs) for j in range(4)]
    with ExitStack() as ctx:
        drained = {"act": g.semaphore(f"{tag}_drained")}
        positive = ctx.enter_context(nc.sbuf_tensor(f"{tag}_positive", [P, 4, width], F32))
        s_squared = g.semaphore(f"{tag}_squared")
        g.picks.share(tag, len(products))
        block = ctx.enter_context(nc.Block())

        @block.gpsimd
        def _(pool):
            g.picks.issue(pool)

        @block.sync
        def _(sp):
            g.w.load_through(sp, last_slab)

        @block.tensor
        def _(pe):
            multiply(g, pe, products, ["act"] * len(products), drained)

        @block.scalar
        def _(act):
            for n, (name, j, _, _, _) in enumerate(products):
                act.wait_ge(g.w.products_done, g.w.product(name, j))
                if n >= 4:
                    act.wait_ge(s_squared, n - 3)
                nc.scalar.activation(positive[:, n % 4, :], g.psum[:, n % BANKS, 0:width], ACT.Relu).then_inc(drained["act"], 1)

        @block.vector
        def _(dve):
            for n in range(len(products)):
                dve.wait_ge(drained["act"], n + 1)
                x = positive[:, n % 4, :]
                nc.vector.tensor_tensor(aT[:, n, :], x, x, ALU.mult).then_inc(s_squared, 1)
                g.picks.use(dve)


def mlp_down_stage(g, tag, half, aT, last_slab):
    nc = g.nc
    groups = D_FF // P // KT
    first, last = HALVES[half]
    n_tiles = last - first
    with ExitStack() as ctx:
        s_added = g.semaphore(f"{tag}_added")
        g.picks.share(tag, 2 * groups)
        block = ctx.enter_context(nc.Block())

        @block.gpsimd
        def _(pool):
            g.picks.issue(pool)

        @block.sync
        def _(sp):
            g.w.load_through(sp, last_slab)

        @block.tensor
        def _(pe):
            for b in range(2):
                for k in range(groups):
                    name = (("ff2", b, k), half)
                    g.w.arrived(pe, name)
                    w = g.w.view(name)
                    for t in range(n_tiles):
                        for i in range(KT):
                            mm = nc.tensor.matmul(g.psum[:, n_tiles * b + t, :], aT[:, KT * k + i, P * t:P * t + P], w[:, i, :],
                                                  start=(k == 0 and i == 0), stop=(k == groups - 1 and i == KT - 1))
                        mm.then_inc(g.w.products_done, 1)

        @block.vector
        def _(dve):
            for b in range(2):
                for k in range(groups):
                    g.picks.use(dve)
                for t in range(n_tiles):
                    h = g.h[:, first + t, 512 * b:512 * b + 512]
                    dve.wait_ge(g.w.products_done, g.w.product((("ff2", b, groups - 1), half), t))
                    nc.vector.tensor_tensor(h, h, g.psum[:, n_tiles * b + t, :], ALU.add).then_inc(s_added, 1)


def load_stage(g, tag, pairs):
    with ExitStack() as ctx:
        s = g.semaphore(f"{tag}_loaded")
        block = ctx.enter_context(g.nc.Block())

        @block.sync
        def _(sp):
            for dst, src in pairs:
                sp.dma_start(dst, src).then_inc(s, 16)
            sp.wait_ge(s, 16 * len(pairs))


def build(nc, a):
    with ExitStack() as whole:
        g = Core(nc)
        alloc = lambda ctx, name, shape, dt=F32: ctx.enter_context(nc.sbuf_tensor(name, shape, dt))
        stage_semaphores = []
        g.picks = NoPicks()

        def semaphore(name):
            stage_semaphores.append(nc.alloc_semaphore(name=name))
            return stage_semaphores[-1]

        def clear_semaphores():
            nc.clear_and_free_semaphores(stage_semaphores)
            nc.all_engine_barrier()
            stage_semaphores.clear()

        g.semaphore = semaphore
        g.psum = whole.enter_context(nc.psum_tensor("psum", [P, BANKS, 512], F32))
        g.w = Weights(nc, whole, weight_plan(a))
        g.h = alloc(whole, "h", [P, NT, D])
        g.identity = alloc(whole, "identity_sb", [P, P])
        gains = alloc(whole, "gains", [P, 96])
        names = [("g_mix", 8), ("g_q_lora", 3), ("g_kv_lora", 2), ("g_ret_gn", 8), ("norm_mix", 8), ("norm_mlp", 8),
                 ("pool_scale", 4)]
        g.gain, at, gain_loads = {}, 0, []
        for name, n in names:
            g.gain[name] = gains[:, at:at + n]
            gain_loads.append((g.gain[name], a[name]))
            at += n
        x_tiles = a["x"].rearrange("(t p) d -> p t d", p=P)

        with ExitStack() as first:
            hnT = alloc(first, "hnT", [P, KT, L])
            o_tok = alloc(first, "mla_o", [P, NT, MH * MV])
            with ExitStack() as s:
                meta = alloc(s, "meta", [META, D])
                loads = [(meta[:], a["meta_tokens"]), (g.h[:], x_tiles), (g.identity[:], a["identity"])] + gain_loads
                sources = [(meta[:], META, row_tile(0)[1])] + [(g.h[:, t, :], P, row_tile(t + 1)[1]) for t in range(NT)]
                norm_stage(g, "n1", sources, D, outT=hnT, gain_columns=g.gain["g_mix"], loads=loads)

            with ExitStack() as mla:
                qT, kT = alloc(mla, "qT", [QK, MH, S]), alloc(mla, "kT", [QK, MH, L])
                kv = alloc(mla, "kv", [P, NT + 1, MH * (NOPE + MV)])
                with ExitStack() as s:
                    ckv = alloc(s, "ckv", [P, NT + 1, KV_LORA + MROPE])
                    q = alloc(s, "q", [P, NT, MH * QK])
                    with ExitStack() as lat:
                        cq = alloc(lat, "cq", [P, NT, Q_LORA])
                        cqT, ckvT = alloc(lat, "cqT", [P, 3, S]), alloc(lat, "ckvT", [P, 2, L])
                        products = [token_major(g, "cq", t, hnT, row_tile(t + 1)[1], P) for t in range(NT)]
                        outputs = [cq[:, t, :] for t in range(NT)]
                        for t in range(NT + 1):
                            rows, columns = row_tile(t)
                            products.append(token_major(g, "ckv", t, hnT, columns, rows))
                            outputs.append(ckv[0:rows, t, :])
                        product_stage(g, "lat", products, outputs, "ckv")
                        norm_stage(g, "nq", [(cq[:, t, :], P, slice(P * t, P * t + P)) for t in range(NT)], Q_LORA,
                                   outT=cqT, gain_columns=g.gain["g_q_lora"])
                        norm_stage(g, "nkv", [(ckv[0:row_tile(t)[0], t, 0:KV_LORA],) + row_tile(t) for t in range(NT + 1)],
                                   KV_LORA, outT=ckvT, gain_columns=g.gain["g_kv_lora"])
                        products, outputs = [], []
                        for b in range(2):
                            for t in range(NT):
                                products.append(token_major(g, ("uq", b), t, cqT, slice(P * t, P * t + P), P))
                                outputs.append(q[:, t, 384 * b:384 * b + 384])
                        for b in range(2):
                            for t in range(NT + 1):
                                rows, columns = row_tile(t)
                                products.append(token_major(g, ("ukv", b), t, ckvT, columns, rows))
                                outputs.append(kv[0:rows, t, 512 * b:512 * b + 512])
                        product_stage(g, "up", products, outputs, ("ukv", 1))
                    with ExitStack() as heads:
                        k_heads = alloc(heads, "k_heads", [P, NT + 1, MH * QK])
                        q_gain, k_gain = alloc(heads, "q_gain", [P, QK]), alloc(heads, "k_gain", [P, QK])
                        table = alloc(heads, "rope_mla_sb", [P, NT + 1, 2, MROPE // 2])
                        load_stage(g, "mla", [(q_gain[:], a["g_qk_q"].partition_broadcast(P)),
                                              (k_gain[:], a["g_qk_k"].partition_broadcast(P)), (table[:], a["rope_mla"])])
                        mla_qk_stage(g, q, kv, ckv[:, :, KV_LORA:], q_gain, k_gain, table, k_heads)
                        sources = []
                        for t in range(NT):
                            for h0 in (0, 4):
                                sources.append(([q[:, t, QK * h:QK * h + QK] for h in range(h0, h0 + 4)], P,
                                                qT[:, h0:h0 + 4, P * t:P * t + P]))
                        turn_stage(g, "tq", sources, QK, scale=QK ** -0.5)
                        sources = []
                        for t in range(NT + 1):
                            rows, columns = row_tile(t)
                            for h0 in (0, 4):
                                sources.append(([k_heads[0:rows, t, QK * h:QK * h + QK] for h in range(h0, h0 + 4)], rows,
                                                kT[:, h0:h0 + 4, columns]))
                        turn_stage(g, "tk", sources, QK)
                with ExitStack() as s:
                    causal = alloc(s, "causal_sb", [P, P])
                    load_stage(g, "causal", [(causal[:], a["causal"])])
                    items = []
                    for t in range(NT):
                        for h in range(MH):
                            lo = 512 - P * (t + 1)
                            v = kv[:, :, 128 * h + NOPE:128 * h + 128]
                            items.append(Item(
                                q=qT[:, h, P * t:P * t + P], columns=(lo, 512 + META),
                                keys=[(kT[:, h, META:META + P * (t + 1)], lo), (kT[:, h, 0:META], 512)],
                                biases=[(causal[:], 512 - P)], seen=None, gate=None, add=False,
                                blocks=[(lo + P * m, P, v[:, m + 1, :]) for m in range(t + 1)] + [(512, META, v[0:META, 0, :])],
                                out=o_tok[:, t, MV * h:MV * h + MV]))
                    attention_stage(g, "ma", items, MV)

            clear_semaphores()
            ynT = alloc(first, "ynT", [P, RH, S])
            with ExitStack() as ret:
                rqT, rkT = alloc(ret, "rqT", [P, RH // 2, S]), alloc(ret, "rkT", [P, RH // 2, L])
                rv = alloc(ret, "rv", [P, NT + 1, RH * RDV])
                with ExitStack() as s:
                    rq, rk = alloc(s, "rq", [P, NT, RH * RDK]), alloc(s, "rk", [P, NT + 1, RH * RDK])
                    table = alloc(s, "rope_ret_sb", [P, NT + 1, 2, RDK // 2])
                    products = [token_major(g, "rq", t, hnT, row_tile(t + 1)[1], P) for t in range(NT)]
                    outputs = [rq[:, t, :] for t in range(NT)]
                    for name, dst, c0 in (("rk", rk, 0), (("rv", 0), rv, 0), (("rv", 1), rv, 512)):
                        for t in range(NT + 1):
                            rows, columns = row_tile(t)
                            products.append(token_major(g, name, t, hnT, columns, rows))
                            outputs.append(dst[0:rows, t, c0:c0 + 512])
                    product_stage(g, "rp", products, outputs, ("rv", 1))
                    load_stage(g, "ropret", [(table[:], a["rope_ret"])])
                    jobs = []
                    for x, t, i in [(rq, t, t + 1) for t in range(NT)] + [(rk, t, t) for t in range(NT + 1)]:
                        rows, _ = row_tile(i)
                        view = x[0:rows, t, :].rearrange("p (h a b) -> p h a b", h=RH, a=2)
                        jobs.append((view, view, table[0:rows, i, :, :]))
                    rope_stage(g, "rr", jobs, RH * RDK)
                    sources = [([rq[:, t, P * c:P * c + P] for c in range(4)], P, rqT[:, :, P * t:P * t + P])
                               for t in range(NT)]
                    for t in range(NT + 1):
                        rows, columns = row_tile(t)
                        sources.append(([rk[0:rows, t, P * c:P * c + P] for c in range(4)], rows, rkT[:, :, columns]))
                    turn_stage(g, "tr", sources, P)
                y = alloc(ret, "ret_y", [P, RH, NT * RDV])
                with ExitStack() as s:
                    decay = alloc(s, "decay_sb", [P, RH, L])
                    load_stage(g, "decay", [(decay[:], a["decay"])])
                    retention_stage(g, rqT, rkT, rv, decay, y, ("rv", 1))
                group_norm_stage(g, y, g.gain["g_ret_gn"], ynT)
            retention_gate_stage(g, hnT, ynT, ("rg", 1))

            with ExitStack() as s:
                oT, mergedT = alloc(s, "oT", [P, 4, S]), alloc(s, "mergedT", [P, KT, S])
                turn_stage(g, "to", [([o_tok[:, t, P * c:P * c + P] for c in range(4)], P, oT[:, :, P * t:P * t + P])
                                     for t in range(NT)], P)
                merge_stage(g, "m1", ("za", "ya", "zr", "yr"), hnT, slice(META, L), (oT, ynT), mergedT, ("yr", 1))
                residual_stage(g, "mix", [("mix", 0), ("mix", 1)], mergedT, (0, NT), ("mix", 1))

        clear_semaphores()
        peer = whole.enter_context(ExitStack())
        expert, gates = alloc(peer, "expert", [P, NT, PICKS], U32), alloc(peer, "gates_sb", [P, NT, PICKS])
        late_x = alloc(peer, "xn_late", [P, 2, D])
        g.picks = Picks(g, peer, a["peer_u"], a["peer_v"], expert, gates, None, SHARES)
        with ExitStack() as front:
            early_x = alloc(front, "xn_early", [P, 2, D])
            g.picks.x = [early_x[:, 0, :], early_x[:, 1, :], late_x[:, 0, :], late_x[:, 1, :]]
            g_ffn = alloc(front, "g_ffn_sb", [P, D])
            keysT, iota = alloc(front, "keysT_sb", [P, PK]), alloc(front, "iota_sb", [P, TOPK])
            pqT = alloc(front, "pqT", [P, PH, S])
            with ExitStack() as s:
                xnT = alloc(s, "xnT", [P, KT, S])
                load_stage(g, "peer", [(g_ffn[:], a["g_ffn"].partition_broadcast(P)), (keysT[:], a["keysT"]), (iota[:], a["iota"])])
                norm_stage(g, "np", [(g.h[:, t, :], P, slice(P * t, P * t + P)) for t in range(NT)], D, outT=xnT,
                           token_out=g.picks.x, gain_rows=g_ffn[:])
                products = [feature_major(g, ("pq", b), j, xnT, slice(0, S)) for b in range(2) for j in range(4)]
                product_stage(g, "pq", products, [pqT[:, h, :] for h in range(PH)], ("pq", 1))
            peer_select_stage(g, "sel0", 0, pqT, keysT, iota[:], expert, gates)
            peer_select_stage(g, "sel1", 1, pqT, keysT, iota[:], expert, gates)
            picks_weight_stage(g)
            peer_select_stage(g, "sel2", 2, pqT, keysT, iota[:], expert, gates)
            peer_select_stage(g, "sel3", 3, pqT, keysT, iota[:], expert, gates)
            picks_weight_stage(g)
            picks_stage(g, "values1")

        with ExitStack() as second:
            uT = alloc(second, "uT", [P, 4, PAD + S])
            kT, kv = alloc(second, "nsa_kT", [HD, 4, S]), alloc(second, "nsa_kv", [P, NT, 512])
            kc = alloc(second, "kc", [P, 2, NG, S])
            k_cmpT, v_cmp = alloc(second, "k_cmpT", [HD, NG, NCMP]), alloc(second, "v_cmp", [NCMP, NG * HD])
            pe_table = alloc(second, "pe_sb", [P, 2, CMP_STRIDE])
            w_pool, w2 = alloc(second, "w_pool_sb", [P, 4, P]), alloc(second, "w2_sb", [P, 2, 2, HD])
            table = alloc(second, "rope_nsa_sb", [P, NT, 2, HD // 2])
            table_cmp = alloc(second, "rope_cmp_sb", [NCMP, 2, HD // 2])
            causal = alloc(second, "causal2_sb", [P, P])
            bias, seen = alloc(second, "cmp_bias_sb", [P, NT, NCMP]), alloc(second, "cmp_seen_sb", [P, NT, NCMP])
            load_stage(g, "nsa", [(pe_table[:], a["pe_table"]), (w2[:, 0], a["w_ck2"].rearrange("(j p) d -> p j d", p=P)),
                                  (w2[:, 1], a["w_cv2"].rearrange("(j p) d -> p j d", p=P)), (table[:], a["rope_nsa"]),
                                  (table_cmp[:], a["rope_cmp"]), (w_pool[:], a["w_pool"].rearrange("g c d -> c g d")),
                                  (causal[:], a["causal"]), (bias[:], a["cmp_bias"]), (seen[:], a["cmp_seen"])])
            assert S // SEL_BLOCK <= N_SEL and WINDOW >= S
            for half, (first_tile, last_tile) in enumerate(HALVES):
                clear_semaphores()
                tiles = range(first_tile, last_tile)
                lo, hi = P * first_tile, P * last_tile
                width = hi - lo
                local = lambda t: slice(P * (t - first_tile), P * (t - first_tile) + P)
                tag = lambda name: f"{name}_{half}"
                with ExitStack() as mixer:
                    h2T, ypT = alloc(mixer, tag("h2T"), [P, KT, width]), alloc(mixer, tag("ypT"), [P, 4, width])
                    o = alloc(mixer, tag("nsa_o"), [P, len(tiles), NH * HD])
                    norm_stage(g, tag("n2"), [(g.h[:, t, :], P, local(t)) for t in tiles], D, outT=h2T,
                               gain_columns=g.gain["norm_mix"])
                    product_stage(g, tag("u"), [feature_major(g, ("u", half), j, h2T, slice(0, width)) for j in range(4)],
                                  [uT[:, j, PAD + lo:PAD + hi] for j in range(4)], ("u", half))
                    with ExitStack() as s:
                        inv_count = alloc(s, tag("inv_count_sb"), [P, 4, S])
                        load_stage(g, tag("pool_in"), [(inv_count[:], a["inv_count"])])
                        pool_stage(g, tag("pool"), uT, (lo, hi), inv_count, w_pool, g.gain["pool_scale"], ypT)
                    with ExitStack() as nsa:
                        qT = alloc(nsa, tag("nsa_qT"), [HD, NH, width])
                        branch_gates = alloc(nsa, tag("branch_gates"), [P, len(tiles), 3 * NH])
                        with ExitStack() as s:
                            q = alloc(s, tag("nsa_q"), [P, len(tiles), NH * HD])
                            products, outputs = [], []
                            for b in range(2):
                                for t in tiles:
                                    products.append(token_major(g, (("q", b), half), t - first_tile, h2T, local(t), P))
                                    outputs.append(q[:, t - first_tile, 512 * b:512 * b + 512])
                            product_stage(g, tag("nq2"), products, outputs, (("q", 1), half))
                            compress_input_stage(g, tag("kc"), h2T, half, pe_table, kc, ("kcvc", half))
                            products, outputs = [], []
                            for t in tiles:
                                products.append(token_major(g, ("kv", half), t - first_tile, h2T, local(t), P))
                                outputs.append(kv[:, t, :])
                            for t in tiles:
                                products.append(token_major(g, ("gn", half), t - first_tile, h2T, local(t), P))
                                outputs.append(branch_gates[:, t - first_tile, :])
                            product_stage(g, tag("nkv2"), products, outputs, ("gn", half),
                                          functions=[None] * len(tiles) + [ACT.Sigmoid] * len(tiles))
                            n_blocks = (hi - CMP_LEN) // CMP_STRIDE + 1
                            compress_stage(g, tag("cmp"), half, n_blocks, kc, w2, table_cmp[0:n_blocks],
                                           k_cmpT[:, :, 0:n_blocks], v_cmp[0:n_blocks, :], ("cv1", half))
                            jobs = []
                            for t in tiles:
                                view = q[:, t - first_tile, :].rearrange("p (h a b) -> p h a b", h=NH, a=2)
                                jobs.append((view, view, table[:, t, :, :]))
                                for c0 in (0, 2 * KVW):
                                    view = kv[:, t, c0:c0 + KVW].rearrange("p (h a b) -> p h a b", h=NG, a=2)
                                    jobs.append((view, view, table[:, t, :, :]))
                            rope_stage(g, tag("nr"), jobs, NH * HD)
                            sources = []
                            for t in tiles:
                                for h0 in range(0, NH, 4):
                                    sources.append(([q[:, t - first_tile, HD * h:HD * h + HD] for h in range(h0, h0 + 4)], P,
                                                    qT[:, h0:h0 + 4, local(t)]))
                            turn_stage(g, tag("tq2"), sources, HD, scale=HD ** -0.5)
                            turn_stage(g, tag("tk2"), [([kv[:, t, c:c + HD] for c in (0, HD, 2 * KVW, 2 * KVW + HD)], P,
                                                        kT[:, :, P * t:P * t + P]) for t in tiles], HD)
                        items = []
                        for t in tiles:
                            for h in range(NH):
                                grp = h // HPG
                                common = dict(q=qT[:, h, local(t)], out=o[:, t - first_tile, HD * h:HD * h + HD])
                                gate = lambda x: branch_gates[:, t - first_tile, 3 * h + x:3 * h + x + 1]
                                items.append(Item(
                                    keys=[(k_cmpT[:, grp, 0:n_blocks], 0)], columns=(0, n_blocks),
                                    biases=[(bias[:, t, 0:n_blocks], 0)],
                                    blocks=[(0, n_blocks, v_cmp[0:n_blocks, HD * grp:HD * grp + HD])],
                                    seen=seen[:, t, 0:n_blocks], gate=gate(0), add=False, **common))
                                for x in range(2):
                                    n = P * (t + 1)
                                    v0 = 2 * KVW * x + KVW + HD * grp
                                    items.append(Item(
                                        keys=[(kT[:, 2 * x + grp, 0:n], 0)], columns=(0, n), biases=[(causal[:], n - P)],
                                        blocks=[(P * m, P, kv[:, m, v0:v0 + HD]) for m in range(t + 1)], seen=None,
                                        gate=gate(1 + x), add=True, **common))
                        attention_stage(g, tag("na"), items, HD)
                    oT = alloc(mixer, tag("nsa_oT"), [P, KT, width])
                    turn_stage(g, tag("to2"), [([o[:, t - first_tile, P * c:P * c + P] for c in range(c0, c0 + 4)], P,
                                                oT[:, c0:c0 + 4, local(t)]) for t in tiles for c0 in (0, 4)], P)
                    mergedT = alloc(mixer, tag("mergedT2"), [P, KT, width])
                    merge_stage(g, tag("m2"), ("ga", "yp", "gb", "yn"), h2T, slice(0, width), (ypT, oT), mergedT,
                                (("yn", 1), half), half)
                    residual_stage(g, tag("out"), [(("out", 0), half), (("out", 1), half)], mergedT, (first_tile, last_tile),
                                   (("out", 1), half))
                if half == 0:
                    picks_weight_stage(g)
                with ExitStack() as mlp:
                    aT = alloc(mlp, tag("aT"), [P, D_FF // P, width])
                    with ExitStack() as s:
                        h3T = alloc(s, tag("h3T"), [P, KT, width])
                        norm_stage(g, tag("n3"), [(g.h[:, t, :], P, local(t)) for t in tiles], D, outT=h3T,
                                   gain_columns=g.gain["norm_mlp"])
                        mlp_up_stage(g, tag("ff1"), half, h3T, aT, (("ff1", D_FF // 512 - 1), half))
                    mlp_down_stage(g, tag("ff2"), half, aT, (("ff2", 1, 3), half))
        with ExitStack() as s:
            final, g_final = alloc(s, "final", [P, NT, D]), alloc(s, "g_final", [P, D])
            load_stage(g, "final", [(g_final[:], a["norm_final"].partition_broadcast(P))])
            norm_stage(g, "nf", [(g.h[:, t, :], P, None) for t in range(NT)], D,
                       token_out=[final[:, t, :] for t in range(NT)], gain_rows=g_final[:],
                       store=a["out"].rearrange("(t p) d -> p t d", p=P))


def arrays(inputs):
    def columns(v):
        return v.reshape(-1, P).T

    one = {k: np.asarray(v)[0] for k, v in inputs.items() if k not in ("meta_tokens", "norm_final_2")}
    w2 = one["w_in_2"]
    kc_vc = w2[:, E_KC:E_KS].reshape(D, 2 * NG, 1, HD)
    first_w = lambda w: w.reshape(2, CMP_STRIDE, HD, CMP_HID).transpose(0, 2, 1, 3).reshape(P, CMP_STRIDE, CMP_HID)
    pe = lambda x: x.reshape(2, CMP_STRIDE, HD).transpose(0, 2, 1).reshape(P, CMP_STRIDE)
    out = {
        "x": one["x"], "meta_tokens": np.asarray(inputs["meta_tokens"]),
        "g_mix": columns(one["g_mix"]), "g_q_lora": columns(one["g_q_lora"]), "g_kv_lora": columns(one["g_kv_lora"]),
        "g_ret_gn": columns(one["g_ret_gn"]), "norm_mix": columns(one["norm_mix_2"]),
        "norm_mlp": columns(one["norm_mlp_2"]), "pool_scale": columns(one["pool_scale_2"]),
        "g_qk_q": one["g_qk_q"], "g_qk_k": one["g_qk_k"], "g_ffn": one["g_ffn"], "norm_final": np.asarray(inputs["norm_final_2"]),
        "w_in": one["w_in"], "w_uq": one["w_uq"], "w_ukv": one["w_ukv"], "w_mla_out": one["w_mla_out"],
        "w_ret_out": one["w_ret_out"], "w_mix_out": one["w_mix_out"], "w_peer_q": one["w_peer_q"],
        "keysT": np.concatenate([one["peer_keys_1"].T, one["peer_keys_2"].T]),
        "peer_u": one["peer_u"], "peer_v": one["peer_v"],
        "w_in2": w2, "w_kcvc": np.broadcast_to(kc_vc, (D, 2 * NG, 2, HD)).reshape(D, 4 * P),
        "w_ck1": first_w(one["w_ck1_2"]), "w_cv1": first_w(one["w_cv1_2"]), "w_ck2": one["w_ck2_2"], "w_cv2": one["w_cv2_2"],
        "pe_table": np.stack([pe(one["pe_k_2"]), pe(one["pe_v_2"])], 1),
        "w_pool": one["w_pool_2"], "w_proj_pool": one["w_proj_pool_2"], "w_proj_nsa": one["w_proj_nsa_2"],
        "w_out": one["w_out_2"], "w_ff1": one["w_ff1_2"], "w_ff2": one["w_ff2_2"],
    }
    return {k: np.ascontiguousarray(v) for k, v in out.items()} | constants()


def kernel(**inputs):
    import concourse.bacc as bacc
    from concourse.bass_utils import run_bass_kernel_spmd

    nc = bacc.Bacc("TRN2", target_bir_lowering=False, num_devices=1)
    data = arrays(inputs)
    views = {k: nc.dram_tensor(f"{k}_dram", v.shape, mybir.dt.from_np(v.dtype), kind="ExternalInput").ap()
             for k, v in data.items()}
    views["out"] = nc.dram_tensor("out_dram", (S, D), F32, kind="ExternalOutput").ap()
    build(nc, views)
    r = run_bass_kernel_spmd(nc, [{f"{k}_dram": v for k, v in data.items()}], core_ids=[0])
    return r.results[0]["out_dram"].reshape(1, S, D)
```

```python
from contextlib import ExitStack

import numpy as np

import concourse.bass as bass
from concourse import mybir

F32 = mybir.dt.float32
U32 = mybir.dt.uint32
ALU = mybir.AluOpType
ACT = mybir.ActivationFunctionType
AX_X = mybir.AxisListType.X

P = 128
D = 1024
S = 512
NT = S // P
META = 16
L = META + S
KT = D // P
EPS = 1e-6
NEG = -1e30
LOWEST = -3.0e38

Q_LORA, KV_LORA, MH, NOPE, MROPE, MV = 384, 256, 8, 64, 32, 64
QK = NOPE + MROPE
RH, RDK, RDV = 8, 64, 128
PH, PK, TOPK = 8, 128, 16
PICKS = PH * TOPK
C_Q, C_KV, C_RQ, C_RK = 0, Q_LORA, Q_LORA + KV_LORA + MROPE, Q_LORA + KV_LORA + MROPE + RH * RDK
C_RV = C_RK + RH * RDK
C_RG = C_RV + RH * RDV
C_ZA = C_RG + RH * RDV
C_ZR = C_ZA + D

STARTS = ((0, 1), (1, NT))
HALVES = ((0, NT // 2), (NT // 2, NT))

POOL_W, WINDOWS = 512, (2, 4, 8, 16)
NH, HD, NG = 16, 64, 2
HPG = NH // NG
KVW = NG * HD
CMP_LEN, CMP_STRIDE, CMP_HID = 32, 16, 256
NCMP = S // CMP_STRIDE - CMP_LEN // CMP_STRIDE + 1
WINDOW, SEL_BLOCK, N_SEL = 512, 64, 16
D_FF = 4 * D
E_Q = POOL_W
E_KC = E_Q + NH * HD
E_KS = E_KC + 2 * KVW
E_GN = E_KS + 4 * KVW
E_GM = E_GN + 3 * NH

RING = 3
SLAB = KT * 512
BANKS = 8
SHARES = {"to_1": 2, "m1_1": 126, "mix_1": 36, "np_1": 12, "pq_1": 30, "sel1": 50, "sel2": 128, "sel3": 128,
          "n2_0": 9, "u_0": 12, "pool_0": 10, "nq2_0": 22, "kc_0": 14, "nkv2_0": 20, "cmp_0": 30, "tq2_0": 6,
          "tk2_0": 3, "na_0": 216, "to2_0": 4, "m2_0": 50, "out_0": 16, "n3_0": 4, "ff1_0": 46, "ff2_0": 50}
GATHERS = 8
PAD = 16


def constants():
    def rope(pos, half):
        inv = (10000.0 ** (-np.arange(half, dtype=np.float32) / half)).astype(np.float32)
        ang = (np.asarray(pos, np.float32)[:, None] * inv[None]).astype(np.float32)
        return np.stack([np.cos(ang), np.sin(ang)], 1).astype(np.float32)

    def tiles(a, tiles_with_meta):
        out = np.zeros((P, NT + tiles_with_meta) + a.shape[1:], np.float32)
        if tiles_with_meta:
            out[:META, 0] = a[:META]
            a = a[META:]
        out[:, tiles_with_meta:] = a.reshape((NT, P) + a.shape[1:]).swapaxes(0, 1)
        return out

    r = np.arange(P)
    gamma = 1.0 - 2.0 ** (-5.0 - np.arange(RH))
    steps = np.arange(L)[None, :] - r[:, None]
    decay = np.where(steps[:, None] >= 0, gamma[None, :, None] ** np.maximum(steps, 0)[:, None] * RDK ** -0.5, 0.0)
    t = np.arange(S)
    ends = np.arange(NCMP) * CMP_STRIDE + CMP_LEN - 1
    seen = (ends[None] <= t[:, None]).astype(np.float32)
    counts = np.stack([1.0 / np.minimum(np.arange(PAD) + 1, w) for w in WINDOWS])
    c = {
        "identity": np.eye(P),
        "rope_mla": tiles(rope(np.arange(L), MROPE // 2), 1),
        "rope_ret": tiles(rope(np.arange(L), RDK // 2), 1),
        "rope_nsa": tiles(rope(t, HD // 2), 0),
        "rope_cmp": rope(ends, HD // 2),
        "decay": decay,
        "causal": np.where(r[None, :] <= r[:, None], 0.0, NEG),
        "cmp_bias": tiles(np.where(seen > 0, 0.0, NEG), 0),
        "cmp_seen": tiles(seen, 0),
        "inv_count": np.broadcast_to(counts[None], (P,) + counts.shape),
        "iota": np.broadcast_to(np.arange(TOPK)[None], (P, TOPK)),
    }
    return {k: np.ascontiguousarray(v, dtype=np.float32) for k, v in c.items()}


class Core:

    def __init__(self, nc):
        self.nc = nc
        self.w = self.picks = self.psum = self.h = self.identity = self.gain = self.semaphore = None


class Item:

    def __init__(self, q, keys, columns, biases, blocks, seen, gates, out, add):
        self.q, self.keys, self.columns, self.biases = q, keys, columns, biases
        self.blocks, self.seen, self.gates, self.out, self.add = blocks, seen, gates, out, add


def linker(eng, sem):
    count = [0]

    def link(ins):
        count[0] += 1
        ins.then_inc(sem, 1)
        eng.wait_ge(sem, count[0])
    return link


def weight_plan(a):
    def cols(w, c0, n, kt=KT, k0=0):
        return w.rearrange("(k p) n -> p k n", p=P)[:, k0:k0 + kt, c0:c0 + n]

    plan = [("cq", cols(a["w_in"], C_Q, Q_LORA), NT), ("ckv", cols(a["w_in"], C_KV, KV_LORA + MROPE), NT + 1)]
    plan += [(("uq", b), cols(a["w_uq"], 384 * b, 384, 3), NT) for b in range(2)]
    plan += [(("ukv", b), cols(a["w_ukv"], 512 * b, 512, 2), NT + 1) for b in range(2)]
    plan += [(("rg", b), cols(a["w_in"], C_RG + 512 * b, 512), 4) for b in range(2)]
    plan += [("rq", cols(a["w_in"], C_RQ, 512), NT), ("rk", cols(a["w_in"], C_RK, 512), NT + 1)]
    plan += [(("rv", b), cols(a["w_in"], C_RV + 512 * b, 512), NT + 1) for b in range(2)]
    for run in range(len(STARTS)):
        n = STARTS[run][1] - STARTS[run][0]
        late = []
        for b in range(2):
            late += [(("za", b), cols(a["w_in"], C_ZA + 512 * b, 512), 4), (("ya", b), cols(a["w_mla_out"], 512 * b, 512, 4), 4),
                     (("zr", b), cols(a["w_in"], C_ZR + 512 * b, 512), 4), (("yr", b), cols(a["w_ret_out"], 512 * b, 512), 4)]
        late += [(("mix", b), cols(a["w_mix_out"], 512 * b, 512), n) for b in range(2)]
        late += [(("pq", b), cols(a["w_peer_q"], 512 * b, 512), 4) for b in range(2)]
        plan += [((name, run), view, products) for name, view, products in late]
    for half in range(len(HALVES)):
        n = HALVES[half][1] - HALVES[half][0]
        second = [("u", cols(a["w_in2"], 0, 512), 4)]
        second += [(("q", b), cols(a["w_in2"], E_Q + 512 * b, 512), n) for b in range(2)]
        second += [("kcvc", a["w_kcvc"].rearrange("(k p) n -> p k n", p=P), 4), ("kv", cols(a["w_in2"], E_KS, 512), n),
                   ("gn", cols(a["w_in2"], E_GN, 3 * NH), n)]
        second += [("ck1", a["w_ck1"], 2), ("cv1", a["w_cv1"], 2)]
        for b in range(2):
            second += [(("ga", b), cols(a["w_in2"], E_GM + 512 * b, 512), 4), (("yp", b), cols(a["w_proj_pool"], 512 * b, 512, 4), 4),
                       (("gb", b), cols(a["w_in2"], E_GM + D + 512 * b, 512), 4), (("yn", b), cols(a["w_proj_nsa"], 512 * b, 512), 4)]
        second += [(("out", b), cols(a["w_out"], 512 * b, 512), n) for b in range(2)]
        second += [(("ff1", b), cols(a["w_ff1"], 512 * b, 512), 4) for b in range(D_FF // 512)]
        second += [(("ff2", b, k), cols(a["w_ff2"], 512 * b, 512, KT, KT * k), n) for b in range(2) for k in range(4)]
        plan += [((name, half), view, products) for name, view, products in second]
    return plan


class Weights:

    def __init__(self, nc, ctx, plan):
        self.nc, self.plan = nc, plan
        self.ring = ctx.enter_context(nc.sbuf_tensor("weight_ring", [P, RING, SLAB], F32))
        self.landed = [ctx.enter_context(nc.semaphore(f"slab_landed{r}")) for r in range(RING)]
        self.products_done = ctx.enter_context(nc.semaphore("products_done"))
        self.number = {name: i for i, (name, _, _) in enumerate(plan)}
        self.products = [0]
        for _, _, n in plan:
            self.products.append(self.products[-1] + n)
        self.loaded = 0

    def view(self, name):
        i = self.number[name]
        _, kt, n = self.plan[i][1].shape
        return self.ring[:, i % RING, 0:kt * n].rearrange("p (k n) -> p k n", k=kt)

    def load_through(self, sp, name):
        last = -1 if name is None else self.number[name]
        while self.loaded < min(last + 1 + RING, len(self.plan)):
            i = self.loaded
            if i >= RING:
                sp.wait_ge(self.products_done, self.products[i - RING + 1])
            sp.dma_start(self.view(self.plan[i][0]), self.plan[i][1]).then_inc(self.landed[i % RING], 16)
            self.loaded += 1

    def arrived(self, pe, name):
        i = self.number[name]
        pe.wait_ge(self.landed[i % RING], 16 * (i // RING + 1))

    def product(self, name, j):
        return self.products[self.number[name]] + j + 1


class Picks:

    def __init__(self, g, ctx, peer_u, peer_v, expert, gates, shares):
        nc, self.g = g.nc, g
        sb = lambda name, shape: ctx.enter_context(nc.sbuf_tensor(f"picks_{name}", shape, F32))
        self.expert, self.gates, self.x, self.shares = expert, gates, None, shares
        self.rows = sb("rows", [P, GATHERS, D])
        self.product = sb("product", [P, D])
        self.dots, self.active, self.weight = (sb(x, [P, PICKS]) for x in ("dots", "active", "weight"))
        self.landed = [ctx.enter_context(nc.semaphore(f"picks_landed{r}")) for r in range(GATHERS)]
        self.rows_used = ctx.enter_context(nc.semaphore("picks_rows_used"))
        self.steps = [(t, table, k) for t in range(NT) for table in (peer_u, peer_v) for k in range(PICKS)]
        self.peer_u = peer_u
        assert sum(shares.values()) == len(self.steps)
        self.issued = self.used = self.first = self.last = 0
        self.known = 0
        self.turn = self.turns = 0
        self.weights = 0
        self.active_ready = ctx.enter_context(nc.semaphore("picks_active_ready"))
        self.weight_ready = ctx.enter_context(nc.semaphore("picks_weight_ready"))

    def share(self, tag, turns):
        self.first, self.last = self.last, self.last + self.shares.get(tag, 0)
        self.turn, self.turns = 0, turns

    def issue(self, pool):
        if self.last == self.first:
            return
        while self.issued < min(self.last + GATHERS, self.known):
            n = self.issued
            t, table, k = self.steps[n]
            if n >= GATHERS:
                pool.wait_ge(self.rows_used, n - GATHERS + 1)
            pool.indirect_dma_start(
                out=self.rows[:, n % GATHERS, :], out_offset=None, in_=table,
                in_offset=bass.IndirectOffsetOnAxis(ap=self.expert[:, t, k:k + 1], axis=0),
            ).then_inc(self.landed[n % GATHERS], 16)
            self.issued += 1

    def after(self, turn):
        return self.first + (self.last - self.first) * min(turn, self.turns) // self.turns

    def activate(self, act, turn=None):
        for t in range(NT):
            dots_end = (2 * t + 1) * PICKS
            if (turn is None and self.last == dots_end) or (
                    turn is not None and self.after(turn - 1) < dots_end <= self.after(turn)):
                act.wait_ge(self.rows_used, dots_end)
                self.g.nc.scalar.activation(self.active[:], self.dots[:], ACT.Gelu).then_inc(self.active_ready, 1)

    def make_weights(self, dve, t):
        dve.wait_ge(self.active_ready, t + 1)
        if t:
            dve.wait_ge(self.rows_used, 2 * t * PICKS)
        self.g.nc.vector.tensor_tensor(self.weight[:], self.active[:], self.gates[:, t, :],
                                       ALU.mult).then_inc(self.weight_ready, 1)
        dve.wait_ge(self.weight_ready, t + 1)
        self.weights = t + 1

    def use(self, dve):
        nc = self.g.nc
        self.turn += 1
        while self.used < self.after(self.turn):
            n = self.used
            t, table, k = self.steps[n]
            if table is not self.peer_u and self.weights == t:
                self.make_weights(dve, t)
            row = self.rows[:, n % GATHERS, :]
            dve.wait_ge(self.landed[n % GATHERS], 16 * (n // GATHERS + 1))
            if n:
                dve.wait_ge(self.rows_used, n)
            if table is self.peer_u:
                ins = nc.vector.tensor_tensor_reduce(out=self.product[:], in0=row, in1=self.x[t], scale=1.0, scalar=0.0,
                                                     op0=ALU.mult, op1=ALU.add, accum_out=self.dots[:, k:k + 1])
            else:
                h = self.g.h[:, t, :]
                ins = nc.vector.scalar_tensor_tensor(out=h, in0=row, scalar=self.weight[:, k:k + 1], in1=h, op0=ALU.mult,
                                                     op1=ALU.add)
            ins.then_inc(self.rows_used, 1)
            self.used += 1


def row_tile(t):
    return (META, slice(0, META)) if t == 0 else (P, slice(META + P * (t - 1), META + P * t))


def evacuations(owners, n):
    return owners[:n + 1].count(owners[n])


def token_major(g, name, t, xT, columns, rows):
    w = g.w.view(name)
    return (name, t, rows, w.shape[2], [(xT[:, k, columns], w[:, k, :]) for k in range(w.shape[1])])


def feature_major(g, name, j, xT, columns):
    w = g.w.view(name)
    return (name, j, P, columns.stop - columns.start,
            [(w[:, k, P * j:P * j + P], xT[:, k, columns]) for k in range(w.shape[1])])


def multiply(g, pe, products, owners, drained):
    for n, (name, j, rows, cols, pairs) in enumerate(products):
        if j == 0:
            g.w.arrived(pe, name)
        if n >= BANKS:
            pe.wait_ge(drained[owners[n - BANKS]], evacuations(owners, n - BANKS))
        for k, (lhsT, rhs) in enumerate(pairs):
            mm = g.nc.tensor.matmul(g.psum[0:rows, n % BANKS, 0:cols], lhsT, rhs, start=(k == 0),
                                    stop=(k == len(pairs) - 1))
        mm.then_inc(g.w.products_done, 1)


def product_stage(g, tag, products, outputs, last_slab, functions=None, ropes=None, loads=()):
    nc = g.nc
    functions = functions or [None] * len(products)
    owners = ["act" if functions[n] or ropes or n % 2 else "dve" for n in range(len(products))]
    with ExitStack() as ctx:
        drained = {e: g.semaphore(f"{tag}_drained_{e}") for e in ("act", "dve")}
        s_link, s_loaded = g.semaphore(f"{tag}_link"), g.semaphore(f"{tag}_loaded")
        if ropes:
            width = max(int(np.prod(src.shape[1:])) for _, (_, src, _) in ropes)
            tmp = [ctx.enter_context(nc.sbuf_tensor(f"{tag}_tmp{i}", [P, width], F32)) for i in range(2)]
        g.picks.share(tag, len(products))
        block = ctx.enter_context(nc.Block())

        def parts(n):
            _, _, rows, cols, _ = products[n]
            if isinstance(outputs[n], list):
                return [(out, part(g.psum[0:rows, n % BANKS, 0:cols])) for out, part in outputs[n]]
            return [(outputs[n], g.psum[0:rows, n % BANKS, 0:cols])]

        @block.gpsimd
        def _(pool):
            g.picks.issue(pool)

        @block.sync
        def _(sp):
            for dst, src in loads:
                sp.dma_start(dst, src).then_inc(s_loaded, 16)
            g.w.load_through(sp, last_slab)
            if loads:
                sp.wait_ge(s_loaded, 16 * len(loads))

        @block.tensor
        def _(pe):
            multiply(g, pe, products, owners, drained)

        @block.scalar
        def _(act):
            for n, (name, j, _, _, _) in enumerate(products):
                if owners[n] == "act":
                    act.wait_ge(g.w.products_done, g.w.product(name, j))
                    for out, src in parts(n):
                        ins = nc.scalar.activation(out, src, functions[n] or ACT.Copy)
                    ins.then_inc(drained["act"], 1)

        @block.vector
        def _(dve):
            link = linker(dve, s_link)
            for n, (name, j, _, _, _) in enumerate(products):
                if owners[n] == "dve":
                    dve.wait_ge(g.w.products_done, g.w.product(name, j))
                    for out, src in parts(n):
                        ins = nc.vector.tensor_copy(out, src)
                    ins.then_inc(drained["dve"], 1)
                for number, (dst, src, table) in ropes or ():
                    if number == n:
                        dve.wait_ge(drained["act"], n + 1)
                        rope(nc, link, dst, src, table, tmp)
                g.picks.use(dve)


def residual_stage(g, tag, names, xT, tiles, last_slab):
    nc = g.nc
    n_tiles = tiles[1] - tiles[0]
    products = [token_major(g, names[b], t, xT, slice(P * t, P * t + P), P) for b in range(2) for t in range(n_tiles)]
    with ExitStack() as ctx:
        drained = {"dve": g.semaphore(f"{tag}_drained")}
        g.picks.share(tag, len(products))
        block = ctx.enter_context(nc.Block())

        @block.gpsimd
        def _(pool):
            g.picks.issue(pool)

        @block.sync
        def _(sp):
            g.w.load_through(sp, last_slab)

        @block.tensor
        def _(pe):
            multiply(g, pe, products, ["dve"] * len(products), drained)

        @block.vector
        def _(dve):
            for n, (name, t, rows, cols, _) in enumerate(products):
                b = n // n_tiles
                h = g.h[:, tiles[0] + t, 512 * b:512 * b + 512]
                g.picks.use(dve)
                dve.wait_ge(g.w.products_done, g.w.product(name, t))
                nc.vector.tensor_tensor(h, h, g.psum[:, n % BANKS, :], ALU.add).then_inc(drained["dve"], 1)


def norm_stage(g, tag, sources, width, outT=None, gain_columns=None, token_out=None, gain_rows=None, loads=None,
               store=None):
    nc = g.nc
    n, chunks = len(sources), width // P
    with ExitStack() as ctx:
        sb = lambda name, shape: ctx.enter_context(nc.sbuf_tensor(f"{tag}_{name}", shape, F32))
        sem = lambda name: g.semaphore(f"{tag}_{name}")
        junk = sb("squares", [P, width])
        sums, mean, root, inverse = (sb(x, [P, n]) for x in ("sums", "mean", "root", "inverse"))
        scaled = None if token_out is not None else sb("scaled", [P, 2, width])
        s_in, s_zero, s_sq, s_mean, s_root, s_inv = (sem(x) for x in ("in", "zero", "sq", "mean_ready", "root_ready", "inv"))
        s_scaled, s_turned, s_drained, s_out = (sem(x) for x in ("scaled_ready", "turned", "drained", "out"))
        n_loads = len(loads) if loads else 0
        g.picks.share(tag, n)
        block = ctx.enter_context(nc.Block())

        @block.gpsimd
        def _(pool):
            g.picks.issue(pool)

        def buffer(t):
            return token_out[t] if token_out is not None else scaled[:, t % 2, :]

        @block.sync
        def _(sp):
            for dst, src in loads or ():
                sp.dma_start(dst, src).then_inc(s_in, 16)
            if loads:
                g.w.load_through(sp, None)
            if store is not None:
                for t in range(n):
                    sp.wait_ge(s_scaled, t + 1)
                    sp.dma_start(store[:, t, :], token_out[t]).then_inc(s_out, 16)
                sp.wait_ge(s_out, 16 * n)

        @block.scalar
        def _(act):
            act.wait_ge(s_zero, 1)
            if loads:
                act.wait_ge(s_in, 16 * n_loads)
            for t, (src, rows, _) in enumerate(sources):
                if t:
                    act.wait_ge(s_sq, t)
                nc.scalar.activation(junk[0:rows], src, ACT.Square, accum_out=sums[0:rows, t:t + 1]).then_inc(s_sq, 1)
            act.wait_ge(s_mean, 1)
            nc.scalar.activation(root[:], mean[:], ACT.Sqrt).then_inc(s_root, 1)

        def drain(dve, t):
            _, rows, columns = sources[t]
            dve.wait_ge(s_turned, t + 1)
            for c in range(0, chunks, 4):
                m = min(4, chunks - c)
                src = g.psum[:, 2 * (t % 2) + c // 4, :].rearrange("p (c r) -> p c r", c=4)[:, 0:m, 0:rows]
                if gain_columns is None:
                    ins = nc.vector.tensor_copy(outT[:, c:c + m, columns], src)
                else:
                    ins = nc.vector.tensor_tensor(outT[:, c:c + m, columns], src,
                                                  gain_columns[:, c:c + m].unsqueeze(2).to_broadcast([P, m, rows]), ALU.mult)
            ins.then_inc(s_drained, 1)

        @block.vector
        def _(dve):
            nc.vector.memset(sums[:], 1.0).then_inc(s_zero, 1)
            dve.wait_ge(s_sq, n)
            nc.vector.tensor_scalar(mean[:], sums[:], 1.0 / width, EPS, ALU.mult, ALU.add).then_inc(s_mean, 1)
            dve.wait_ge(s_root, 1)
            nc.vector.reciprocal(inverse[:], root[:]).then_inc(s_inv, 1)
            dve.wait_ge(s_inv, 1)
            for t, (src, rows, _) in enumerate(sources):
                g.picks.use(dve)
                if token_out is not None:
                    nc.vector.scalar_tensor_tensor(out=buffer(t)[0:rows], in0=src, scalar=inverse[0:rows, t:t + 1],
                                                   in1=gain_rows, op0=ALU.mult, op1=ALU.mult).then_inc(s_scaled, 1)
                else:
                    if t >= 2:
                        dve.wait_ge(s_turned, t - 1)
                    nc.vector.tensor_scalar(buffer(t)[0:rows], src, inverse[0:rows, t:t + 1], None,
                                            ALU.mult).then_inc(s_scaled, 1)
                if outT is not None and t >= 1:
                    drain(dve, t - 1)
            if outT is not None:
                drain(dve, n - 1)

        if outT is not None:
            @block.tensor
            def _(pe):
                for t, (_, rows, _) in enumerate(sources):
                    pe.wait_ge(s_scaled, t + 1)
                    if t >= 2:
                        pe.wait_ge(s_drained, t - 1)
                    for c in range(chunks):
                        mm = nc.tensor.transpose(g.psum[:, 2 * (t % 2) + c // 4, P * (c % 4):P * (c % 4) + rows],
                                                 buffer(t)[0:rows, P * c:P * c + P], g.identity[0:rows, 0:rows])
                    mm.then_inc(s_turned, 1)


def turn_stage(g, tag, sources, rows_out, scale=1.0):
    nc = g.nc
    with ExitStack() as ctx:
        s_turned = g.semaphore(f"{tag}_turned")
        s_drained = [g.semaphore(f"{tag}_drained{e}") for e in range(2)]
        g.picks.share(tag, len(sources))
        block = ctx.enter_context(nc.Block())

        @block.gpsimd
        def _(pool):
            g.picks.issue(pool)

        def bank(n, m, rows):
            return g.psum[0:rows_out, n % BANKS, :].rearrange("p (c r) -> p c r", c=4)[:, 0:m, 0:rows]

        @block.tensor
        def _(pe):
            for n, (blocks, rows, _) in enumerate(sources):
                if n >= BANKS:
                    pe.wait_ge(s_drained[n % 2], (n - BANKS) // 2 + 1)
                for c, src in enumerate(blocks):
                    mm = nc.tensor.transpose(g.psum[0:rows_out, n % BANKS, P * c:P * c + rows], src,
                                             g.identity[0:rows, 0:rows])
                mm.then_inc(s_turned, 1)

        @block.scalar
        def _(act):
            for n, (blocks, rows, dst) in enumerate(sources):
                if n % 2 == 0:
                    act.wait_ge(s_turned, n + 1)
                    nc.scalar.activation(dst, bank(n, len(blocks), rows), ACT.Copy, scale=scale).then_inc(s_drained[0], 1)

        @block.vector
        def _(dve):
            for n, (blocks, rows, dst) in enumerate(sources):
                if n % 2 == 1:
                    dve.wait_ge(s_turned, n + 1)
                    nc.vector.tensor_scalar(dst, bank(n, len(blocks), rows), scale, None, ALU.mult).then_inc(s_drained[1], 1)
                g.picks.use(dve)


def rope(nc, link, dst, src, table, tmp):
    shape = list(src.shape)
    rows, heads, _, half = shape
    tmp = [x[0:rows, 0:heads * 2 * half].rearrange("p (h a b) -> p h a b", h=heads, a=2) for x in tmp]
    cos = table[:, 0, :].unsqueeze(1).unsqueeze(1).to_broadcast(shape)
    sin = table[:, 1, :].unsqueeze(1).unsqueeze(1).to_broadcast(shape)
    nc.vector.tensor_tensor(tmp[0], src, cos, ALU.mult)
    link(nc.vector.tensor_tensor(tmp[1], src, sin, ALU.mult))
    nc.vector.tensor_tensor(dst[:, :, 0, :], tmp[0][:, :, 0, :], tmp[1][:, :, 1, :], ALU.subtract)
    link(nc.vector.tensor_tensor(dst[:, :, 1, :], tmp[1][:, :, 0, :], tmp[0][:, :, 1, :], ALU.add))


def mla_qk_stage(g, q, k, k_pe, q_gain, k_gain, rope_table, hnT, gateT, last_slab):
    nc = g.nc
    products = [feature_major(g, ("rg", b), j, hnT, slice(META, L)) for b in range(2) for j in range(4)]
    assert len(products) <= BANKS
    with ExitStack() as ctx:
        sb = lambda name, shape: ctx.enter_context(nc.sbuf_tensor(f"mla_{name}", shape, F32))
        sem = lambda name: g.semaphore(f"mla_{name}")
        n = 2 * NT + 1
        squares = sb("head_squares", [P, MH, QK])
        sums, mean, root, inverse = (sb(x, [P, n, MH]) for x in ("head_sums", "head_mean", "head_root", "head_inverse"))
        tmp = [sb(f"rope_tmp{i}", [P, MH * MROPE]) for i in range(2)]
        s_link, s_mean, s_root = sem("qk_link"), sem("qk_mean"), sem("qk_root")
        block = ctx.enter_context(nc.Block())
        units = []
        for t in range(NT):
            x = q[:, t, :].rearrange("p (h d) -> p h d", h=MH)
            units.append((x, x[:, :, NOPE:QK], q_gain, t + 1))
        for t in range(NT + 1):
            rows, _ = row_tile(t)
            pe_part = k_pe[0:rows, t, :].unsqueeze(1).to_broadcast([rows, MH, MROPE])
            units.append((k[0:rows, t, :].rearrange("p (h d) -> p h d", h=MH), pe_part, k_gain, t))

        @block.sync
        def _(sp):
            g.w.load_through(sp, last_slab)

        @block.tensor
        def _(pe):
            multiply(g, pe, products, None, None)

        @block.scalar
        def _(act):
            act.wait_ge(s_mean, 1)
            nc.scalar.activation(root[:], mean[:], ACT.Sqrt).then_inc(s_root, 1)
            for i, (name, j, _, _, _) in enumerate(products):
                act.wait_ge(g.w.products_done, g.w.product(name, j))
                nc.scalar.activation(gateT[:, i, :], g.psum[:, i, :], ACT.Silu)

        @block.vector
        def _(dve):
            link = linker(dve, s_link)
            link(nc.vector.memset(sums[:], 1.0))
            for i, (x, roped, _, _) in enumerate(units):
                rows, nope = x.shape[0], x[:, :, 0:NOPE]
                nc.vector.tensor_tensor(squares[0:rows, :, 0:NOPE], nope, nope, ALU.mult)
                link(nc.vector.tensor_tensor(squares[0:rows, :, NOPE:QK], roped, roped, ALU.mult))
                link(nc.vector.tensor_reduce(sums[0:rows, i, :], squares[0:rows], AX_X, ALU.add))
            nc.vector.tensor_scalar(mean[:], sums[:], 1.0 / QK, EPS, ALU.mult, ALU.add).then_inc(s_mean, 1)
            dve.wait_ge(s_root, 1)
            link(nc.vector.reciprocal(inverse[:], root[:]))
            for i, (x, roped, gain, t) in enumerate(units):
                rows = x.shape[0]
                scale = inverse[0:rows, i, :].unsqueeze(2)
                nc.vector.tensor_tensor(x[:, :, 0:NOPE], x[:, :, 0:NOPE], scale.to_broadcast([rows, MH, NOPE]), ALU.mult)
                link(nc.vector.tensor_tensor(x[:, :, NOPE:QK], roped, scale.to_broadcast([rows, MH, MROPE]), ALU.mult))
                link(nc.vector.tensor_tensor(x, x, gain[0:rows].unsqueeze(1).to_broadcast([rows, MH, QK]), ALU.mult))
                y = x[:, :, NOPE:QK].rearrange("p h (a b) -> p h a b", a=2)
                rope(nc, link, y, y, rope_table[0:rows, t, :, :], tmp)


def attention_stage(g, tag, items, head_dim, group, buffers=None):
    nc = g.nc
    n_items = len(items)
    widest = max(it.columns[1] for it in items)
    depth = 4 if widest <= 512 else 2
    lag, late = (3, 5) if depth == 4 else (1, 2)
    score_width = 4 * 512 // depth
    ring = 4 * group
    assert n_items % group == 0
    with ExitStack() as ctx:
        sb = lambda name, shape: ctx.enter_context(nc.sbuf_tensor(f"{tag}_{name}", shape, F32))
        sem = lambda name: g.semaphore(f"{tag}_{name}")
        probs, probsT = buffers or (sb("probs", [P, depth, widest]), sb("probsT", [P, 2, (widest + P - 1) // P * P]))
        negmax, rowsum, factor = sb("negmax", [P, 4]), sb("rowsum", [P, ring]), sb("factor", [P, ring])
        s_scores, s_max, s_exp, s_seen, s_turned, s_copied = (
            sem(x) for x in ("scores", "max", "exp", "seen_done", "turned", "copied"))
        s_values, s_out, s_link = sem("values"), sem("out_done"), sem("link")
        g.picks.share(tag, n_items)
        block = ctx.enter_context(nc.Block())

        @block.gpsimd
        def _(pool):
            g.picks.issue(pool)
        with_mask = [it.seen is not None for it in items]

        def scores(i):
            at = (i % depth) * score_width
            return g.psum[:, 0:4, :].rearrange("p a b -> p (a b)")[:, at:at + score_width]

        def turned(i, m, keys):
            if m < 4:
                return g.psum[0:keys, 4 + i % 2, P * m:P * m + P]
            return g.psum[0:keys, 6 + i % 2, P:2 * P]

        def values(i):
            return g.psum[:, 6 + i % 2, 0:head_dim]

        @block.sync
        def _(sp):
            g.w.load_through(sp, None)

        @block.tensor
        def _(pe):
            for i in range(n_items + late):
                if i < n_items:
                    it = items[i]
                    if i >= depth:
                        pe.wait_ge(s_exp, i - depth + 1)
                    for (kT, col) in it.keys:
                        mine = [(b, c) for b, c in it.biases if col <= c < col + kT.shape[1]]
                        mm = nc.tensor.matmul(scores(i)[:, col:col + kT.shape[1]], it.q, kT, start=True, stop=not mine)
                        for b, c in mine:
                            mm = nc.tensor.matmul(scores(i)[:, c:c + b.shape[1]], g.identity[:], b, start=False, stop=True)
                    mm.then_inc(s_scores, 1)
                if i >= late:
                    j, it = i - late, items[i - late]
                    pe.wait_ge(s_copied, j + 1)
                    if j >= 2:
                        pe.wait_ge(s_out, j - 1)
                    for m, (_, keys, v) in enumerate(it.blocks):
                        mm = nc.tensor.matmul(values(j), probsT[0:keys, j % 2, P * m:P * m + P], v, start=(m == 0),
                                              stop=(m == len(it.blocks) - 1))
                    mm.then_inc(s_values, 1)
                if lag <= i < n_items + lag:
                    j, it = i - lag, items[i - lag]
                    pe.wait_ge(s_exp, j + 1)
                    if it.seen is not None:
                        pe.wait_ge(s_seen, sum(with_mask[:j + 1]))
                    if j >= 2:
                        pe.wait_ge(s_copied, j - 1)
                    if j >= 2 and len(it.blocks) > 4:
                        pe.wait_ge(s_out, j - 1)
                    for m, (col, keys, _) in enumerate(it.blocks):
                        mm = nc.tensor.transpose(turned(j, m, keys), probs[:, j % depth, col:col + keys], g.identity[:])
                    mm.then_inc(s_turned, 1)

        @block.scalar
        def _(act):
            for i in range(n_items + lag):
                if i < n_items:
                    lo, hi = items[i].columns
                    act.wait_ge(s_max, i + 1)
                    if i >= depth:
                        act.wait_ge(s_turned, i - depth + 1)
                    nc.scalar.activation(probs[:, i % depth, lo:hi], scores(i)[:, lo:hi], ACT.Exp, bias=negmax[:, i % 4:i % 4 + 1],
                                         accum_out=rowsum[:, i % ring:i % ring + 1]).then_inc(s_exp, 1)
                if i >= lag:
                    j = i - lag
                    act.wait_ge(s_turned, j + 1)
                    if j >= 2:
                        act.wait_ge(s_values, j - 1)
                    blocks = items[j].blocks
                    full = [m for m, b in enumerate(blocks) if m < 4 and b[1] == P]
                    if full:
                        ins = nc.scalar.copy(probsT[:, j % 2, 0:P * len(full)], g.psum[:, 4 + j % 2, 0:P * len(full)])
                    for m, (_, keys, _) in enumerate(blocks):
                        if m not in full:
                            ins = nc.scalar.copy(probsT[0:keys, j % 2, P * m:P * m + P], turned(j, m, keys))
                    ins.then_inc(s_copied, 1)
                g.picks.activate(act, i + 1)

        @block.vector
        def _(dve):
            link = linker(dve, s_link)
            for i in range(n_items + late + 1):
                if i < n_items:
                    lo, hi = items[i].columns
                    dve.wait_ge(s_scores, i + 1)
                    nc.vector.tensor_reduce(negmax[:, i % 4:i % 4 + 1], scores(i)[:, lo:hi], AX_X, ALU.max,
                                            negate=True).then_inc(s_max, 1)
                if 1 <= i <= n_items and items[i - 1].seen is not None:
                    j = i - 1
                    lo, hi = items[j].columns
                    dve.wait_ge(s_exp, j + 1)
                    p = probs[:, j % depth, lo:hi]
                    nc.vector.tensor_tensor(p, p, items[j].seen, ALU.mult).then_inc(s_seen, 1)
                if i >= late + 1:
                    j, it = i - late - 1, items[i - late - 1]
                    if j % group == 0:
                        dve.wait_ge(s_exp, j + group)
                        at = j % ring
                        link(nc.vector.reciprocal(factor[:, at:at + group], rowsum[:, at:at + group]))
                        if it.gates is not None:
                            link(nc.vector.tensor_tensor(factor[:, at:at + group], factor[:, at:at + group], it.gates, ALU.mult))
                    f = factor[:, j % ring:j % ring + 1]
                    dve.wait_ge(s_values, j + 1)
                    if it.add:
                        dve.wait_ge(s_out, j)
                        ins = nc.vector.scalar_tensor_tensor(out=it.out, in0=values(j), scalar=f, in1=it.out, op0=ALU.mult,
                                                             op1=ALU.add)
                    else:
                        ins = nc.vector.tensor_scalar(it.out, values(j), f, None, ALU.mult)
                    ins.then_inc(s_out, 1)
                g.picks.use(dve)


RET_Q0 = [0] + [P * t for t in range(NT)]
RET_OFF = [0, S, 2 * S, 3 * S - P, 4 * S - 3 * P]
RET_WIDTH = RET_OFF[-1] + P


def retention_stage(g, rqT, rkT, rv, decay, y, decayed, last_slab):
    nc = g.nc
    n_m = NT + 1
    with ExitStack() as ctx:
        sem = lambda name: g.semaphore(f"ret_{name}")
        s_scores, s_decayed, s_y, s_copied = (sem(x) for x in ("scores", "decayed_ready", "y_ready", "y_copied"))
        block = ctx.enter_context(nc.Block())

        @block.sync
        def _(sp):
            g.w.load_through(sp, last_slab)

        @block.tensor
        def _(pe):
            for h in range(RH + 1):
                if h < RH:
                    part = slice(RDK * (h % 2), RDK * (h % 2) + RDK)
                    for m in range(n_m):
                        n = n_m * h + m
                        rows, columns = row_tile(m)
                        if n >= 4:
                            pe.wait_ge(s_decayed, n - 3)
                        nc.tensor.matmul(g.psum[0:rows, n % 4, 0:S - RET_Q0[m]], rkT[part, h // 2, columns],
                                         rqT[part, h // 2, RET_Q0[m]:S], start=True, stop=True).then_inc(s_scores, 1)
                if h >= 1:
                    j = h - 1
                    pe.wait_ge(s_decayed, n_m * h)
                    if j >= 4:
                        pe.wait_ge(s_copied, j - 3)
                    for t in range(NT):
                        for m in range(t + 2):
                            rows, _ = row_tile(m)
                            at = RET_OFF[m] + P * t - RET_Q0[m]
                            mm = nc.tensor.matmul(g.psum[:, 4 + j % 4, RDV * t:RDV * t + RDV], decayed[0:rows, j % 2, at:at + P],
                                                  rv[0:rows, m, RDV * j:RDV * j + RDV], start=(m == 0), stop=(m == t + 1))
                    mm.then_inc(s_y, 1)

        @block.vector
        def _(dve):
            for h in range(RH):
                for m in range(n_m):
                    n = n_m * h + m
                    rows, _ = row_tile(m)
                    width = S - RET_Q0[m]
                    dve.wait_ge(s_scores, n + 1)
                    if m == 0 and h >= 2:
                        dve.wait_ge(s_y, h - 1)
                    d = decay[0:rows, h, META:L] if m == 0 else decay[0:rows, h, 0:width]
                    nc.vector.tensor_tensor(decayed[0:rows, h % 2, RET_OFF[m]:RET_OFF[m] + width],
                                            g.psum[0:rows, n % 4, 0:width], d, ALU.mult).then_inc(s_decayed, 1)

        @block.scalar
        def _(act):
            for h in range(RH):
                act.wait_ge(s_y, h + 1)
                nc.scalar.copy(y[:, h, :], g.psum[:, 4 + h % 4, :]).then_inc(s_copied, 1)


def group_norm_stage(g, y, gains, ynT):
    nc = g.nc
    with ExitStack() as ctx:
        sb = lambda name, shape: ctx.enter_context(nc.sbuf_tensor(f"gn_{name}", shape, F32))
        sem = lambda name: g.semaphore(f"gn_{name}")
        n = RH * NT
        stats, moments = sb("stats", [P, n, 6]), sb("moments", [P, n, 2])
        root, inverse = sb("root", [P, n]), sb("inverse", [P, n])
        s_link, s_var, s_root, s_normed, s_turned, s_drained = (
            sem(x) for x in ("link", "var", "root_ready", "normed", "turned", "drained"))
        block = ctx.enter_context(nc.Block())

        @block.vector
        def _(dve):
            link = linker(dve, s_link)
            for i in range(n):
                ins = nc.vector.bn_stats(stats[:, i, :], y[:, i // NT, RDV * (i % NT):RDV * (i % NT) + RDV])
            link(ins)
            for i in range(n):
                ins = nc.vector.bn_aggr(moments[:, i, :], stats[:, i, :])
            link(ins)
            nc.vector.tensor_scalar(inverse[:], moments[:, :, 1], EPS, None, ALU.add).then_inc(s_var, 1)
            dve.wait_ge(s_root, 1)
            link(nc.vector.reciprocal(inverse[:], root[:]))
            def drain(h):
                dve.wait_ge(s_turned, h + 1)
                nc.vector.scalar_tensor_tensor(out=ynT[:, h, :], in0=g.psum[:, h % 4, :], scalar=gains[:, h:h + 1],
                                               in1=ynT[:, h, :], op0=ALU.mult, op1=ALU.mult).then_inc(s_drained, 1)

            for h in range(RH):
                for t in range(NT):
                    i, yi = NT * h + t, y[:, h, RDV * t:RDV * t + RDV]
                    nc.vector.tensor_scalar(yi, yi, moments[:, i, 0:1], inverse[:, i:i + 1], ALU.subtract,
                                            ALU.mult).then_inc(s_normed, 1)
                if h:
                    drain(h - 1)
            drain(RH - 1)

        @block.tensor
        def _(pe):
            for h in range(RH):
                pe.wait_ge(s_normed, NT * (h + 1))
                if h >= 4:
                    pe.wait_ge(s_drained, h - 3)
                for t in range(NT):
                    mm = nc.tensor.transpose(g.psum[:, h % 4, P * t:P * t + P], y[:, h, RDV * t:RDV * t + RDV], g.identity[:])
                mm.then_inc(s_turned, 1)

        @block.scalar
        def _(act):
            act.wait_ge(s_var, 1)
            nc.scalar.activation(root[:], inverse[:], ACT.Sqrt).then_inc(s_root, 1)


def merge_stage(g, tag, half, names, gate_input, gate_columns, inputs, mergedT):
    nc = g.nc
    gate_a, prod_a, gate_b, prod_b = names
    products, owners = [], []
    width = gate_columns.stop - gate_columns.start
    for b in range(2):
        for gate, prod, (x, columns) in ((gate_a, prod_a, inputs[0]), (gate_b, prod_b, inputs[1])):
            products += [feature_major(g, ((gate, b), half), j, gate_input, gate_columns) for j in range(4)]
            products += [feature_major(g, ((prod, b), half), j, x, columns) for j in range(4)]
            owners += ["act"] * 4 + ["dve"] * 4
    with ExitStack() as ctx:
        gates = ctx.enter_context(nc.sbuf_tensor(f"{tag}_gates", [P, 8, width], F32))
        term = ctx.enter_context(nc.sbuf_tensor(f"{tag}_term", [P, 2, width], F32))
        drained = {e: g.semaphore(f"{tag}_drained_{e}") for e in ("act", "dve")}
        s_merged = g.semaphore(f"{tag}_merged")
        g.picks.share(tag, 16)
        block = ctx.enter_context(nc.Block())

        @block.gpsimd
        def _(pool):
            g.picks.issue(pool)

        @block.sync
        def _(sp):
            g.w.load_through(sp, ((prod_b, 1), half))

        @block.tensor
        def _(pe):
            multiply(g, pe, products, owners, drained)

        @block.scalar
        def _(act):
            done = 0
            for n, (name, j, _, _, _) in enumerate(products):
                if owners[n] != "act":
                    continue
                act.wait_ge(g.w.products_done, g.w.product(name, j))
                if done >= 8:
                    act.wait_ge(drained["dve"], done - 7)
                nc.scalar.activation(gates[:, done % 8, :], g.psum[:, n % BANKS, 0:width], ACT.Sigmoid).then_inc(drained["act"], 1)
                done += 1
                g.picks.activate(act, done)

        @block.vector
        def _(dve):
            done = 0
            for n, (name, j, _, _, _) in enumerate(products):
                if owners[n] != "dve":
                    continue
                second = (n // 8) % 2
                out = mergedT[:, 4 * (n // 16) + j, :]
                dve.wait_ge(g.w.products_done, g.w.product(name, j))
                dve.wait_ge(drained["act"], done + 1)
                nc.vector.tensor_tensor(term[:, j % 2, :] if second else out, g.psum[:, n % BANKS, 0:width],
                                        gates[:, done % 8, :], ALU.mult).then_inc(drained["dve"], 1)
                done += 1
                if second:
                    dve.wait_ge(drained["dve"], done)
                    nc.vector.tensor_tensor(out, out, term[:, j % 2, :], ALU.add).then_inc(s_merged, 1)
                g.picks.use(dve)


def peer_select_stage(g, tag, t, columns, pqT, keysT, iota, expert, gates):
    nc = g.nc
    with ExitStack() as ctx:
        sb = lambda name, shape, dt=F32: ctx.enter_context(nc.sbuf_tensor(f"{tag}_{name}", shape, dt))
        sem = lambda name: g.semaphore(f"{tag}_{name}")
        scratch = sb("scratch", [P, 2 * PH * PK])
        rest = scratch[:].rearrange("p (n k) -> p n k", n=2 * PH)
        best = sb("best", [P, PH, 2, TOPK])
        at = sb("at", [P, PH, 2, TOPK], U32)
        at_f = sb("at_f", [P, PH, 2, TOPK])
        cand = sb("cand", [P, PH, TOPK, TOPK])
        cand_rest = scratch[:].rearrange("p (h k) -> p h k", h=PH)
        top, pick = sb("top", [P, PH, TOPK]), sb("pick", [P, PH, TOPK], U32)
        part, part_f = sb("part", [P, 2, PH, TOPK], U32), sb("part_f", [P, 2, PH, TOPK])
        equal = scratch[:].rearrange("p (h a b) -> p h a b", h=PH, a=TOPK)
        number = sb("number", [P, 2, PH, TOPK])
        over, weight = sb("over", [P, PH, TOPK]), sb("weight", [P, PH, TOPK])
        total, inverse = sb("total", [P, PH]), sb("inverse", [P, PH])
        s_scores, s_over, s_exp, s_link = (sem(x) for x in ("scores", "over_ready", "exp", "link"))
        g.picks.share(tag, 4 * 3 * PH)
        block = ctx.enter_context(nc.Block())

        def scores(n):
            h, half = n // 2, n % 2
            return g.psum[:, 2 * half + h // 4, PK * (h % 4):PK * (h % 4) + PK]

        @block.gpsimd
        def _(pool):
            g.picks.issue(pool)

        @block.tensor
        def _(pe):
            for h in range(PH):
                for half in range(2):
                    rows = slice(64 * half, 64 * half + 64)
                    mm = nc.tensor.matmul(scores(2 * h + half), pqT[rows, h, columns], keysT[rows, :],
                                          start=True, stop=True)
            mm.then_inc(s_scores, 1)

        @block.scalar
        def _(act):
            act.wait_ge(s_over, 1)
            nc.scalar.activation(weight[:], over[:], ACT.Exp).then_inc(s_exp, 1)

        @block.vector
        def _(dve):
            link = linker(dve, s_link)

            def top16(lists):
                for values, _, src, _ in lists:
                    ins = nc.vector.max(values[:, 0:8], src)
                    g.picks.use(dve)
                link(ins)
                for values, places, src, rest in lists:
                    nc.vector.max_index(places[:, 0:8], values[:, 0:8], src)
                    ins = nc.vector.match_replace(rest, values[:, 0:8], src, LOWEST)
                    g.picks.use(dve)
                link(ins)
                for values, _, _, rest in lists:
                    ins = nc.vector.max(values[:, 8:16], rest)
                    g.picks.use(dve)
                link(ins)
                for values, places, _, rest in lists:
                    ins = nc.vector.max_index(places[:, 8:16], values[:, 8:16], rest)
                    g.picks.use(dve)
                link(ins)

            dve.wait_ge(s_scores, 1)
            top16([(best[:, h, half, :], at[:, h, half, :], scores(2 * h + half), rest[:, 2 * h + half, :])
                   for h in range(PH) for half in range(2)])
            nc.vector.tensor_copy(at_f[:], at[:])
            link(nc.vector.tensor_tensor(cand[:], best[:, :, 0, :].unsqueeze(3).to_broadcast([P, PH, TOPK, TOPK]),
                                         best[:, :, 1, :].unsqueeze(2).to_broadcast([P, PH, TOPK, TOPK]), ALU.add))
            top16([(top[:, h, :], pick[:, h, :], cand[:, h].rearrange("p a b -> p (a b)"), cand_rest[:, h, :])
                   for h in range(PH)])
            nc.vector.tensor_tensor(over[:], top[:], top[:, :, 0:1].to_broadcast([P, PH, TOPK]),
                                    ALU.subtract).then_inc(s_over, 1)
            nc.vector.tensor_scalar(part[:, 0], pick[:], 4, None, ALU.logical_shift_right)
            link(nc.vector.tensor_scalar(part[:, 1], pick[:], TOPK - 1, None, ALU.bitwise_and))
            link(nc.vector.tensor_copy(part_f[:], part[:]))
            for half in range(2):
                shape = [P, PH, TOPK, TOPK]
                link(nc.vector.tensor_tensor(equal, part_f[:, half].unsqueeze(3).to_broadcast(shape),
                                             iota.unsqueeze(1).unsqueeze(1).to_broadcast(shape), ALU.is_equal))
                link(nc.vector.tensor_tensor(equal, equal, at_f[:, :, half, :].unsqueeze(2).to_broadcast(shape),
                                             ALU.mult))
                link(nc.vector.tensor_reduce(number[:, half], equal, AX_X, ALU.add))
            link(nc.vector.scalar_tensor_tensor(out=expert[:, t, :], in0=number[:, 0].rearrange("p h k -> p (h k)"),
                                                scalar=float(PK), in1=number[:, 1].rearrange("p h k -> p (h k)"),
                                                op0=ALU.mult, op1=ALU.add))
            dve.wait_ge(s_exp, 1)
            link(nc.vector.tensor_reduce(total[:], weight[:], AX_X, ALU.add))
            link(nc.vector.reciprocal(inverse[:], total[:]))
            link(nc.vector.tensor_tensor(gates[:, t, :].rearrange("p (h k) -> p h k", h=PH), weight[:],
                                         inverse[:].unsqueeze(2).to_broadcast([P, PH, TOPK]), ALU.mult))


def picks_weight_stage(g):
    with ExitStack() as ctx:
        block = ctx.enter_context(g.nc.Block())

        @block.scalar
        def _(act):
            g.picks.activate(act)

        @block.vector
        def _(dve):
            g.picks.make_weights(dve, g.picks.weights)


def compress_input_stage(g, tag, h2T, half, pe_table, kc, last_slab):
    nc = g.nc
    first, last = (P * t // CMP_STRIDE for t in HALVES[half])
    name = ("kcvc", half)
    products = [feature_major(g, name, j, h2T, slice(0, CMP_STRIDE * (last - first))) for j in range(4)]
    with ExitStack() as ctx:
        drained = {"dve": g.semaphore(f"{tag}_drained")}
        g.picks.share(tag, 4)
        block = ctx.enter_context(nc.Block())

        @block.gpsimd
        def _(pool):
            g.picks.issue(pool)

        @block.sync
        def _(sp):
            g.w.load_through(sp, last_slab)

        @block.tensor
        def _(pe):
            multiply(g, pe, products, ["dve"] * 4, drained)

        @block.vector
        def _(dve):
            for j in range(4):
                dve.wait_ge(g.w.products_done, g.w.product(name, j))
                for part in range(2):
                    rows = slice(HD * part, HD * part + HD)
                    n0, n1 = max(first - part, 0), min(last - part, NCMP)
                    at = CMP_STRIDE * (n0 + part - first)
                    ins = nc.vector.tensor_tensor(
                        kc[rows, j // 2, j % 2, CMP_STRIDE * n0:CMP_STRIDE * n1].rearrange("p (n l) -> p n l", l=CMP_STRIDE),
                        g.psum[rows, j, at:at + CMP_STRIDE * (n1 - n0)].rearrange("p (n l) -> p n l", l=CMP_STRIDE),
                        pe_table[rows, j // 2, :].unsqueeze(1).to_broadcast([HD, n1 - n0, CMP_STRIDE]), ALU.add)
                ins.then_inc(drained["dve"], 1)
                g.picks.use(dve)


def compress_stage(g, tag, half, n, kc, w2, rope_cmp, k_cmpT, v_cmp, last_slab):
    nc = g.nc
    with ExitStack() as ctx:
        sb = lambda name, shape: ctx.enter_context(nc.sbuf_tensor(f"{tag}_{name}", shape, F32))
        sem = lambda name: g.semaphore(f"{tag}_{name}")
        hidden = sb("hidden", [P, 2, 2, NG * n])
        k_tok, k_roped = sb("k_tok", [n, NG * HD]), sb("k_roped", [n, NG * HD])
        tmp = [sb(f"tmp{i}", [n, NG * HD]) for i in range(2)]
        s_hidden, s_out, s_copied, s_link, s_roped, s_turned = (
            sem(x) for x in ("hidden_ready", "out_ready", "copied", "link", "roped", "turned"))
        g.picks.share(tag, 3)
        block = ctx.enter_context(nc.Block())

        @block.gpsimd
        def _(pool):
            g.picks.issue(pool)

        @block.sync
        def _(sp):
            g.w.load_through(sp, last_slab)

        @block.tensor
        def _(pe):
            for x, name in enumerate((("ck1", half), ("cv1", half))):
                g.w.arrived(pe, name)
                w1 = g.w.view(name)
                for j in range(2):
                    for l in range(CMP_STRIDE):
                        rhs = kc[:, x, :, :].rearrange("p g (n l) -> p g n l", l=CMP_STRIDE)[:, :, 0:n, l]
                        mm = nc.tensor.matmul(g.psum[:, 2 * x + j, 0:NG * n].rearrange("p (g n) -> p g n", g=NG),
                                              w1[:, l, P * j:P * j + P], rhs, start=(l == 0), stop=(l == CMP_STRIDE - 1))
                    mm.then_inc(g.w.products_done, 1)
            for x in range(2):
                pe.wait_ge(s_hidden, 2 * x + 2)
                for grp in range(NG):
                    for j in range(2):
                        mm = nc.tensor.matmul(g.psum[0:n, 4 + x, HD * grp:HD * grp + HD],
                                              hidden[:, x, j, n * grp:n * grp + n], w2[:, x, j, :],
                                              start=(j == 0), stop=(j == 1))
                mm.then_inc(s_out, 1)
            pe.wait_ge(s_roped, 1)
            for grp in range(NG):
                mm = nc.tensor.transpose(g.psum[0:HD, 6, P * grp:P * grp + n], k_roped[:, HD * grp:HD * grp + HD],
                                         g.identity[0:n, 0:n])
            mm.then_inc(s_turned, 1)

        @block.scalar
        def _(act):
            for x, name in enumerate((("ck1", half), ("cv1", half))):
                for j in range(2):
                    act.wait_ge(g.w.products_done, g.w.product(name, j))
                    nc.scalar.activation(hidden[:, x, j, :], g.psum[:, 2 * x + j, 0:NG * n],
                                         ACT.Gelu_apprx_tanh).then_inc(s_hidden, 1)

        @block.vector
        def _(dve):
            link = linker(dve, s_link)
            g.picks.use(dve)
            dve.wait_ge(s_out, 1)
            link(nc.vector.tensor_copy(k_tok[:], g.psum[0:n, 4, 0:NG * HD]))
            view = lambda x: x[:].rearrange("p (h a b) -> p h a b", h=NG, a=2)
            rope(nc, link, view(k_roped), view(k_tok), rope_cmp, tmp)
            nc.vector.memset(k_tok[:, 0:1], 0.0).then_inc(s_roped, 1)
            g.picks.use(dve)
            dve.wait_ge(s_out, 2)
            nc.vector.tensor_copy(v_cmp, g.psum[0:n, 5, 0:NG * HD])
            g.picks.use(dve)
            dve.wait_ge(s_turned, 1)
            link(nc.vector.tensor_copy(k_cmpT, g.psum[0:HD, 6, :].rearrange("p (g n) -> p g n", g=4)[:, 0:NG, 0:n]))


def pool_stage(g, tag, uT, tokens, inv_count, w_pool, pool_scale, ypT):
    nc = g.nc
    n = len(WINDOWS)
    lo, hi = tokens
    width = hi - lo
    with ExitStack() as ctx:
        sem = lambda name: g.semaphore(f"{tag}_{name}")
        sums = [ctx.enter_context(nc.sbuf_tensor(f"{tag}_sums{i}", [P, n, PAD + width], F32)) for i in range(2)]
        s_link, s_diff, s_y = sem("link"), sem("diff"), sem("y")
        g.picks.share(tag, n)
        block = ctx.enter_context(nc.Block())

        @block.gpsimd
        def _(pool):
            g.picks.issue(pool)

        @block.vector
        def _(dve):
            link = linker(dve, s_link)
            if lo == 0:
                link(nc.vector.memset(uT[:, :, 0:PAD], 0.0))
            mine = uT[:, :, lo:PAD + hi]
            src = mine
            for j in range(n):
                dst = sums[j % 2]
                step = 2 ** j
                at = 2 * step
                link(nc.vector.tensor_tensor(dst[:, j:n, at:], src[:, j:n, at:], src[:, j:n, at - step:PAD + width - step],
                                             ALU.add))
                short = PAD if lo == 0 else 0
                ins = nc.vector.scalar_tensor_tensor(out=ypT[:, j, short:], in0=dst[:, j, PAD + short:],
                                                     scalar=1.0 / WINDOWS[j], in1=mine[:, j, PAD + short:],
                                                     op0=ALU.mult, op1=ALU.subtract)
                if short:
                    link(nc.vector.tensor_tensor(ypT[:, j, 0:short], dst[:, j, PAD:PAD + short], inv_count[:, j, :], ALU.mult))
                    ins = nc.vector.tensor_tensor(ypT[:, j, 0:short], ypT[:, j, 0:short], mine[:, j, PAD:PAD + short],
                                                  ALU.subtract)
                if j < n - 1:
                    link(ins)
                else:
                    ins.then_inc(s_diff, 1)
                src = dst
                g.picks.use(dve)

        @block.tensor
        def _(pe):
            pe.wait_ge(s_diff, 1)
            for j in range(n):
                nc.tensor.matmul(g.psum[:, j, 0:width], w_pool[:, j, :], ypT[:, j, :], start=True, stop=True).then_inc(s_y, 1)

        @block.scalar
        def _(act):
            for j in range(n):
                act.wait_ge(s_y, j + 1)
                nc.scalar.activation(ypT[:, j, :], g.psum[:, j, 0:width], ACT.Copy, scale=pool_scale[:, j:j + 1])


def mlp_up_stage(g, tag, half, h2T, aT, last_slab):
    nc = g.nc
    n_slabs = D_FF // 512
    width = P * (HALVES[half][1] - HALVES[half][0])
    products = [feature_major(g, (("ff1", b), half), j, h2T, slice(0, width)) for b in range(n_slabs) for j in range(4)]
    with ExitStack() as ctx:
        drained = {"act": g.semaphore(f"{tag}_drained")}
        positive = ctx.enter_context(nc.sbuf_tensor(f"{tag}_positive", [P, 4, width], F32))
        s_squared = g.semaphore(f"{tag}_squared")
        g.picks.share(tag, len(products))
        block = ctx.enter_context(nc.Block())

        @block.gpsimd
        def _(pool):
            g.picks.issue(pool)

        @block.sync
        def _(sp):
            g.w.load_through(sp, last_slab)

        @block.tensor
        def _(pe):
            multiply(g, pe, products, ["act"] * len(products), drained)

        @block.scalar
        def _(act):
            for n, (name, j, _, _, _) in enumerate(products):
                act.wait_ge(g.w.products_done, g.w.product(name, j))
                if n >= 4:
                    act.wait_ge(s_squared, n - 3)
                nc.scalar.activation(positive[:, n % 4, :], g.psum[:, n % BANKS, 0:width], ACT.Relu).then_inc(drained["act"], 1)

        @block.vector
        def _(dve):
            for n in range(len(products)):
                dve.wait_ge(drained["act"], n + 1)
                x = positive[:, n % 4, :]
                nc.vector.tensor_tensor(aT[:, n, :], x, x, ALU.mult).then_inc(s_squared, 1)
                g.picks.use(dve)


def mlp_down_stage(g, tag, half, aT, last_slab):
    nc = g.nc
    groups = D_FF // P // KT
    first, last = HALVES[half]
    n_tiles = last - first
    with ExitStack() as ctx:
        s_added = g.semaphore(f"{tag}_added")
        g.picks.share(tag, 2 * groups)
        block = ctx.enter_context(nc.Block())

        @block.gpsimd
        def _(pool):
            g.picks.issue(pool)

        @block.sync
        def _(sp):
            g.w.load_through(sp, last_slab)

        @block.tensor
        def _(pe):
            for b in range(2):
                for k in range(groups):
                    name = (("ff2", b, k), half)
                    g.w.arrived(pe, name)
                    w = g.w.view(name)
                    for t in range(n_tiles):
                        for i in range(KT):
                            mm = nc.tensor.matmul(g.psum[:, n_tiles * b + t, :], aT[:, KT * k + i, P * t:P * t + P], w[:, i, :],
                                                  start=(k == 0 and i == 0), stop=(k == groups - 1 and i == KT - 1))
                        mm.then_inc(g.w.products_done, 1)

        @block.vector
        def _(dve):
            for b in range(2):
                for k in range(groups):
                    g.picks.use(dve)
                for t in range(n_tiles):
                    h = g.h[:, first + t, 512 * b:512 * b + 512]
                    dve.wait_ge(g.w.products_done, g.w.product((("ff2", b, groups - 1), half), t))
                    nc.vector.tensor_tensor(h, h, g.psum[:, n_tiles * b + t, :], ALU.add).then_inc(s_added, 1)


def load_stage(g, tag, pairs):
    with ExitStack() as ctx:
        s = g.semaphore(f"{tag}_loaded")
        block = ctx.enter_context(g.nc.Block())

        @block.sync
        def _(sp):
            for dst, src in pairs:
                sp.dma_start(dst, src).then_inc(s, 16)
            sp.wait_ge(s, 16 * len(pairs))


def build(nc, a):
    with ExitStack() as whole:
        g = Core(nc)
        alloc = lambda ctx, name, shape, dt=F32: ctx.enter_context(nc.sbuf_tensor(name, shape, dt))
        stage_semaphores = []
        def semaphore(name):
            stage_semaphores.append(nc.alloc_semaphore(name=name))
            return stage_semaphores[-1]

        def clear_semaphores():
            nc.clear_and_free_semaphores(stage_semaphores)
            nc.all_engine_barrier()
            stage_semaphores.clear()

        g.semaphore = semaphore
        g.psum = whole.enter_context(nc.psum_tensor("psum", [P, BANKS, 512], F32))
        g.w = Weights(nc, whole, weight_plan(a))
        g.h = alloc(whole, "h", [P, NT, D])
        g.identity = alloc(whole, "identity_sb", [P, P])
        gains = alloc(whole, "gains", [P, 96])
        names = [("g_mix", 8), ("g_q_lora", 3), ("g_kv_lora", 2), ("g_ret_gn", 8), ("norm_mix", 8), ("norm_mlp", 8),
                 ("pool_scale", 4)]
        g.gain, at, gain_loads = {}, 0, []
        for name, n in names:
            g.gain[name] = gains[:, at:at + n]
            gain_loads.append((g.gain[name], a[name]))
            at += n
        x_tiles = a["x"].rearrange("(t p) d -> p t d", p=P)
        expert, gates = alloc(whole, "expert", [P, NT, PICKS], U32), alloc(whole, "gates_sb", [P, NT, PICKS])
        late_x = alloc(whole, "xn_late", [P, 2, D])
        g.picks = Picks(g, whole, a["peer_u"], a["peer_v"], expert, gates, SHARES)

        def lend(tensor, shape, at=0):
            n = int(np.prod(shape[1:]))
            names = " ".join("abc"[:len(shape) - 1])
            flat = tensor[:].rearrange("p a b -> p (a b)")[:, at:at + n]
            return flat.rearrange(f"p ({names}) -> p {names}", **dict(zip("abc", shape[1:])))


        with ExitStack() as first:
            hnT = alloc(first, "hnT", [P, KT, L])
            ret_table = alloc(first, "rope_ret_sb", [P, NT + 1, 2, RDK // 2])
            o_tok = alloc(first, "mla_o", [P, NT, MH * MV])
            ynT = alloc(first, "ynT", [P, RH, S])
            with ExitStack() as s:
                meta = alloc(s, "meta", [META, D])
                loads = [(meta[:], a["meta_tokens"]), (g.h[:], x_tiles), (g.identity[:], a["identity"]),
                         (ret_table[:], a["rope_ret"])] + gain_loads
                sources = [(meta[:], META, row_tile(0)[1])] + [(g.h[:, t, :], P, row_tile(t + 1)[1]) for t in range(NT)]
                norm_stage(g, "n1", sources, D, outT=hnT, gain_columns=g.gain["g_mix"], loads=loads)

            with ExitStack() as mla:
                qT, kT = alloc(mla, "qT", [QK, MH, S]), alloc(mla, "kT", [QK, MH, L])
                v = alloc(mla, "mla_v", [P, NT + 1, MH * MV])
                causal = alloc(mla, "causal_sb", [P, P])
                with ExitStack() as s:
                    ckv = lend(late_x, [P, NT + 1, KV_LORA + MROPE])
                    q = lend(g.picks.rows, [P, NT, MH * QK])
                    k_heads = lend(g.picks.rows, [P, NT + 1, MH * QK], NT * MH * QK)
                    q_gain, k_gain = alloc(s, "q_gain", [P, QK]), alloc(s, "k_gain", [P, QK])
                    table = alloc(s, "rope_mla_sb", [P, NT + 1, 2, MROPE // 2])
                    tables = [(q_gain[:], a["g_qk_q"].partition_broadcast(P)), (k_gain[:], a["g_qk_k"].partition_broadcast(P)),
                              (table[:], a["rope_mla"]), (causal[:], a["causal"])]
                    with ExitStack() as lat:
                        cq, cqT = lend(ynT, [P, NT, Q_LORA]), lend(ynT, [P, 3, S], NT * Q_LORA)
                        ckvT = lend(g.picks.rows, [P, 2, L], (2 * NT + 1) * MH * QK)
                        products = [token_major(g, "cq", t, hnT, row_tile(t + 1)[1], P) for t in range(NT)]
                        outputs = [cq[:, t, :] for t in range(NT)]
                        for t in range(NT + 1):
                            rows, columns = row_tile(t)
                            products.append(token_major(g, "ckv", t, hnT, columns, rows))
                            outputs.append(ckv[0:rows, t, :])
                        product_stage(g, "lat", products, outputs, "ckv")
                        norm_stage(g, "nq", [(cq[:, t, :], P, slice(P * t, P * t + P)) for t in range(NT)], Q_LORA,
                                   outT=cqT, gain_columns=g.gain["g_q_lora"])
                        norm_stage(g, "nkv", [(ckv[0:row_tile(t)[0], t, 0:KV_LORA],) + row_tile(t) for t in range(NT + 1)],
                                   KV_LORA, outT=ckvT, gain_columns=g.gain["g_kv_lora"])
                        products, outputs = [], []
                        for b in range(2):
                            for t in range(NT):
                                products.append(token_major(g, ("uq", b), t, cqT, slice(P * t, P * t + P), P))
                                outputs.append(q[:, t, 384 * b:384 * b + 384])
                        for b in range(2):
                            for t in range(NT + 1):
                                rows, columns = row_tile(t)
                                products.append(token_major(g, ("ukv", b), t, ckvT, columns, rows))
                                heads = slice(4 * b, 4 * b + 4)
                                keys = k_heads[0:rows, t, :].rearrange("p (h d) -> p h d", h=MH)[:, heads, 0:NOPE]
                                vals = v[0:rows, t, :].rearrange("p (h d) -> p h d", h=MH)[:, heads, :]
                                outputs.append([(keys, lambda x: x.rearrange("p (h d) -> p h d", h=4)[:, :, 0:NOPE]),
                                                (vals, lambda x: x.rearrange("p (h d) -> p h d", h=4)[:, :, NOPE:])])
                        product_stage(g, "up", products, outputs, ("ukv", 1), loads=tables)
                    mla_qk_stage(g, q, k_heads, ckv[:, :, KV_LORA:], q_gain, k_gain, table, hnT, ynT, ("rg", 1))
                    sources = []
                    for t in range(NT):
                        for h0 in (0, 4):
                            sources.append(([q[:, t, QK * h:QK * h + QK] for h in range(h0, h0 + 4)], P,
                                            qT[:, h0:h0 + 4, P * t:P * t + P]))
                    turn_stage(g, "tq", sources, QK, scale=QK ** -0.5)
                    sources = []
                    for t in range(NT + 1):
                        rows, columns = row_tile(t)
                        for h0 in (0, 4):
                            sources.append(([k_heads[0:rows, t, QK * h:QK * h + QK] for h in range(h0, h0 + 4)], rows,
                                            kT[:, h0:h0 + 4, columns]))
                    turn_stage(g, "tk", sources, QK)
                for last, tiles in ((False, range(NT - 1)), (True, range(NT - 1, NT))):
                    items = []
                    for t in tiles:
                        for h in range(MH):
                            n = P * (t + 1)
                            meta_at = 512 if last else n
                            vh = v[:, :, MV * h:MV * h + MV]
                            items.append(Item(
                                q=qT[:, h, P * t:P * t + P], columns=(0, meta_at + META),
                                keys=[(kT[:, h, META:META + n], 0), (kT[:, h, 0:META], meta_at)],
                                biases=[(causal[:], n - P)], seen=None, gates=None, add=False,
                                blocks=[(P * m, P, vh[:, m + 1, :]) for m in range(t + 1)] + [(meta_at, META, vh[0:META, 0, :])],
                                out=o_tok[:, t, MV * h:MV * h + MV]))
                    depth, width = (2, S + META) if last else (4, S - P + META)
                    attention_stage(g, f"ma{int(last)}", items, MV, 2, (
                        lend(g.picks.rows, [P, depth, width]), lend(g.picks.rows, [P, 2, 5 * P], depth * width)))

            clear_semaphores()
            with ExitStack() as ret:
                rqT, rkT = lend(late_x, [P, RH // 2, S]), alloc(ret, "rkT", [P, RH // 2, L])
                rv = alloc(ret, "rv", [P, NT + 1, RH * RDV])
                rq, rk = lend(g.picks.rows, [P, NT, RH * RDK]), lend(g.picks.rows, [P, NT + 1, RH * RDK], NT * RH * RDK)
                decay = alloc(ret, "decay_sb", [P, RH, L])
                products, outputs, ropes = [], [], []
                for name, dst, c0 in (("rq", rq, 0), ("rk", rk, 0), (("rv", 0), rv, 0), (("rv", 1), rv, 512)):
                    for t in range(NT if name == "rq" else NT + 1):
                        i = t + 1 if name == "rq" else t
                        rows, columns = row_tile(i)
                        products.append(token_major(g, name, t, hnT, columns, rows))
                        outputs.append(dst[0:rows, t, c0:c0 + 512])
                        if name in ("rq", "rk"):
                            view = dst[0:rows, t, :].rearrange("p (h a b) -> p h a b", h=RH, a=2)
                            ropes.append((len(products) - 1, (view, view, ret_table[0:rows, i, :, :])))
                product_stage(g, "rp", products, outputs, ("rv", 1), ropes=ropes, loads=[(decay[:], a["decay"])])
                sources = [([rq[:, t, P * c:P * c + P] for c in range(4)], P, rqT[:, :, P * t:P * t + P])
                           for t in range(NT)]
                for t in range(NT + 1):
                    rows, columns = row_tile(t)
                    sources.append(([rk[0:rows, t, P * c:P * c + P] for c in range(4)], rows, rkT[:, :, columns]))
                turn_stage(g, "tr", sources, P)
                y = lend(g.picks.rows, [P, RH, NT * RDV])
                retention_stage(g, rqT, rkT, rv, decay, y, lend(g.picks.rows, [P, 2, RET_WIDTH], RH * NT * RDV), ("rv", 1))
                group_norm_stage(g, y, g.gain["g_ret_gn"], ynT)
            g_ffn = alloc(first, "g_ffn_sb", [P, D])
            keysT, iota = alloc(first, "keysT_sb", [P, PK]), alloc(first, "iota_sb", [P, TOPK])
            early_x = alloc(first, "xn_early", [P, 2, D])
            g.picks.x = [early_x[:, 0, :], early_x[:, 1, :], late_x[:, 0, :], late_x[:, 1, :]]
            load_stage(g, "peer", [(g_ffn[:], a["g_ffn"].partition_broadcast(P)), (keysT[:], a["keysT"]), (iota[:], a["iota"])])
            for run, (first_tile, last_tile) in enumerate(STARTS):
                clear_semaphores()
                tiles = range(first_tile, last_tile)
                width = P * len(tiles)
                local = lambda t: slice(P * (t - first_tile), P * (t - first_tile) + P)
                tag = lambda name: f"{name}_{run}"
                whole_range = slice(P * first_tile, P * last_tile)
                with ExitStack() as s:
                    oT, mergedT = alloc(s, tag("oT"), [P, 4, width]), alloc(s, tag("mergedT"), [P, KT, width])
                    turn_stage(g, tag("to"), [([o_tok[:, t, P * c:P * c + P] for c in range(4)], P, oT[:, :, local(t)])
                                              for t in tiles], P)
                    merge_stage(g, tag("m1"), run, ("za", "ya", "zr", "yr"), hnT,
                                slice(META + P * first_tile, META + P * last_tile),
                                ((oT, slice(0, width)), (ynT, whole_range)), mergedT)
                    residual_stage(g, tag("mix"), [(("mix", 0), run), (("mix", 1), run)], mergedT, (first_tile, last_tile),
                                   (("mix", 1), run))
                with ExitStack() as s:
                    pqT = alloc(s, tag("pqT"), [P, PH, width])
                    with ExitStack() as n:
                        xnT = alloc(n, tag("xnT"), [P, KT, width])
                        norm_stage(g, tag("np"), [(g.h[:, t, :], P, local(t)) for t in tiles], D, outT=xnT,
                                   token_out=g.picks.x[first_tile:last_tile], gain_rows=g_ffn[:])
                        products = [feature_major(g, (("pq", b), run), j, xnT, slice(0, width)) for b in range(2) for j in range(4)]
                        product_stage(g, tag("pq"), products, [pqT[:, h, :] for h in range(PH)], (("pq", 1), run))
                    for t in tiles:
                        peer_select_stage(g, f"sel{t}", t, local(t), pqT, keysT, iota[:], expert, gates)
                        g.picks.known = 2 * PICKS * (t + 1)
                        if t == 2:
                            picks_weight_stage(g)

        with ExitStack() as second:
            uT = alloc(second, "uT", [P, 4, PAD + S])
            kT, kv = alloc(second, "nsa_kT", [HD, 4, S]), alloc(second, "nsa_kv", [P, NT, 512])
            kc = alloc(second, "kc", [P, 2, NG, S])
            k_cmpT, v_cmp = alloc(second, "k_cmpT", [HD, NG, NCMP]), alloc(second, "v_cmp", [NCMP, NG * HD])
            pe_table = alloc(second, "pe_sb", [P, 2, CMP_STRIDE])
            w_pool, w2 = alloc(second, "w_pool_sb", [P, 4, P]), alloc(second, "w2_sb", [P, 2, 2, HD])
            table = alloc(second, "rope_nsa_sb", [P, NT, 2, HD // 2])
            table_cmp = alloc(second, "rope_cmp_sb", [NCMP, 2, HD // 2])
            causal, inv_count = alloc(second, "causal2_sb", [P, P]), alloc(second, "inv_count_sb", [P, 4, PAD])
            bias, seen = alloc(second, "cmp_bias_sb", [P, NT, NCMP]), alloc(second, "cmp_seen_sb", [P, NT, NCMP])
            load_stage(g, "nsa", [(pe_table[:], a["pe_table"]), (w2[:, 0], a["w_ck2"].rearrange("(j p) d -> p j d", p=P)),
                                  (w2[:, 1], a["w_cv2"].rearrange("(j p) d -> p j d", p=P)), (table[:], a["rope_nsa"]),
                                  (table_cmp[:], a["rope_cmp"]), (w_pool[:], a["w_pool"].rearrange("g c d -> c g d")),
                                  (causal[:], a["causal"]), (inv_count[:], a["inv_count"]), (bias[:], a["cmp_bias"]), (seen[:], a["cmp_seen"])])
            assert S // SEL_BLOCK <= N_SEL and WINDOW >= S
            for half, (first_tile, last_tile) in enumerate(HALVES):
                clear_semaphores()
                tiles = range(first_tile, last_tile)
                lo, hi = P * first_tile, P * last_tile
                width = hi - lo
                local = lambda t: slice(P * (t - first_tile), P * (t - first_tile) + P)
                tag = lambda name: f"{name}_{half}"
                with ExitStack() as mixer:
                    h2T, ypT = alloc(mixer, tag("h2T"), [P, KT, width]), alloc(mixer, tag("ypT"), [P, 4, width])
                    o = alloc(mixer, tag("nsa_o"), [P, len(tiles), NH * HD])
                    norm_stage(g, tag("n2"), [(g.h[:, t, :], P, local(t)) for t in tiles], D, outT=h2T,
                               gain_columns=g.gain["norm_mix"])
                    product_stage(g, tag("u"), [feature_major(g, ("u", half), j, h2T, slice(0, width)) for j in range(4)],
                                  [uT[:, j, PAD + lo:PAD + hi] for j in range(4)], ("u", half))
                    pool_stage(g, tag("pool"), uT, (lo, hi), inv_count, w_pool, g.gain["pool_scale"], ypT)
                    with ExitStack() as nsa:
                        qT = alloc(nsa, tag("nsa_qT"), [HD, NH, width])
                        branch_gates = alloc(nsa, tag("branch_gates"), [P, len(tiles), 3 * NH])
                        with ExitStack() as s:
                            q = alloc(s, tag("nsa_q"), [P, len(tiles), NH * HD])
                            products, outputs, ropes = [], [], []
                            for b in range(2):
                                for t in tiles:
                                    products.append(token_major(g, (("q", b), half), t - first_tile, h2T, local(t), P))
                                    outputs.append(q[:, t - first_tile, 512 * b:512 * b + 512])
                                    view = outputs[-1].rearrange("p (h a b) -> p h a b", h=512 // HD, a=2)
                                    ropes.append((len(products) - 1, (view, view, table[:, t, :, :])))
                            product_stage(g, tag("nq2"), products, outputs, (("q", 1), half), ropes=ropes)
                            compress_input_stage(g, tag("kc"), h2T, half, pe_table, kc, ("kcvc", half))
                            products, outputs, ropes = [], [], []
                            for t in tiles:
                                products.append(token_major(g, ("kv", half), t - first_tile, h2T, local(t), P))
                                outputs.append(kv[:, t, :])
                                for c0 in (0, 2 * KVW):
                                    view = kv[:, t, c0:c0 + KVW].rearrange("p (h a b) -> p h a b", h=NG, a=2)
                                    ropes.append((len(products) - 1, (view, view, table[:, t, :, :])))
                            for t in tiles:
                                products.append(token_major(g, ("gn", half), t - first_tile, h2T, local(t), P))
                                outputs.append(branch_gates[:, t - first_tile, :])
                            product_stage(g, tag("nkv2"), products, outputs, ("gn", half),
                                          functions=[None] * len(tiles) + [ACT.Sigmoid] * len(tiles), ropes=ropes)
                            n_blocks = (hi - CMP_LEN) // CMP_STRIDE + 1
                            compress_stage(g, tag("cmp"), half, n_blocks, kc, w2, table_cmp[0:n_blocks],
                                           k_cmpT[:, :, 0:n_blocks], v_cmp[0:n_blocks, :], ("cv1", half))
                            sources = []
                            for t in tiles:
                                for h0 in range(0, NH, 4):
                                    sources.append(([q[:, t - first_tile, HD * h:HD * h + HD] for h in range(h0, h0 + 4)], P,
                                                    qT[:, h0:h0 + 4, local(t)]))
                            turn_stage(g, tag("tq2"), sources, HD, scale=HD ** -0.5)
                            turn_stage(g, tag("tk2"), [([kv[:, t, c:c + HD] for c in (0, HD, 2 * KVW, 2 * KVW + HD)], P,
                                                        kT[:, :, P * t:P * t + P]) for t in tiles], HD)
                        items = []
                        for t in tiles:
                            for h in range(NH):
                                grp = h // HPG
                                common = dict(q=qT[:, h, local(t)], out=o[:, t - first_tile, HD * h:HD * h + HD])
                                gates3 = branch_gates[:, t - first_tile, 3 * h:3 * h + 3]
                                items.append(Item(
                                    keys=[(k_cmpT[:, grp, 0:n_blocks], 0)], columns=(0, n_blocks),
                                    biases=[(bias[:, t, 0:n_blocks], 0)],
                                    blocks=[(0, n_blocks, v_cmp[0:n_blocks, HD * grp:HD * grp + HD])],
                                    seen=seen[:, t, 0:n_blocks], gates=gates3, add=False, **common))
                                for x in range(2):
                                    n = P * (t + 1)
                                    v0 = 2 * KVW * x + KVW + HD * grp
                                    items.append(Item(
                                        keys=[(kT[:, 2 * x + grp, 0:n], 0)], columns=(0, n), biases=[(causal[:], n - P)],
                                        blocks=[(P * m, P, kv[:, m, v0:v0 + HD]) for m in range(t + 1)], seen=None,
                                        gates=gates3, add=True, **common))
                        attention_stage(g, tag("na"), items, HD, 3)
                    oT = alloc(mixer, tag("nsa_oT"), [P, KT, width])
                    turn_stage(g, tag("to2"), [([o[:, t - first_tile, P * c:P * c + P] for c in range(c0, c0 + 4)], P,
                                                oT[:, c0:c0 + 4, local(t)]) for t in tiles for c0 in (0, 4)], P)
                    mergedT = alloc(mixer, tag("mergedT2"), [P, KT, width])
                    merge_stage(g, tag("m2"), half, ("ga", "yp", "gb", "yn"), h2T, slice(0, width),
                                ((ypT, slice(0, width)), (oT, slice(0, width))), mergedT)
                    residual_stage(g, tag("out"), [(("out", 0), half), (("out", 1), half)], mergedT, (first_tile, last_tile),
                                   (("out", 1), half))
                with ExitStack() as mlp:
                    aT = alloc(mlp, tag("aT"), [P, D_FF // P, width])
                    with ExitStack() as s:
                        h3T = alloc(s, tag("h3T"), [P, KT, width])
                        norm_stage(g, tag("n3"), [(g.h[:, t, :], P, local(t)) for t in tiles], D, outT=h3T,
                                   gain_columns=g.gain["norm_mlp"])
                        mlp_up_stage(g, tag("ff1"), half, h3T, aT, (("ff1", D_FF // 512 - 1), half))
                    mlp_down_stage(g, tag("ff2"), half, aT, (("ff2", 1, 3), half))
        with ExitStack() as s:
            final, g_final = alloc(s, "final", [P, NT, D]), alloc(s, "g_final", [P, D])
            load_stage(g, "final", [(g_final[:], a["norm_final"].partition_broadcast(P))])
            norm_stage(g, "nf", [(g.h[:, t, :], P, None) for t in range(NT)], D,
                       token_out=[final[:, t, :] for t in range(NT)], gain_rows=g_final[:],
                       store=a["out"].rearrange("(t p) d -> p t d", p=P))


def arrays(inputs):
    def columns(v):
        return v.reshape(-1, P).T

    one = {k: np.asarray(v)[0] for k, v in inputs.items() if k not in ("meta_tokens", "norm_final_2")}
    w2 = one["w_in_2"]
    kc_vc = w2[:, E_KC:E_KS].reshape(D, 2 * NG, 1, HD)
    first_w = lambda w: w.reshape(2, CMP_STRIDE, HD, CMP_HID).transpose(0, 2, 1, 3).reshape(P, CMP_STRIDE, CMP_HID)
    pe = lambda x: x.reshape(2, CMP_STRIDE, HD).transpose(0, 2, 1).reshape(P, CMP_STRIDE)
    out = {
        "x": one["x"], "meta_tokens": np.asarray(inputs["meta_tokens"]),
        "g_mix": columns(one["g_mix"]), "g_q_lora": columns(one["g_q_lora"]), "g_kv_lora": columns(one["g_kv_lora"]),
        "g_ret_gn": columns(one["g_ret_gn"]), "norm_mix": columns(one["norm_mix_2"]),
        "norm_mlp": columns(one["norm_mlp_2"]), "pool_scale": columns(one["pool_scale_2"]),
        "g_qk_q": one["g_qk_q"], "g_qk_k": one["g_qk_k"], "g_ffn": one["g_ffn"], "norm_final": np.asarray(inputs["norm_final_2"]),
        "w_in": one["w_in"], "w_uq": one["w_uq"], "w_ukv": one["w_ukv"], "w_mla_out": one["w_mla_out"],
        "w_ret_out": one["w_ret_out"], "w_mix_out": one["w_mix_out"], "w_peer_q": one["w_peer_q"],
        "keysT": np.concatenate([one["peer_keys_1"].T, one["peer_keys_2"].T]),
        "peer_u": one["peer_u"], "peer_v": one["peer_v"],
        "w_in2": w2, "w_kcvc": np.broadcast_to(kc_vc, (D, 2 * NG, 2, HD)).reshape(D, 4 * P),
        "w_ck1": first_w(one["w_ck1_2"]), "w_cv1": first_w(one["w_cv1_2"]), "w_ck2": one["w_ck2_2"], "w_cv2": one["w_cv2_2"],
        "pe_table": np.stack([pe(one["pe_k_2"]), pe(one["pe_v_2"])], 1),
        "w_pool": one["w_pool_2"], "w_proj_pool": one["w_proj_pool_2"], "w_proj_nsa": one["w_proj_nsa_2"],
        "w_out": one["w_out_2"], "w_ff1": one["w_ff1_2"], "w_ff2": one["w_ff2_2"],
    }
    return {k: np.ascontiguousarray(v) for k, v in out.items()} | constants()


def kernel(**inputs):
    import concourse.bacc as bacc
    from concourse.bass_utils import run_bass_kernel_spmd

    nc = bacc.Bacc("TRN2", target_bir_lowering=False, num_devices=1)
    data = arrays(inputs)
    views = {k: nc.dram_tensor(f"{k}_dram", v.shape, mybir.dt.from_np(v.dtype), kind="ExternalInput").ap()
             for k, v in data.items()}
    views["out"] = nc.dram_tensor("out_dram", (S, D), F32, kind="ExternalOutput").ap()
    build(nc, views)
    r = run_bass_kernel_spmd(nc, [{f"{k}_dram": v for k, v in data.items()}], core_ids=[0])
    return r.results[0]["out_dram"].reshape(1, S, D)
```
